# Optimizing a Trainium2 kernel written in Bass

```python
import math
import jax
import jax.numpy as jnp
from jax import lax
import numpy as np

D_MODEL = 1024
BATCH = 1
SEQ = 128
DEPTH = 1
DEC_BATCH = 1
DEC_SEQ = 1024
PAST_LEN = 128

GRID_W = 64
SSD_EXPAND = 2
D_SSD = SSD_EXPAND * D_MODEL
SSD_HEADDIM = 64
SSD_HEADS = D_SSD // SSD_HEADDIM
SSD_GROUPS = 8
D_STATE = 128
D_CONV = 5
SSD_CHUNK = 128
CONV_DIM = D_SSD + 2 * SSD_GROUPS * D_STATE
HGRN_HEADS = 8
HGRN_KDIM = 128
HGRN_FDIM = HGRN_HEADS * HGRN_KDIM
HGRN_WIDTH = D_MODEL
HGRN_VDIM = HGRN_WIDTH // HGRN_HEADS
HGRN_CHUNK = 16
N_BRANCHES = 2
IN_COLS = CONV_DIM + D_SSD + 2 * SSD_HEADS + HGRN_FDIM + 2 * HGRN_FDIM + 2 * HGRN_WIDTH + N_BRANCHES * D_MODEL
FFN_HIDDEN = ((8 * D_MODEL + 767) // 768) * 256
RMS_EPS = 1e-6

kernel_name = "hybrid_ssd_hgrn2_diffusion_step"

def _rmsnorm(x, w):
    x32 = x.astype(jnp.float32)
    y = x32 * lax.rsqrt(jnp.mean(x32 * x32, axis=-1, keepdims=True) + RMS_EPS)
    return (y * w.astype(jnp.float32)).astype(x.dtype)

def _centred_dwconv_silu(u, w, b):
    length = u.shape[-2]
    pad = D_CONV // 2
    up = jnp.pad(u, [(0, 0)] * (u.ndim - 2) + [(pad, pad), (0, 0)])
    out = b
    for k in range(D_CONV):
        out = out + up[..., k:k + length, :] * w[k]
    return jax.nn.silu(out)

def _carry_chunk_states(chunk_decay, chunk_contrib, s0):
    def step(s, inp):
        d, u = inp
        return d * s + u, s
    s_final, starts = lax.scan(step, s0, (jnp.moveaxis(chunk_decay, 1, 0), jnp.moveaxis(chunk_contrib, 1, 0)))
    return jnp.moveaxis(starts, 0, 1), s_final

def _ssd_scan(x, dt, a_neg, bmat, cmat, s0):
    f32 = jnp.float32
    bt, length, n_heads, hd = x.shape
    g, n = bmat.shape[2], bmat.shape[3]
    r = n_heads // g
    q = SSD_CHUNK
    nc = length // q
    xg = x.astype(f32).reshape(bt, nc, q, g, r, hd)
    dtg = dt.astype(f32).reshape(bt, nc, q, g, r)
    bg = bmat.astype(f32).reshape(bt, nc, q, g, n)
    cg = cmat.astype(f32).reshape(bt, nc, q, g, n)
    cs = jnp.cumsum(dtg * a_neg.astype(f32).reshape(g, r), axis=2)
    causal = jnp.tril(jnp.ones((q, q), dtype=bool))[:, :, None, None]
    decay = jnp.exp(jnp.where(causal, cs[:, :, :, None] - cs[:, :, None, :], -jnp.inf))
    cb = jnp.einsum("bcign,bcjgn->bcijg", cg, bg)
    xdt = dtg[..., None] * xg
    y_diag = jnp.einsum("bcijgr,bcjgrp->bcigrp", cb[..., None] * decay, xdt)
    to_end = jnp.exp(cs[:, :, -1:] - cs)
    contrib = jnp.einsum("bcjgn,bcjgrp->bcgrpn", bg, to_end[..., None] * xdt)
    chunk_decay = jnp.exp(cs[:, :, -1])[..., None, None]
    starts, s_fin = _carry_chunk_states(chunk_decay, contrib, s0.astype(f32).reshape(bt, g, r, hd, n))
    y_off = jnp.einsum("bcign,bcgrpn->bcigrp", cg, starts) * jnp.exp(cs)[..., None]
    y = (y_diag + y_off).reshape(bt, length, n_heads, hd)
    return y.astype(x.dtype), s_fin.reshape(bt, n_heads, hd, n).astype(x.dtype)

def _hgrn2_scan(q, log_f, k, v, s0):
    f32 = jnp.float32
    bt, length, n_heads, kd = q.shape
    vd = v.shape[-1]
    c = HGRN_CHUNK
    nc = length // c
    qc = q.astype(f32).reshape(bt, nc, c, n_heads, kd)
    kc = k.astype(f32).reshape(bt, nc, c, n_heads, kd)
    vc = v.astype(f32).reshape(bt, nc, c, n_heads, vd)
    b = jnp.cumsum(log_f.astype(f32).reshape(bt, nc, c, n_heads, kd), axis=2)
    causal = jnp.tril(jnp.ones((c, c), dtype=bool))[:, :, None, None]
    decay = jnp.exp(jnp.where(causal, b[:, :, :, None] - b[:, :, None, :], -jnp.inf))
    attn = jnp.einsum("bcihk,bcijhk,bcjhk->bcijh", qc, decay, kc)
    o_intra = jnp.einsum("bcijh,bcjhv->bcihv", attn, vc)
    contrib = jnp.einsum("bcjhk,bcjhv->bchkv", kc * jnp.exp(b[:, :, -1:] - b), vc)
    chunk_decay = jnp.exp(b[:, :, -1])[..., None]
    starts, s_fin = _carry_chunk_states(chunk_decay, contrib, s0.astype(f32))
    o_off = jnp.einsum("bcihk,bchkv->bcihv", qc * jnp.exp(b), starts)
    o = (o_intra + o_off).reshape(bt, length, n_heads, vd)
    return o.astype(q.dtype), s_fin.astype(q.dtype)

def _hybrid_mixer(h, lw, lb, s_ssm0, s_hgrn0, latent):
    f32 = jnp.float32
    bt, length, _ = h.shape
    proj = h @ lw["w_in"]
    cuts = np.cumsum([CONV_DIM, D_SSD, 2 * SSD_HEADS, HGRN_FDIM, 2 * HGRN_FDIM, HGRN_WIDTH, HGRN_WIDTH]).tolist()
    xbc, z, dt_raw, hq, hf, hi, hg, gate_logits = jnp.split(proj, cuts, axis=-1)

    if latent:
        rows = length // GRID_W
        xbc = _centred_dwconv_silu(xbc.reshape(bt, rows, GRID_W, CONV_DIM), lw["ssd_conv_w"], lw["ssd_conv_b"]).reshape(bt, length, CONV_DIM)
    else:
        xbc = _centred_dwconv_silu(xbc, lw["ssd_conv_w"], lw["ssd_conv_b"])
    xs, bm, cm = jnp.split(xbc, [D_SSD, D_SSD + SSD_GROUPS * D_STATE], axis=-1)
    xs = xs.reshape(bt, length, SSD_HEADS, SSD_HEADDIM)
    bm = bm.reshape(bt, length, SSD_GROUPS, D_STATE)
    cm = cm.reshape(bt, length, SSD_GROUPS, D_STATE)
    dt = jax.nn.softplus(dt_raw.astype(f32).reshape(bt, length, 2, SSD_HEADS) + lw["ssd_dt_bias"].astype(f32))
    a_neg = -jnp.exp(lw["ssd_a_log"].astype(f32))
    y_f, sf = _ssd_scan(xs, dt[:, :, 0], a_neg[0], bm, cm, s_ssm0[:, 0])
    y_b, sb = _ssd_scan(xs[:, ::-1], dt[:, ::-1, 1], a_neg[1], bm[:, ::-1], cm[:, ::-1], s_ssm0[:, 1])
    y = y_f + y_b[:, ::-1] + lw["ssd_d"][:, None] * xs
    y = y.reshape(bt, length, D_SSD) * jax.nn.silu(z)
    y = _rmsnorm(y.reshape(bt, length, SSD_GROUPS, D_SSD // SSD_GROUPS), lw["ssd_norm_w"].reshape(SSD_GROUPS, -1)).reshape(bt, length, D_SSD)
    y_ssd = y @ lw["w_ssd_out"]

    q = jax.nn.silu(hq).reshape(bt, length, HGRN_HEADS, HGRN_KDIM)
    v = hi.reshape(bt, length, HGRN_HEADS, HGRN_VDIM)
    u = hf.astype(f32).reshape(bt, length, 2, HGRN_HEADS, HGRN_KDIM)
    lb3 = lb.reshape(2, HGRN_HEADS, HGRN_KDIM)
    log_f = jnp.logaddexp(jnp.log(lb3), jnp.log1p(-lb3) + jax.nn.log_sigmoid(u))
    k = -jnp.expm1(log_f)
    o_f, hf_state = _hgrn2_scan(q, log_f[:, :, 0], k[:, :, 0], v, s_hgrn0[:, 0])
    o_b, hb_state = _hgrn2_scan(q[:, ::-1], log_f[:, ::-1, 1], k[:, ::-1, 1], v[:, ::-1], s_hgrn0[:, 1])
    o = o_f + o_b[:, ::-1]
    o = _rmsnorm(o, lw["hgrn_norm_w"].reshape(HGRN_HEADS, HGRN_VDIM)).reshape(bt, length, HGRN_WIDTH) * jax.nn.silu(hg)
    y_hgrn = o @ lw["w_hgrn_out"]

    g_ssd, g_hgrn = jnp.split(jax.nn.sigmoid(gate_logits), N_BRANCHES, axis=-1)
    out = (g_ssd * y_ssd + g_hgrn * y_hgrn) @ lw["w_out"]
    return out, jnp.stack([sf, sb], axis=1), jnp.stack([hf_state, hb_state], axis=1)

def _layer(x, mod, lw, lb, s_ssm0, s_hgrn0, latent):
    sh_m, sc_m, g_m, sh_f, sc_f, g_f = jnp.split(mod, 6, axis=-1)
    h = _rmsnorm(x, lw["norm_mix_w"]) * (1 + sc_m) + sh_m
    mix, s_ssm, s_hgrn = _hybrid_mixer(h, lw, lb, s_ssm0, s_hgrn0, latent)
    x = x + g_m * mix
    h = _rmsnorm(x, lw["norm_ffn_w"]) * (1 + sc_f) + sh_f
    ffn = (jax.nn.silu(h @ lw["ffn_w1"]) * (h @ lw["ffn_w3"])) @ lw["ffn_w2"]
    x = x + g_f * ffn
    return x, s_ssm, s_hgrn

def setup_inputs(seed: int = 0) -> dict:
    key = jax.random.key(seed)
    ks = jax.random.split(key, 26)
    f32 = jnp.float32

    def nrm(k, shape, scale):
        return jax.random.normal(k, shape, f32) * scale

    dt0 = jnp.exp(jax.random.uniform(ks[13], (DEPTH, 2, SSD_HEADS), f32, math.log(1e-3), math.log(1e-1)))
    return {
        "x_prompt": nrm(ks[0], (BATCH, SEQ, D_MODEL), 1.0),
        "x_sample": nrm(ks[1], (DEC_BATCH, DEC_SEQ, D_MODEL), 1.0),
        "c": nrm(ks[2], (DEC_BATCH, D_MODEL), 1.0),
        "state_ssm": nrm(ks[3], (DEC_BATCH, DEPTH, 2, SSD_HEADS, SSD_HEADDIM, D_STATE), 0.3),
        "state_hgrn": nrm(ks[4], (DEC_BATCH, DEPTH, 2, HGRN_HEADS, HGRN_KDIM, HGRN_VDIM), 0.5),
        "c_ctx": nrm(ks[5], (D_MODEL,), 1.0),
        "norm_mix_w": 1.0 + nrm(ks[6], (DEPTH, D_MODEL), 0.02),
        "norm_ffn_w": 1.0 + nrm(ks[7], (DEPTH, D_MODEL), 0.02),
        "ada_w": nrm(ks[8], (DEPTH, D_MODEL, 6 * D_MODEL), 0.5 * D_MODEL ** -0.5),
        "ada_b": nrm(ks[9], (DEPTH, 6 * D_MODEL), 0.02),
        "w_in": nrm(ks[10], (DEPTH, D_MODEL, IN_COLS), D_MODEL ** -0.5),
        "ssd_conv_w": nrm(ks[11], (DEPTH, D_CONV, CONV_DIM), D_CONV ** -0.5),
        "ssd_conv_b": nrm(ks[12], (DEPTH, CONV_DIM), 0.02),
        "ssd_dt_bias": dt0 + jnp.log(-jnp.expm1(-dt0)),
        "ssd_a_log": jnp.log(jax.random.uniform(ks[14], (DEPTH, 2, SSD_HEADS), f32, 1.0, 16.0)),
        "ssd_d": 1.0 + nrm(ks[15], (DEPTH, SSD_HEADS), 0.1),
        "ssd_norm_w": 1.0 + nrm(ks[16], (DEPTH, D_SSD), 0.02),
        "hgrn_lower_bounds": nrm(ks[17], (DEPTH, 2, HGRN_FDIM), 1.0),
        "hgrn_norm_w": 1.0 + nrm(ks[18], (DEPTH, HGRN_WIDTH), 0.02),
        "w_ssd_out": nrm(ks[19], (DEPTH, D_SSD, D_MODEL), D_SSD ** -0.5),
        "w_hgrn_out": nrm(ks[20], (DEPTH, HGRN_WIDTH, D_MODEL), HGRN_WIDTH ** -0.5),
        "w_out": nrm(ks[21], (DEPTH, D_MODEL, D_MODEL), D_MODEL ** -0.5),
        "ffn_w1": nrm(ks[22], (DEPTH, D_MODEL, FFN_HIDDEN), D_MODEL ** -0.5),
        "ffn_w3": nrm(ks[23], (DEPTH, D_MODEL, FFN_HIDDEN), D_MODEL ** -0.5),
        "ffn_w2": nrm(ks[24], (DEPTH, FFN_HIDDEN, D_MODEL), FFN_HIDDEN ** -0.5),
        "norm_final_w": 1.0 + nrm(ks[25], (D_MODEL,), 0.02),
    }

def reference(x_prompt, x_sample, c, state_ssm, state_hgrn, c_ctx, norm_mix_w, norm_ffn_w, ada_w, ada_b, w_in,
              ssd_conv_w, ssd_conv_b, ssd_dt_bias, ssd_a_log, ssd_d, ssd_norm_w, hgrn_lower_bounds, hgrn_norm_w,
              w_ssd_out, w_hgrn_out, w_out, ffn_w1, ffn_w3, ffn_w2, norm_final_w):
    lb_all = jnp.cumsum(jax.nn.softmax(hgrn_lower_bounds.astype(jnp.float32), axis=0), axis=0)
    lb_all = lb_all - lb_all[:1]
    bp = x_prompt.shape[0]
    zero_ssm = jnp.zeros((bp, 2, SSD_HEADS, SSD_HEADDIM, D_STATE), x_prompt.dtype)
    zero_hgrn = jnp.zeros((bp, 2, HGRN_HEADS, HGRN_KDIM, HGRN_VDIM), x_prompt.dtype)
    ctx, lat = x_prompt, x_sample
    ssm_states, hgrn_states = [], []
    for l in range(DEPTH):
        lw = {
            "norm_mix_w": norm_mix_w[l], "norm_ffn_w": norm_ffn_w[l], "w_in": w_in[l],
            "ssd_conv_w": ssd_conv_w[l], "ssd_conv_b": ssd_conv_b[l], "ssd_dt_bias": ssd_dt_bias[l],
            "ssd_a_log": ssd_a_log[l], "ssd_d": ssd_d[l], "ssd_norm_w": ssd_norm_w[l],
            "hgrn_norm_w": hgrn_norm_w[l], "w_ssd_out": w_ssd_out[l], "w_hgrn_out": w_hgrn_out[l],
            "w_out": w_out[l], "ffn_w1": ffn_w1[l], "ffn_w3": ffn_w3[l], "ffn_w2": ffn_w2[l],
        }
        mod_ctx = (jax.nn.silu(c_ctx) @ ada_w[l] + ada_b[l])[None, None, :]
        mod_lat = (jax.nn.silu(c) @ ada_w[l] + ada_b[l])[:, None, :]
        ctx, s_ssm, s_hgrn = _layer(ctx, mod_ctx, lw, lb_all[l], zero_ssm, zero_hgrn, False)
        lat, _, _ = _layer(lat, mod_lat, lw, lb_all[l], state_ssm[:, l], state_hgrn[:, l], True)
        ssm_states.append(s_ssm)
        hgrn_states.append(s_hgrn)
    y_prompt = _rmsnorm(ctx, norm_final_w)
    y_sample = _rmsnorm(lat, norm_final_w)
    new_state_ssm = jnp.stack(ssm_states, axis=1)
    new_state_hgrn = jnp.stack(hgrn_states, axis=1)
    return (y_prompt, y_sample, new_state_ssm, new_state_hgrn)


_drawn_inputs = setup_inputs


def setup_inputs(seed=0):
    import zlib

    import numpy as np

    out = dict(_drawn_inputs(seed))
    spreads = {}
    factors = {'state_hgrn': 29.103,
     'norm_ffn_w': 8.0,
     'ssd_d': 8.0,
     'ssd_norm_w': 22.465,
     'hgrn_norm_w': 34.855,
     'norm_final_w': 7.698}
    for name, (base, spread) in spreads.items():
        noise = np.random.default_rng([zlib.crc32(name.encode()), seed]).standard_normal(out[name].shape)
        drawn = base * np.exp(spread * noise) if base else spread * noise
        out[name] = jnp.asarray(drawn.astype(out[name].dtype))
    for name, factor in factors.items():
        out[name] = (out[name] * factor).astype(out[name].dtype)
    return out
```

```python
from contextlib import ExitStack

import concourse.bass as bass
from concourse import mybir

F32 = mybir.dt.float32
F32R = mybir.dt.float32r
BF16 = mybir.dt.bfloat16
U8 = mybir.dt.uint8
ALU = mybir.AluOpType
ACT = mybir.ActivationFunctionType

P = 128
D = 1024
KT = D // P
CTX = 128
T = 1152
NC = T // P
NB = 3
BW = T // NB
CB = BW // P
GRID = 64
ROWS = BW // GRID
G = 8
HPG = 4
HD = 64
GW = HPG * HD
TAPS = 5
FFN = 2816
EPS = 1e-6

COL_X, COL_B, COL_C, COL_Z, COL_DT = 0, 2048, 3072, 4096, 6144
COL_Q, COL_FF, COL_FB, COL_I, COL_G, COL_GATE = 6208, 7232, 8256, 9280, 10304, 11328

V_TAP4, V_CONVB, V_ADAB, V_MIX, V_FFN = 128, 160, 192, 240, 248
V_SSDN, V_HGRN, V_C, V_CCTX, V_D, V_END = 256, 272, 280, 288, 296, 312

TILES_BEFORE = 7
TILES_GROUP = 12
UNITS_BEFORE = TILES_BEFORE * NB
UNITS_GROUP = TILES_GROUP * NB
SLOTS = 18

LEVELS = 7
STEPS = [("kb", 2, 0), ("kb", 1, 0), ("kb", 0, 0), ("kf", 0, 0)]
for _b in range(NB):
    STEPS += [("lv", _b, _l) for _l in range(LEVELS)] + [("dg", _b, LEVELS), ("q", _b, 0)]
    if _b < NB - 1:
        STEPS.append(("kf", _b + 1, 0))
NSTEP = len(STEPS)
ACT_ROUND, DVE_ROUND, DT_ACT, DT_DVE = 13, 124, 7, 17
KSTEPS = [n for n, s in enumerate(STEPS) if s[0] in ("kb", "kf")]
QSTEPS = [n for n, s in enumerate(STEPS) if s[0] == "q"]
ASTEPS = [n for n, s in enumerate(STEPS) if s[0] in ("kb", "kf", "lv")]
ESTEPS = [n for n, s in enumerate(STEPS) if s[0] != "dg"]
MSTEPS = [n for n, s in enumerate(STEPS) if s[0] in ("lv", "dg")]


def slot_of(n):
    return 0 if n < 4 else (n - 2) // 2


def steps_in(slot):
    return [n for n in range(NSTEP) if slot_of(n) == slot]


def ksteps_contrib(slot):
    return [n for n in KSTEPS if slot_of(n) + (2 if n < 2 or n > 3 else 3) == slot]


class Count:

    def __init__(self, sem, per_round=0, before=0):
        self.sem, self.per, self.before = sem, per_round, before

    def at(self, g, n):
        return n if g is None else g * self.per + (self.before + n)


class Chain:

    def __init__(self, sem, per_round=0, before=0):
        self.sem, self.per, self.before, self.n, self.g = sem, per_round, before, 0, 0

    def round(self, g):
        self.g, self.n = g, 0

    def add(self, ins):
        self.n += 1
        ins.then_inc(self.sem, 1)
        return ins

    def wait(self, eng):
        if self.n > 0:
            eng.wait_ge(self.sem, self.g * self.per + (self.before + self.n))


CONV_TILES = (0, 1, 4, 5)


def conv_index(k):
    return k if k < 2 * NB else k - 2 * NB


def halves(v, s):
    v = v.rearrange("p (n two s) -> p n two s", two=2, s=s)
    return v[:, :, 0, :], v[:, :, 1, :]


def blk(b):
    return slice(b * BW, (b + 1) * BW)


def chunk(c):
    return slice(c * P, (c + 1) * P)


def ranges(b):
    return [(0, 0, CTX), (1, CTX, BW)] if b == 0 else [(1, b * BW, (b + 1) * BW)]


K_ID, K_ONE, K_RESET, K_M64 = 0, 128, 256, 640
K_EPS, K_EPS4, K_1, K_W = 768, 769, 770, 772


def build(nc, cst_in, neg_in, masks_in, x_prompt, x_sample, c_in, state_ssm, state_hgrn, c_ctx, norm_mix_w, norm_ffn_w,
          ada_w, ada_b, w_in, ssd_conv_w, ssd_conv_b, ssd_dt_bias, ssd_a_log, ssd_d, ssd_norm_w, hgrn_norm_w,
          w_ssd_out, w_hgrn_out, w_out, ffn_w1, ffn_w3, ffn_w2, norm_final_w,
          y_prompt, y_sample, new_ssm, new_hgrn):
    with ExitStack() as ctx:
        def sb(name, shape, dt=F32, stack=ctx):
            return stack.enter_context(nc.sbuf_tensor(name, shape, dt))

        def sem(name):
            return ctx.enter_context(nc.semaphore(name))

        mem = {}
        cst = sb("cst", [P, K_W])
        vec = sb("vec", [P, V_END])
        mod = sb("mod", [P, 48, 2])
        raw = [sb(f"raw{i}", [P, KT, P]) for i in range(2)]
        banks = [ctx.enter_context(nc.psum_tensor(f"bank{i}", [P, 512], F32)) for i in range(8)]
        y_dram = nc.dram_tensor("y_scratch", [24, P, T], F32, kind="Internal").ap()
        gate_dram = nc.dram_tensor("gate_scratch", [16, P, T], F32, kind="Internal").ap()
        x_dram = nc.dram_tensor("x_scratch", [KT, P, T], F32, kind="Internal").ap()
        ident, ones = cst[:, K_ID:K_ID + P], cst[:, K_ONE:K_ONE + P]

        def x_rows(c):
            return x_prompt[0] if c == 0 else x_sample[0, (c - 1) * P:c * P, :]

        def w_tile(w, col, width=P):
            return w[:, col:col + width] if isinstance(col, int) else w[:, bass.ds(col, width)]

        def w_src(w, col, width=P):
            return w_tile(w, col, width).rearrange("(k p) c -> p k c", p=P)

        with ExitStack() as keep_h:
            masks = sb("masks", [P, LEVELS, P], U8, keep_h)
            h_hi = sb("h_hi", [P, KT, T], F32R, keep_h)
            h_lo = sb("h_lo", [P, KT, T], F32R, keep_h)
            with ExitStack() as scope:
                setup(nc, scope, sb, sem, locals())
            with ExitStack() as scope:
                mixers(nc, scope, sb, sem, locals())
        x_acc = sb("x_acc", [P, KT, T])
        with ExitStack() as scope:
            merge_and_ffn(nc, scope, sb, sem, locals())
        with ExitStack() as scope:
            last_norm(nc, scope, sb, sem, locals())


def setup(nc, scope, sb, sem, m):
    cst, masks, vec, mod, banks, ident = m["cst"], m["masks"], m["vec"], m["mod"], m["banks"], m["ident"]
    h_hi, h_lo, x_rows = m["h_hi"], m["h_lo"], m["x_rows"]
    ada_w = m["ada_w"][0]
    ADA_T = 6
    ADA_N = 48 // ADA_T
    rows = sb("rows", [P, 3, P], F32, scope)
    ada = [sb(f"ada{i}", [P, KT, ADA_T * P], F32, scope) for i in range(2)]
    xt = [sb(f"xt{i}", [P, D], F32, scope) for i in range(3)]
    xn_t = sb("xn_t", [P, KT, T], F32, scope)
    d_all = sb("d_all", [P, 32], F32, scope)
    junk = sb("junk", [P, D], F32, scope)
    stat = sb("stat", [P, NC, 3], F32, scope)
    cs = sb("cs", [P, KT, 2], F32, scope)
    cth = sb("cth", [P, 16], F32, scope)
    aff = sb("aff", [P, KT, 2], F32, scope)
    xs = [sb(f"xs{i}", [P, KT, P], F32, scope) for i in range(2)]

    consts_in, rows_in = sem("consts_in"), sem("rows_in")
    masks_in, masks_ok = sem("masks_in"), sem("masks_ok")
    x_in = [sem(f"x_in{i}") for i in range(3)]
    ada_in = [sem(f"ada_in{i}") for i in range(2)]
    rows_turned, vec_ready, c_ready = sem("rows_turned"), sem("vec_ready"), sem("c_ready")
    x_scaled, x_turned, x_kept = sem("x_scaled"), sem("x_turned"), sem("x_kept")
    x_kept2 = sem("x_kept2")
    raw_turned, raw_kept, raw_kept2 = sem("raw_turned"), sem("raw_kept"), sem("raw_kept2")
    xs_stored = [sem("xs_stored0"), sem("xs_stored1")]
    ada_used, mod_summed, aff_ready = sem("ada_used"), sem("mod_summed"), sem("aff_ready")
    h_made, rstd_ready, th_ready = sem("h_made"), sem("rstd_ready"), sem("th_ready")
    act_s, dve_s = sem("setup_act"), sem("setup_dve")

    def keep_dve(dve, c):
        dve.wait_ge(x_turned, c + 1)
        dve.tensor_copy(xn_t[:, 0:4, chunk(c)],
                        banks[2 + 2 * (c % 2)][:, :].rearrange("p (k t) -> p k t", t=P)
                        ).then_inc(x_kept, 1)

    with nc.Block() as block:
        @block.sync
        def _(sp):
            sp.dma_start(cst[:, :], m["cst_in"]).then_inc(consts_in, 16)
            sp.dma_start(junk[:, 0:LEVELS * P], m["masks_in"].rearrange("p l i -> p (l i)")).then_inc(masks_in, 16)

            def row(part, col, src, n):
                sp.dma_start(rows[part:part + n, col, :], src).then_inc(rows_in, 16)

            row(0, 0, m["ssd_conv_w"][0, 0:4, :].rearrange("k (t p) -> (k t) p", p=P), 128)
            row(0, 1, m["ssd_conv_w"][0, 4, :].rearrange("(t p) -> t p", p=P), 32)
            row(32, 1, m["ssd_conv_b"][0].rearrange("(t p) -> t p", p=P), 32)
            row(64, 1, m["ada_b"][0].rearrange("(t p) -> t p", p=P), 48)
            row(112, 1, m["norm_mix_w"][0].rearrange("(t p) -> t p", p=P), 8)
            row(120, 1, m["norm_ffn_w"][0].rearrange("(t p) -> t p", p=P), 8)
            row(0, 2, m["ssd_norm_w"][0].rearrange("(t p) -> t p", p=P), 16)
            row(16, 2, m["hgrn_norm_w"][0].rearrange("(t p) -> t p", p=P), 8)
            row(24, 2, m["c_in"][0].rearrange("(t p) -> t p", p=P), 8)
            row(32, 2, m["c_ctx"].rearrange("(t p) -> t p", p=P), 8)
            sp.dma_start(d_all[:, :], m["ssd_d"][0].rearrange("(a h) -> a h", a=1).broadcast_to([P, 32])
                         ).then_inc(rows_in, 16)
            for j in range(2):
                sp.dma_start(ada[j][:, :, :], ada_w[:, j * ADA_T * P:(j + 1) * ADA_T * P]
                             .rearrange("(k p) c -> p k c", p=P)).then_inc(ada_in[j], 16)
            for c in range(3):
                sp.dma_start(xt[c][:, :], x_rows(c)).then_inc(x_in[c], 16)
            for j in range(2, ADA_N):
                sp.wait_ge(ada_used, j - 1)
                sp.dma_start(ada[j % 2][:, :, :], ada_w[:, j * ADA_T * P:(j + 1) * ADA_T * P]
                             .rearrange("(k p) c -> p k c", p=P)).then_inc(ada_in[j % 2], 16)
                c = j + 1
                sp.wait_ge(x_turned, c - 2)
                sp.dma_start(xt[c % 3][:, :], x_rows(c)).then_inc(x_in[c % 3], 16)

        @block.tensor
        def _(pe):
            pe.wait_ge(consts_in, 16)
            pe.wait_ge(rows_in, 16 * 11)
            for i in range(3):
                n = P if i < 2 else 40
                last = pe.transpose(banks[0][:, i * P:i * P + n], rows[0:n, i, :], ident[0:n, 0:n])
            last.then_inc(rows_turned, 1)

            def turn_raw(c):
                pe.wait_ge(x_in[c % 3], 16 * (c // 3 + 1))
                if c > 0:
                    pe.wait_ge(raw_kept, c)
                    pe.wait_ge(raw_kept2, c)
                for k in range(KT):
                    last = pe.transpose(banks[6 + k // 4][:, (k % 4) * P:(k % 4 + 1) * P],
                                        xt[c % 3][:, k * P:(k + 1) * P], ident)
                last.then_inc(raw_turned, 1)

            def turn(c):
                pe.wait_ge(x_scaled, c + 1)
                if c >= 2:
                    pe.wait_ge(x_kept, c - 1)
                    pe.wait_ge(x_kept2, c - 1)
                for k in range(KT):
                    last = pe.transpose(banks[2 + 2 * (c % 2) + k // 4][:, (k % 4) * P:(k % 4 + 1) * P],
                                        xt[c % 3][:, k * P:(k + 1) * P], ident)
                last.then_inc(x_turned, 1)

            pe.wait_ge(c_ready, 2)
            for j in range(ADA_N):
                turn_raw(j)
                pe.wait_ge(ada_in[j % 2], 16 * (j // 2 + 1))
                for t in range(ADA_T):
                    col = 2 * (j * ADA_T + t)
                    for k in range(KT):
                        last = pe.matmul(banks[1][:, col:col + 2], ada[j % 2][:, k, t * P:(t + 1) * P],
                                         cs[:, k, :], start=(k == 0), stop=(k == KT - 1))
                last.then_inc(ada_used, 1)
                turn(j)
            turn_raw(NC - 1)
            turn(NC - 1)

        @block.scalar
        def _(act):
            ch = Chain(act_s)
            act.wait_ge(rows_turned, 1)
            ch.add(act.activation(vec[:, 0:256], banks[0][:, 0:256], ACT.Copy))
            for e in range(2):
                r = slice(e * HD, (e + 1) * HD)
                ch.add(act.activation(vec[r, V_D:V_END], d_all[r, e:32:2], ACT.Copy))
            act.activation(vec[:, 256:V_D], banks[0][:, 256:V_D], ACT.Copy).then_inc(vec_ready, 1)
            act.wait_ge(vec_ready, 1)
            act.activation(cth[:, :], vec[:, V_C:V_C + 16], ACT.Tanh, scale=0.5).then_inc(th_ready, 1)
            ch.wait(act)
            ch.add(act.mul(vec[:, 0:V_ADAB], vec[:, 0:V_ADAB], 0.5))
            ch.add(act.mul(vec[:, V_HGRN:V_HGRN + 8], vec[:, V_HGRN:V_HGRN + 8], 0.5))

            def rstd(c):
                act.wait_ge(x_in[c % 3], 16 * (c // 3 + 1))
                ch.wait(act)
                ch.add(act.activation(junk[:, :], xt[c % 3][:, :], ACT.Square, accum_out=stat[:, c, 0:1]))
                ch.wait(act)
                ch.add(act.activation(stat[:, c, 1:2], stat[:, c, 0:1], ACT.Ln, scale=1.0 / D,
                                      bias=cst[:, K_EPS:K_EPS + 1]))
                ch.wait(act)
                act.activation(stat[:, c, 2:3], stat[:, c, 1:2], ACT.Exp, scale=-0.5).then_inc(rstd_ready, 1)

            def keep(c):
                act.wait_ge(x_turned, c + 1)
                act.activation(xn_t[:, 4:8, chunk(c)],
                               banks[3 + 2 * (c % 2)][:, :].rearrange("p (k t) -> p k t", t=P),
                               ACT.Copy).then_inc(x_kept2, 1)

            act.wait_ge(masks_ok, 1)
            for c in range(NC + 1):
                if c < NC:
                    rstd(c)
                    act.wait_ge(raw_turned, c + 1)
                    if c >= 2:
                        act.wait_ge(xs_stored[c % 2], 16 * (c // 2))
                    act.activation(xs[c % 2][:, 4:8, :], banks[7][:, :].rearrange("p (k t) -> p k t", t=P),
                                   ACT.Copy).then_inc(raw_kept2, 1)
                    act.wait_ge(raw_kept2, c + 1)
                    act.wait_ge(raw_kept, c + 1)
                    act.dma_start(m["x_dram"][:, :, chunk(c)].rearrange("k p t -> p k t"),
                                  xs[c % 2][:, :, :]).then_inc(xs_stored[c % 2], 16)
                if c > 0:
                    keep(c - 1)
            act.wait_ge(aff_ready, 1)
            act.wait_ge(x_kept2, NC)
            act.wait_ge(x_kept, NC)
            for b in range(NB):
                for k in range(KT):
                    for who, lo, hi in ranges(b):
                        last = act.activation(xn_t[:, k, lo:hi], xn_t[:, k, lo:hi], ACT.Identity,
                                              scale=aff[:, k, who:who + 1], bias=mod[:, k, who:who + 1])
                    last.then_inc(h_made, 1)
            for i in range(2):
                act.wait_ge(xs_stored[i], 16 * ((NC + 1 - i) // 2))

        @block.vector
        def _(dve):
            ch = Chain(dve_s)
            dve.wait_ge(masks_in, 16)
            dve.tensor_copy(masks[:, :, :].rearrange("p l i -> p (l i)"), junk[:, 0:LEVELS * P]
                            ).then_inc(masks_ok, 1)
            dve.wait_ge(th_ready, 1)
            for who, col in ((1, V_C), (0, V_CCTX)):
                dve.scalar_tensor_tensor(cs[:, :, who], cth[:, col - V_C:col - V_C + 8], 1.0,
                                         vec[:, col:col + 8], ALU.add, ALU.mult).then_inc(c_ready, 1)
            for c in range(NC):
                dve.wait_ge(raw_turned, c + 1)
                if c >= 2:
                    dve.wait_ge(xs_stored[c % 2], 16 * (c // 2))
                dve.tensor_copy(xs[c % 2][:, 0:4, :], banks[6][:, :].rearrange("p (k t) -> p k t", t=P)
                                ).then_inc(raw_kept, 1)
                dve.wait_ge(rstd_ready, c + 1)
                dve.tensor_scalar(xt[c % 3][:, :], xt[c % 3][:, :], stat[:, c, 2:3], None,
                                  ALU.mult).then_inc(x_scaled, 1)
                if c > 0:
                    keep_dve(dve, c - 1)
            keep_dve(dve, NC - 1)
            dve.wait_ge(ada_used, ADA_N)
            adab = vec[:, V_ADAB:V_ADAB + 48].rearrange("p (m a) -> p m a", a=1).broadcast_to([P, 48, 2])
            ch.add(dve.scalar_tensor_tensor(mod[:, :, :], banks[1][:, 0:96].rearrange("p (m a) -> p m a", a=2),
                                            0.5, adab, ALU.mult, ALU.add))
            ch.wait(dve)
            mix = vec[:, V_MIX:V_MIX + 8].rearrange("p (m a) -> p m a", a=1).broadcast_to([P, 8, 2])
            ffn = vec[:, V_FFN:V_FFN + 8].rearrange("p (m a) -> p m a", a=1).broadcast_to([P, 8, 2])
            dve.scalar_tensor_tensor(aff[:, :, :], mod[:, 8:16, :], 1.0, mix, ALU.add,
                                     ALU.mult).then_inc(aff_ready, 1)
            ch.add(dve.scalar_tensor_tensor(mod[:, 32:40, :], mod[:, 32:40, :], 1.0, ffn, ALU.add, ALU.mult))
            ch.add(dve.tensor_scalar(mod[:, 16:24, :], mod[:, 16:24, :], 0.5, None, ALU.mult))
            ch.add(dve.tensor_scalar(mod[:, 40:48, :], mod[:, 40:48, :], 0.5, None, ALU.mult))
            n = 0
            for b in range(NB):
                for k in range(KT):
                    n += 1
                    dve.wait_ge(h_made, n)
                    ch.add(dve.tensor_copy(h_hi[:, k, blk(b)], xn_t[:, k, blk(b)]))
                    ch.wait(dve)
                    ch.add(dve.tensor_tensor(h_lo[:, k, blk(b)], xn_t[:, k, blk(b)],
                                             h_hi[:, k, blk(b)].bitcast(F32), ALU.subtract))



def mixers(nc, scope, sb, sem, m):
    cst, masks, vec, raw, banks = m["cst"], m["masks"], m["vec"], m["raw"], m["banks"]
    ident, ones = m["ident"], m["ones"]
    h_hi, h_lo, w_src = m["h_hi"], m["h_lo"], m["w_src"]
    w_in, y_dram, gate_dram = m["w_in"][0], m["y_dram"], m["gate_dram"]
    S = banks[2:8]
    reset = cst[:, K_RESET:K_RESET + BW]

    w_hi = [sb(f"w_hi{i}", [P, KT, P], F32R, scope) for i in range(2)]
    w_lo = [sb(f"w_lo{i}", [P, KT, P], F32R, scope) for i in range(2)]
    pad = [sb(f"pad{b}", [P, ROWS, GRID + 4], F32, scope) for b in range(NB)]
    acc = [sb(f"acc{i}", [P, BW], F32, scope) for i in range(2)]
    th = [sb(f"th{i}", [P, BW], F32, scope) for i in range(2)]
    x_t = sb("x_t", [P, 2, T], F32, scope)
    z_t = sb("z_t", [P, 2, T], F32, scope)
    b_t = sb("b_t", [P, T], F32, scope)
    c_t = sb("c_t", [P, T], F32, scope)
    f_t = sb("f_t", [P, T], F32, scope)
    g_t = sb("g_t", [P, T], F32, scope)
    kf_t = sb("kf_t", [P, T], F32, scope)
    kb_t = sb("kb_t", [P, T], F32, scope)
    q_t = sb("q_t", [P, T], F32, scope)
    s_t = sb("s_t", [P, T], F32, scope)
    v_tok = sb("v_tok", [P, NC, P], F32, scope)
    cum = sb("cum", [64, T], F32, scope)
    tok = sb("tok", [P, 3, NC, 64], F32, scope)
    dec = sb("dec", [P, NC, 64], F32, scope)
    tok_g = sb("tok_g", [P, 3, NC, 8], F32, scope)
    dec_g = sb("dec_g", [P, NC, 8], F32, scope)
    sel = sb("sel", [64, 8, P], F32, scope)
    taps = sb("taps", [P, 4, TAPS + 1], F32, scope)
    vec_g = sb("vec_g", [P, 5], F32, scope)
    id_bf = sb("id_bf", [P, P], BF16, scope)
    neg_bf = [sb(f"neg_bf{d}", [P, P], BF16, scope) for d in range(2)]
    cols = sb("cols", [64, 4], F32, scope)

    st_in = sb("st_in", [P, 4, P], F32, scope)
    so_h = sb("so_h", [P, 2, P], F32, scope)
    with ExitStack() as ssd_scope:
        xb = [sb(f"xb{i}", [P, 512], F32, ssd_scope) for i in range(4)]
        xp = sb("xp", [P, 2, GW], F32, ssd_scope)
        s_b = sb("s_b", [P, NC - 1, GW], F32, ssd_scope)
        s_f = sb("s_f", [P, GW], F32, ssd_scope)
        t_off = sb("t_off", [P, 512], F32, ssd_scope)
        y_tok = t_off[:, 0:GW]
        me = sb("me", [P, 2048], F32, ssd_scope)
        mm = me[:, 0:1024].rearrange("p (e n) -> p e n", e=2)
        ex = me[:, 1024:2048]
        rstd = me[:, 2048 - T:2048]
    with ExitStack() as hgrn_scope:
        qk = [sb(f"qk{i}", [P, 2, BW], F32, hgrn_scope) for i in range(4)]
        ktok = [sb(f"ktok{i}", [P, BW], F32, hgrn_scope) for i in range(4)]
        at = [sb(f"at{i}", [P, BW], F32, hgrn_scope) for i in range(2)]
        hs_f = sb("hs_f", [P, NC - 1, P], F32, hgrn_scope)
        hs_b = sb("hs_b", [P, NC - 1, P], F32, hgrn_scope)
        hdec = sb("hdec", [P, 2, NC], F32, hgrn_scope)
    dt_v, dt_a, dt_b, dt_c, dt_d, dt_e = f_t, g_t, kf_t, kb_t, q_t, s_t

    w_landed = [sem("w_landed0"), sem("w_landed1")]
    w_high, w_split = Count(sem("w_high"), TILES_GROUP), Count(sem("w_split"), TILES_GROUP)
    unit_done = Count(sem("unit_done"), UNITS_GROUP)
    bank_free = [sem("bank_free0"), sem("bank_free1")]
    cols_in, cols_ok, bf_ok = sem("cols_in"), sem("cols_ok"), sem("bf_ok")
    pads_zero, taps_ok = sem("pads_zero"), sem("taps_ok")
    conved, silu_done = Count(sem("conved"), 4 * NB, 4 * NB), Count(sem("silu_done"), 4 * NB, 4 * NB)
    th_ok = Count(sem("th_ok"), 8 * NB, 6 * NB)
    gate_stored = [sem("gate_stored0"), sem("gate_stored1")]
    v_turned, v_kept = sem("v_turned"), sem("v_kept")
    dt_act, dt_dve, dt_turned, dt_kept = sem("dt_act"), sem("dt_dve"), sem("dt_turned"), sem("dt_kept")
    f_raw, f_log, f_lnk, f_ready = sem("f_raw"), sem("f_log"), sem("f_lnk"), sem("f_ready")
    k_ready = sem("k_ready")
    act_s = Chain(sem("act_step"), ACT_ROUND)
    dve_s = Chain(sem("dve_step"), DVE_ROUND)
    NTR, NA1, NA1P = 1 + 7 + NC, 7, 4
    st_loaded = sem("st_loaded")
    tr_ready, tr_kept = Count(sem("tr_ready"), NTR), Count(sem("tr_kept"), NTR)
    grp_ready, sel_ready = sem("grp_ready"), sem("sel_ready")
    xp_ready = Count(sem("xp_ready"), NA1P + NC)
    ctb_ready, ctb_used = Count(sem("ctb_ready"), NA1P), Count(sem("ctb_used"), NA1P)
    arg_ready, exp_ready = Count(sem("arg_ready"), NC), Count(sem("exp_ready"), NC)
    sum_ready, m_ready = Count(sem("sum_ready"), NC), Count(sem("m_ready"), NC)
    y_ready, y_made = Count(sem("y_ready"), NC), Count(sem("y_made"), NC)
    yt_ready, yt_made = Count(sem("yt_ready"), NC), Count(sem("yt_made"), NC)
    sq_ready, ms_ready = Count(sem("sq_ready"), NB), Count(sem("ms_ready"), NB)
    rstd_ok, y_final, y_stored, so_stored = sem("rstd_ok"), sem("y_final"), sem("y_stored"), sem("so_stored")
    NK, NM = len(KSTEPS), len(MSTEPS)
    hs_loaded, hdec_ok = sem("hs_loaded"), sem("hdec_ok")
    arg_made, exp_made = Count(sem("arg_made"), len(ASTEPS)), Count(sem("exp_made"), len(ESTEPS))
    qk_ready = Count(sem("qk_ready"), NSTEP)
    kt_ready, kt_kept = Count(sem("kt_ready"), NK), Count(sem("kt_kept"), NK)
    kc_ready, kc_used = Count(sem("kc_ready"), NK), Count(sem("kc_used"), NK)
    lv_ready, lv_used = Count(sem("lv_ready"), NM), Count(sem("lv_used"), NM)
    merge_clear = sem("merge_clear")
    o_ready, o_kept = Count(sem("o_ready"), NB), Count(sem("o_kept"), NB)
    hms_ready, hms_kept = Count(sem("hms_ready"), NB), Count(sem("hms_kept"), NB, before=1)
    hrstd_ok, o_final, o_stored, soh_stored = sem("hrstd_ok"), sem("o_final"), sem("o_stored"), sem("soh_stored")

    def numbered(const, g):
        if g is None:
            return const % 2, const // 2, const
        return const % 2, g * (UNITS_GROUP // 2) + const // 2, g * UNITS_GROUP + const

    def used_by_pe(eng, g, n):
        for count, steps in ((kt_ready, KSTEPS), (lv_ready, MSTEPS), (o_ready, QSTEPS)):
            if n in steps:
                eng.wait_ge(count.sem, count.at(g, steps.index(n) + 1))

    def a_unit(g, k):
        return numbered(UNITS_BEFORE + k, g)

    def b_unit(g, k):
        return numbered(NB + k, None) if g is None else numbered(UNITS_BEFORE + SLOTS + k, g)

    def tile(g, t):
        if g is None:
            return t % 2, t // 2, t
        n = TILES_BEFORE + t
        return n % 2, g * (TILES_GROUP // 2) + n // 2, g * TILES_GROUP + n

    PRO_COLS = [(COL_DT, 64), (COL_B, P), (COL_C, P), (COL_Z, P), (COL_Z + P, P), (COL_X, P), (COL_X + P, P)]
    A_COLS = [(COL_FF, P), (COL_FB, P), (COL_Q, P), (COL_G, P), (COL_GATE, P), (COL_I, P)]
    B_COLS = [(COL_B, P), (COL_C, P), (COL_Z, GW), (COL_Z + P, GW), (COL_X, GW), (COL_X + P, GW)]

    with nc.Block() as block:
        @block.sync
        def _(sp):
            def load(g, t, col, width=P):
                i, _, n = tile(g, t)
                if not (g is None and t < 2):
                    sp.wait_ge(w_split.sem, n - 1)
                sp.dma_start(raw[i][:, :, 0:width], w_src(w_in, col, width)).then_inc(w_landed[i], 16)

            def stage_a(g):
                for t, (base, step) in enumerate(A_COLS):
                    load(g, t, g * step + base)

            def stores(g, last):
                sp.wait_ge(y_final, g + 1)
                dst = y_dram[2 * g:2 * g + 2] if isinstance(g, int) else y_dram[bass.ds(g * 2, 2)]
                sp.dma_start(dst.rearrange("t p n -> p t n"), x_t[:, :, :]).then_inc(y_stored, 16)
                hs = slice(HPG * g, HPG * (g + 1)) if isinstance(g, int) else bass.ds(g * HPG, HPG)
                for d in range(2):
                    sp.dma_start(m["new_ssm"][0, 0, d, hs].rearrange("(t e) p n -> (e p) t n", e=2),
                                 st_in[:, 2 * d:2 * d + 2, :]).then_inc(so_stored, 16)

            def store_h(g):
                sp.wait_ge(kc_used.sem, kc_used.at(g, 4))
                hh = slice(g, g + 1) if isinstance(g, int) else bass.ds(g, 1)
                for d in range(2):
                    sp.dma_start(m["new_hgrn"][0, 0, d, hh].rearrange("a k v -> k (a v)"),
                                 so_h[:, d, :]).then_inc(soh_stored, 16)

            sp.dma_start(cols[:, 0:1], m["ssd_dt_bias"][0].rearrange("d (h a) -> (d h) a", a=1)
                         ).then_inc(cols_in, 16)
            sp.dma_start(cols[:, 1:2], m["ssd_a_log"][0].rearrange("d (h a) -> (d h) a", a=1)
                         ).then_inc(cols_in, 16)
            sp.dma_start(acc[0][:, 0:2 * P], m["neg_in"].rearrange("p d i -> p (d i)")).then_inc(cols_in, 16)
            for t, (col, _) in enumerate(PRO_COLS):
                load(None, t, col, HD if t == 0 else P)

            with sp.Fori(0, G - 1) as g:
                stage_a(g)
                for t, (base, step) in enumerate(B_COLS):
                    if t == 4:
                        stores(g, False)
                    load(g, 6 + t, g * step + (base + step))
                store_h(g)
            g = G - 1
            stage_a(g)
            for t in range(8):
                if t == 4:
                    stores(g, True)
                load(g, 6 + t, COL_GATE + D + t * P)
            store_h(g)
            sp.wait_ge(y_stored, 16 * G)
            sp.wait_ge(so_stored, 32 * (G + 1))
            sp.wait_ge(soh_stored, 32 * (G + 1))
            sp.wait_ge(o_stored, 16 * (G + 1))
            for i in range(2):
                sp.wait_ge(gate_stored[i], 16 * (G * (1 + i) + 4 * NB))

        @block.tensor
        def _(pe):
            def project(g, t, b, cols_n=P):
                i, _, n = tile(g, t)
                ui, used, _ = numbered(t * NB + b, None) if g is None else a_unit(g, t * NB + b)
                if b == 0:
                    pe.wait_ge(w_split.sem, n + 1)
                if not (g is None and t * NB + b < 2):
                    pe.wait_ge(bank_free[ui], used)
                out = banks[ui][0:cols_n, 0:BW]
                for k in range(KT):
                    for j, (w, h) in enumerate(((w_hi, h_hi), (w_hi, h_lo), (w_lo, h_hi))):
                        last = pe.matmul(out, w[i][:, k, 0:cols_n], h[:, k, blk(b)],
                                         start=(k == 0 and j == 0), stop=(k == KT - 1 and j == 2))
                last.then_inc(unit_done.sem, 1)

            def turn_xb(c, bank, with_cb):
                for e in range(2):
                    last = pe.transpose(bank[:, e * P:(e + 1) * P], x_t[:, e, chunk(c)], ident)
                last = pe.transpose(bank[:, GW:GW + P], b_t[:, chunk(c)], ident)
                if with_cb:
                    last = pe.matmul(bank[:, GW + P:GW + 2 * P], b_t[:, chunk(c)], c_t[:, chunk(c)],
                                     start=True, stop=True)
                return last

            def ssd(g, k):
                if k == 0:
                    pe.wait_ge(hms_kept.sem, hms_kept.at(g, 0))
                    pe.wait_ge(st_loaded, (g + 1) * 32)
                    for j in range(4):
                        last = pe.transpose(S[3][:, j * P:(j + 1) * P], st_in[:, j, :], ident)
                    last.then_inc(tr_ready.sem, 1)
                    pe.wait_ge(silu_done.sem, silu_done.at(g, 0))
                if k < NA1P:
                    if k > 0:
                        pe.wait_ge(tr_kept.sem, tr_kept.at(g, 2 * k + 1))
                    turn_xb(8 - 2 * k, S[0], False).then_inc(tr_ready.sem, 1)
                    if k < 3:
                        turn_xb(7 - 2 * k, S[1], False).then_inc(tr_ready.sem, 1)
                if 2 <= k < 2 + NA1P:
                    p = k - 2
                    pe.wait_ge(xp_ready.sem, xp_ready.at(g, p + 1))
                    if p > 0:
                        pe.wait_ge(ctb_used.sem, ctb_used.at(g, p))
                    for j in range(2 if p < 3 else 1):
                        last = pe.matmul(S[2][:, j * GW:(j + 1) * GW], xb[2 * (p % 2) + j][:, GW:GW + P],
                                         xp[:, j, :], start=True, stop=True)
                    last.then_inc(ctb_ready.sem, 1)
                if 4 <= k < 4 + NC:
                    c = k - 4
                    pe.wait_ge(tr_kept.sem, tr_kept.at(g, 8 + c))
                    turn_xb(c, S[0], True).then_inc(tr_ready.sem, 1)
                    if c > 0:
                        pe.wait_ge(exp_ready.sem, exp_ready.at(g, c))
                    else:
                        pe.wait_ge(sel_ready, g + 1)
                    for d in range(2):
                        pe.matmul(S[3 + d][:, :].rearrange("p (h i) -> p h i", i=P), id_bf[:, :],
                                  neg_bf[d][:, :].rearrange("p (a i) -> p a i", a=1).broadcast_to([P, HPG, P]),
                                  start=True, stop=False, skip_group_check=True)
                        for h in range(HPG):
                            last = pe.matmul(S[3 + d][:, h * P:(h + 1) * P], sel[:, d * HPG + h, :],
                                             cum[:, chunk(c)], start=False, stop=(h == HPG - 1),
                                             skip_group_check=True)
                    last.then_inc(arg_ready.sem, 1)
                if 6 <= k < 6 + NC:
                    c = k - 6
                    pe.wait_ge(m_ready.sem, m_ready.at(g, c + 1))
                    pe.wait_ge(xp_ready.sem, xp_ready.at(g, NA1P + c + 1))
                    if c > 0:
                        pe.wait_ge(y_made.sem, y_made.at(g, c))
                    else:
                        pe.wait_ge(ctb_used.sem, ctb_used.at(g, NA1P))
                    x, bt = xb[c % 2], xb[c % 2][:, GW:GW + P]
                    for h in range(HPG):
                        last = pe.matmul(S[2][:, h * HD:(h + 1) * HD], mm[:, c % 2, h * P:(h + 1) * P],
                                         x[:, h * HD:(h + 1) * HD], start=True, stop=True)
                    if c == 0:
                        for e in range(2):
                            pe.matmul(S[2][:, GW + e * P:GW + (e + 1) * P], xp[:, 0, e * P:(e + 1) * P], bt,
                                      start=True, stop=True)
                        for e in range(2):
                            last = pe.matmul(S[5][:, e * P:(e + 1) * P], xp[:, 1, e * P:(e + 1) * P], bt,
                                             start=True, stop=True)
                    else:
                        if c < NC - 1:
                            pe.matmul(S[2][:, GW:2 * GW], bt, xp[:, c % 2, :], start=True, stop=True)
                        pe.matmul(S[5][:, 0:GW], c_t[:, chunk(c)], s_f[:, :], start=True, stop=True)
                        last = pe.matmul(S[5][:, GW:2 * GW], c_t[:, chunk(c)], s_b[:, c - 1, :],
                                         start=True, stop=True)
                    last.then_inc(y_ready.sem, 1)
                if 7 <= k < 7 + NC:
                    c = k - 7
                    pe.wait_ge(y_made.sem, y_made.at(g, c + 1))
                    if c > 0:
                        pe.wait_ge(yt_made.sem, yt_made.at(g, c))
                    for e in range(2):
                        last = pe.transpose(S[1][:, e * P:(e + 1) * P], y_tok[:, e * P:(e + 1) * P], ident)
                    last.then_inc(yt_ready.sem, 1)
                if k >= SLOTS - NB:
                    b = k - (SLOTS - NB)
                    bank = (S[3], S[4], S[0])[b]
                    pe.wait_ge(sq_ready.sem, sq_ready.at(g, b + 1))
                    for e in range(2):
                        last = pe.matmul(bank[:, 0:BW], ones, mm[:, e, 0:BW], start=(e == 0), stop=(e == 1))
                    last.then_inc(ms_ready.sem, 1)

            def turn_v(g, b):
                bank = (S[5], S[2], S[5])[b]
                ui, used, _ = a_unit(g, 5 * NB + b)
                pe.wait_ge(bank_free[ui], used + 1)
                if b == 2:
                    pe.wait_ge(v_kept, g * NB + 1)
                for j in range(CB):
                    last = pe.transpose(bank[:, chunk(j)], th[ui][:, chunk(j)], ident)
                last.then_inc(v_turned, 1)

            def hgrn(g, k):
                if k == 0:
                    return
                for n in steps_in(k - 1):
                    kind, b, lv = STEPS[n]
                    q = qk[n % 4]
                    pe.wait_ge(qk_ready.sem, qk_ready.at(g, n + 1))
                    if kind in ("kb", "kf"):
                        i = KSTEPS.index(n)
                        bank = (S[5], S[0], S[1], S[2], S[5], S[5])[i]
                        if i > 3:
                            pe.wait_ge(kt_kept.sem, kt_kept.at(g, 1 if i == 4 else i))
                        else:
                            pe.wait_ge(rstd_ok, g + 1)
                            pe.wait_ge(v_kept, (g + 1) * NB)
                        for j in range(CB):
                            last = pe.transpose(bank[:, chunk(j)], q[:, 0, chunk(j)], ident)
                        last.then_inc(kt_ready.sem, 1)
                    elif kind in ("lv", "dg"):
                        i = MSTEPS.index(n)
                        pe.wait_ge(kt_kept.sem, kt_kept.at(g, 4))
                        if i > 2:
                            pe.wait_ge(lv_used.sem, lv_used.at(g, i - 2))
                        for j in range(CB):
                            rhs = q[:, 0, chunk(j)] if kind == "lv" else q_t[:, chunk(b * CB + j)]
                            last = pe.matmul(S[i % 3][:, chunk(j)], q[:, 1, chunk(j)], rhs,
                                             start=True, stop=True)
                        last.then_inc(lv_ready.sem, 1)
                    else:
                        pe.wait_ge(lv_used.sem, lv_used.at(g, 8 * (b + 1)))
                        pe.wait_ge(kc_used.sem, kc_used.at(g, 4 + b))
                        if b > 0:
                            pe.wait_ge(hms_kept.sem, hms_kept.at(g, b))
                        for j in range(CB):
                            c = b * CB + j
                            last = pe.matmul(S[3][:, chunk(j)], v_tok[:, c, :], at[b % 2][:, chunk(j)],
                                             start=True, stop=(c == 0))
                            if c > 0:
                                pe.matmul(S[3][:, chunk(j)], hs_f[:, c - 1, :], q[:, 0, chunk(j)],
                                          start=False, stop=False)
                                last = pe.matmul(S[3][:, chunk(j)], hs_b[:, c - 1, :], q[:, 1, chunk(j)],
                                                 start=False, stop=True)
                        last.then_inc(o_ready.sem, 1)
                for n in ksteps_contrib(k):
                    i = KSTEPS.index(n)
                    kind, b, _ = STEPS[n]
                    bank = S[4] if i % 2 == 0 or i > 3 else S[3]
                    pe.wait_ge(kt_kept.sem, kt_kept.at(g, i + 1))
                    if i in (2, 3):
                        pe.wait_ge(kc_used.sem, kc_used.at(g, i - 1))
                    if i > 3:
                        pe.wait_ge(kc_used.sem, kc_used.at(g, i))
                    kt = ktok[i if i < 4 else 0]
                    for j in range(CB):
                        last = pe.matmul(bank[:, chunk(j)], kt[:, chunk(j)], v_tok[:, b * CB + j, :],
                                         start=True, stop=True)
                    last.then_inc(kc_ready.sem, 1)
                for n in QSTEPS:
                    if slot_of(n) + 2 == k:
                        b = STEPS[n][1]
                        pe.wait_ge(o_kept.sem, o_kept.at(g, b + 1))
                        pe.matmul(S[3][:, 0:BW], ones, ktok[2][:, :], start=True,
                                  stop=True).then_inc(hms_ready.sem, 1)

            pe.wait_ge(bf_ok, 3)
            for t in range(TILES_BEFORE):
                for b in range(NB):
                    project(None, t, b, 64 if t == 0 else P)
            pe.wait_ge(dt_dve, DT_DVE)
            pe.wait_ge(dt_act, DT_ACT)
            for a, src in enumerate((dt_d, dt_e, dt_b)):
                for c in range(NC):
                    i = a * NC + c
                    pe.transpose(S[i // 8][:, (i % 8) * 64:(i % 8 + 1) * 64], src[0:64, chunk(c)],
                                 ident[0:64, 0:64])
            flat = v_tok[0:64, :, :].rearrange("p c t -> p (c t)")
            for j in range(2):
                last = pe.matmul(S[4 + j][:, 0:288], ones[0:64, :], flat[:, j * 288:(j + 1) * 288],
                                 start=True, stop=True)
            last.then_inc(dt_turned, 1)
            pe.wait_ge(dt_kept, 1)

            with pe.Fori(0, G - 1) as g:
                for k in range(SLOTS):
                    project(g, k // NB, k % NB)
                    ssd(g, k)
                    if k >= SLOTS - 2:
                        turn_v(g, k - (SLOTS - 2))
                for k in range(SLOTS):
                    project(g, 6 + k // NB, k % NB)
                    if k == 0:
                        turn_v(g, 2)
                    hgrn(g, k)
            g = G - 1
            for k in range(SLOTS):
                project(g, k // NB, k % NB)
                ssd(g, k)
                if k >= SLOTS - 2:
                    turn_v(g, k - (SLOTS - 2))
            for k in range(8 * NB):
                project(g, 6 + k // NB, k % NB)
                if k == 0:
                    turn_v(g, 2)
                hgrn(g, k)

        @block.scalar
        def _(act):
            ch = act_s

            def wait(count, g, n):
                act.wait_ge(count.sem, count.at(g, n))

            def high(g, t):
                i, used, n = tile(g, t)
                act.wait_ge(w_landed[i], used * 16 + 16)
                if not (g is None and t < 2):
                    act.wait_ge(unit_done.sem, (n - 1) * NB)
                act.activation(w_hi[i][:, :, :], raw[i][:, :, :], ACT.Copy).then_inc(w_high.sem, 1)

            def conv_tanh(g, k):
                ui = b_unit(g, k)[0]
                ci = conv_index(k)
                wait(conved, g, ci + 1)
                act.activation(th[ui][:, :], acc[ui][:, :], ACT.Tanh).then_inc(th_ok.sem, 1)

            def b_evac(g, k):
                t, b = divmod(k, NB)
                ui, used, n = b_unit(g, k)
                act.wait_ge(unit_done.sem, n + 1)
                bank = banks[ui]
                if t in CONV_TILES:
                    ci = conv_index(k)
                    if g is not None or ci >= NB:
                        wait(conved, g, ci - NB + 1)
                    else:
                        act.wait_ge(pads_zero, NB)
                    src = bank[:, 0:BW].rearrange("p (r c) -> p r c", c=GRID)
                    if b == 0:
                        act.activation(pad[0][:, 0, GRID + 2:GRID + 4], bank[:, GRID:GRID + 2], ACT.Copy)
                        act.activation(pad[0][:, 1, 0:2], bank[:, GRID - 2:GRID], ACT.Copy)
                    act.activation(pad[b][:, :, 2:2 + GRID], src, ACT.Copy).then_inc(bank_free[ui], 1)
                else:
                    if t == 2 and k >= NB * 2:
                        wait(silu_done, g, min(k - 1, 6))
                    act.activation(th[ui][:, :], bank[:, 0:BW], ACT.Tanh, scale=0.5).then_inc(th_ok.sem, 1)

            def b_th_free(g, k):
                ci = conv_index(k)
                if k < 2:
                    if g is not None:
                        act.wait_ge(v_turned, g * NB + (k + 2))
                elif ci >= 2 and k not in (12, 13):
                    wait(silu_done, g, ci - 1)

            def a_evac(g, k):
                t, b = divmod(k, NB)
                ui, used, n = a_unit(g, k)
                act.wait_ge(unit_done.sem, n + 1)
                bank = banks[ui][:, 0:BW]
                if t < 2:
                    u, e = ((kf_t, f_t), (kb_t, g_t))[t]
                    act.wait_ge(o_final, g + 1)
                    act.activation(u[:, blk(b)], bank, ACT.Copy)
                    act.activation(e[:, blk(b)], bank, ACT.Abs).then_inc(bank_free[ui], 1)
                    act.wait_ge(bank_free[ui], used + 1)
                    ch.add(act.activation(e[:, blk(b)], e[:, blk(b)], ACT.Exp, scale=-1.0))
                elif t < 4:
                    if k == 6 or k == 7:
                        wait(silu_done, g, 0)
                    act.activation(th[ui][:, :], bank, ACT.Tanh, scale=0.5).then_inc(th_ok.sem, 1)
                elif t == 4:
                    if b == 2:
                        act.wait_ge(gate_stored[ui], g * 32 + 16)
                    act.activation(th[ui][:, :], bank, ACT.Tanh, scale=0.5).then_inc(bank_free[ui], 1)
                    act.wait_ge(bank_free[ui], used + 1)
                    dst = gate_dram[g:g + 1] if isinstance(g, int) else gate_dram[bass.ds(g, 1)]
                    act.dma_start(dst[:, :, blk(b)].rearrange("a p n -> p (a n)"),
                                  th[ui][:, :]).then_inc(gate_stored[ui], 16)
                else:
                    if b == 0:
                        act.wait_ge(gate_stored[ui], g * 16 + 16)
                    elif b == 1:
                        act.wait_ge(gate_stored[ui], g * 32 + 32)
                    else:
                        act.wait_ge(v_turned, g * NB + 1)
                    act.activation(th[ui][:, :], bank, ACT.Copy).then_inc(bank_free[ui], 1)

            def keep_v(g, b):
                bank = (S[5], S[2], S[5])[b]
                act.wait_ge(v_turned, g * NB + (b + 1))
                act.activation(v_tok[:, b * CB:(b + 1) * CB, :].rearrange("p c t -> p (c t)"), bank[:, 0:BW],
                               ACT.Copy).then_inc(v_kept, 1)

            def ssd(g, k):
                if k == 0:
                    act.wait_ge(so_stored, g * 32 + 32)
                    hs = slice(HPG * g, HPG * (g + 1)) if isinstance(g, int) else bass.ds(g * HPG, HPG)
                    for d in range(2):
                        act.dma_start(st_in[:, 2 * d:2 * d + 2, :],
                                      m["state_ssm"][0, 0, d, hs].rearrange("(t e) p n -> (e p) t n", e=2)
                                      ).then_inc(st_loaded, 16)
                if k == 1:
                    wait(tr_ready, g, 1)
                    act.activation(s_f[:, :], S[3][:, 0:GW], ACT.Copy)
                    act.activation(s_b[:, NC - 2, :], S[3][:, GW:2 * GW], ACT.Copy).then_inc(tr_kept.sem, 1)
                if 1 <= k < 1 + NA1P:
                    p = k - 1
                    if p >= 2:
                        wait(ctb_ready, g, p - 1)
                    for j in range(2 if p < 3 else 1):
                        wait(tr_ready, g, 2 + 2 * p + j)
                        act.activation(xb[2 * (p % 2) + j][:, 0:BW], S[j][:, 0:BW],
                                       ACT.Copy).then_inc(tr_kept.sem, 1)
                if 5 <= k < 5 + NC:
                    c = k - 5
                    wait(tr_ready, g, 9 + c)
                    if c < 2:
                        wait(ctb_ready, g, 3)
                    else:
                        wait(y_ready, g, c - 1)
                    act.activation(xb[c % 2][:, :], S[0][:, :], ACT.Copy).then_inc(tr_kept.sem, 1)
                    wait(arg_ready, g, c + 1)
                    if c == 0:
                        act.wait_ge(grp_ready, g + 1)
                    else:
                        wait(sum_ready, g, c)
                    for d in range(2):
                        for h in range(HPG):
                            o = d * 512 + h * P
                            last = act.activation(ex[:, o:o + P], S[3 + d][:, h * P:(h + 1) * P], ACT.Exp,
                                                  bias=tok_g[:, 0, c, d * HPG + h:d * HPG + h + 1])
                    last.then_inc(exp_ready.sem, 1)
                if k >= SLOTS - NB:
                    b = k - (SLOTS - NB)
                    wait(yt_made, g, CB * (b + 1))
                    if b == 0:
                        wait(y_ready, g, NC)
                    else:
                        wait(ms_ready, g, b)
                    act.activation(mm[:, :, 0:BW], x_t[:, :, blk(b)], ACT.Square).then_inc(sq_ready.sem, 1)

            def ssd_rstd(g):
                wait(sum_ready, g, NC)
                for b, bank in enumerate((S[3], S[4], S[0])):
                    wait(ms_ready, g, b + 1)
                    ch.add(act.activation(rstd[:, blk(b)], bank[:, 0:BW], ACT.Ln, scale=1.0 / GW,
                                          bias=cst[:, K_EPS4:K_EPS4 + 1]))
                ch.wait(act)
                act.activation(rstd, rstd, ACT.Exp, scale=-0.5).then_inc(rstd_ok, 1)

            def hgrn(g, k):
                if k == 2:
                    act.wait_ge(y_final, g + 1)
                    hh = slice(g, g + 1) if isinstance(g, int) else bass.ds(g, 1)
                    for d, dst in enumerate((hs_f[:, 0, :], hs_b[:, NC - 2, :])):
                        act.dma_start(dst, m["state_hgrn"][0, 0, d, hh].rearrange("a k v -> k (a v)")
                                      ).then_inc(hs_loaded, 16)
                    act.activation(hdec[:, 0, :], f_t[:, P - 1:T:P], ACT.Exp)
                    act.activation(hdec[:, 1, :], g_t[:, 0:T:P], ACT.Exp).then_inc(hdec_ok, 1)
                for i, n in enumerate(KSTEPS):
                    if k == slot_of(n) + 2:
                        wait(kt_ready, g, i + 1)
                        if i == 4:
                            wait(kc_ready, g, 1)
                        elif i == 5:
                            wait(kc_ready, g, 5)
                        bank = (S[5], S[0], S[1], S[2], S[5], S[5])[i]
                        act.activation(ktok[i if i < 4 else 0][:, :], bank[:, 0:BW],
                                       ACT.Copy).then_inc(kt_kept.sem, 1)
                for n in QSTEPS:
                    b = STEPS[n][1]
                    if k == slot_of(n) + 2:
                        wait(o_ready, g, b + 1)
                        ch.add(act.activation(q_t[:, blk(b)], S[3][:, 0:BW], ACT.Copy))
                        act.activation(ktok[2][:, :], S[3][:, 0:BW], ACT.Square).then_inc(o_kept.sem, 1)
                    if k == slot_of(n) + 3:
                        wait(hms_ready, g, b + 1)
                        act.activation(g_t[:, blk(b)], S[3][:, 0:BW], ACT.Copy).then_inc(hms_kept.sem, 1)
                for n in steps_in(k):
                    kind, b, lv = STEPS[n]
                    if kind == "dg":
                        continue
                    q = qk[n % 4]
                    if kind == "q":
                        used_by_pe(act, g, n - 4)
                        act.wait_ge(f_ready, g * 2 + 2)
                        act.activation(q[:, 0, :], f_t[:, blk(b)], ACT.Exp)
                        last = act.activation(q[:, 1, :], g_t[:, blk(b)], ACT.Exp)
                    else:
                        wait(arg_made, g, ASTEPS.index(n) + 1)
                        v = q[:, 0, :] if kind in ("kb", "kf") else q[:, :, :]
                        last = act.activation(v, v, ACT.Exp)
                    last.then_inc(exp_made.sem, 1)

            def hgrn_rstd(g):
                wait(hms_kept, g, NB)
                ch.add(act.activation(g_t[:, :], g_t[:, :], ACT.Ln, scale=1.0 / P,
                                      bias=cst[:, K_EPS4:K_EPS4 + 1]))
                ch.wait(act)
                act.activation(g_t[:, :], g_t[:, :], ACT.Exp, scale=-0.5).then_inc(hrstd_ok, 1)
                act.wait_ge(o_final, g + 2)
                dst = y_dram[16 + g:17 + g] if isinstance(g, int) else y_dram[bass.ds(g + 16, 1)]
                act.dma_start(dst.rearrange("a p n -> p (a n)"), q_t[:, :]).then_inc(o_stored, 16)

            def stage_a(g):
                for k in range(SLOTS):
                    if k == 6:
                        ch.wait(act)
                        for e in (f_t, g_t):
                            act.activation(e[:, :], e[:, :], ACT.Ln,
                                           bias=cst[:, K_1:K_1 + 1]).then_inc(f_log, 1)
                    if k in (8, 10):
                        e = kf_t if k == 8 else kb_t
                        act.wait_ge(f_lnk, g * 2 + (k // 2 - 3))
                        act.activation(e[:, :], e[:, :], ACT.Exp).then_inc(k_ready, 1)
                    ssd(g, k)
                    if k == SLOTS - 1:
                        keep_v(g, 0)
                    a_evac(g, k)
                    if k % NB == 0:
                        high(g, k // NB + 1)

            def stage_b_start(g, k):
                if k == 0:
                    keep_v(g, 1)
                    ssd_rstd(g)
                if k == 1:
                    keep_v(g, 2)

            act.sem_inc(hms_kept.sem, 1)
            act.sem_inc(o_stored, 16)
            act.sem_inc(so_stored, 32)
            act.sem_inc(soh_stored, 32)
            act.wait_ge(cols_in, 48)
            for b in range(NB):
                if b == 0:
                    i = 0
                    act.wait_ge(w_landed[0], 16)
                    act.activation(w_hi[0][:, :, 0:64], raw[0][:, :, 0:64], ACT.Copy).then_inc(w_high.sem, 1)
                    high(None, 1)
                ui, used, n = numbered(b, None)
                act.wait_ge(unit_done.sem, n + 1)
                act.activation(dt_v[0:64, blk(b)], banks[ui][0:64, 0:BW], ACT.Identity,
                               bias=cols[:, 0:1]).then_inc(bank_free[ui], 1)
            act.wait_ge(bank_free[0], 2)
            act.wait_ge(bank_free[1], 1)
            dt = Chain(dt_act)

            def dt_step(out, in_, f, **kw):
                dt.add(act.activation(out, in_, f, **kw))
                dt.wait(act)

            dt_step(cols[:, 2:3], cols[:, 1:2], ACT.Exp)
            dt_step(dt_a[0:64, :], dt_v[0:64, :], ACT.Abs)
            dt_step(dt_a[0:64, :], dt_a[0:64, :], ACT.Exp, scale=-1.0)
            dt_step(dt_a[0:64, :], dt_a[0:64, :], ACT.Ln, bias=cst[0:64, K_1:K_1 + 1])
            act.wait_ge(dt_dve, 2)
            dt_step(dt_d[0:64, :], dt_d[0:64, :], ACT.Ln)
            act.wait_ge(dt_dve, 14)
            dt_step(dt_e[0:64, :], dt_e[0:64, :], ACT.Exp)
            dt_step(dt_b[0:64, :], cum[:, :], ACT.Exp)
            assert dt.n == DT_ACT, dt.n
            for k in range(SLOTS):
                if k > 0 and (k - 1) // NB in CONV_TILES:
                    b_th_free(None, k - 1)
                    conv_tanh(None, k - 1)
                b_evac(None, k)
                if k % NB == 0:
                    high(None, k // NB + 2) if k < SLOTS - NB else high(0, 0)
            b_th_free(None, SLOTS - 1)
            conv_tanh(None, SLOTS - 1)
            act.wait_ge(dt_turned, 1)
            flat = tok[:, :, :, :].rearrange("p a c r -> p (a c r)")
            for i in range(4):
                n = min(512, 3 * NC * 64 - i * 512)
                act.activation(flat[:, i * 512:i * 512 + n], S[i][:, 0:n], ACT.Copy)
            flat = dec[:, :, :].rearrange("p c r -> p (c r)")
            for i in range(2):
                last = act.activation(flat[:, i * 288:(i + 1) * 288], S[4 + i][:, 0:288], ACT.Copy)
            last.then_inc(dt_kept, 1)

            def stage_b(g):
                for k in range(SLOTS):
                    stage_b_start(g, k)
                    if k > 0 and (k - 1) // NB in CONV_TILES:
                        b_th_free(g, k - 1)
                        conv_tanh(g, k - 1)
                    hgrn(g, k)
                    b_evac(g, k)
                    if k % NB == 0:
                        high(g, 6 + k // NB + 1)
                b_th_free(g, SLOTS - 1)
                conv_tanh(g, SLOTS - 1)
                hgrn(g, SLOTS)
                hgrn_rstd(g)

            with act.Fori(0, G - 1) as g:
                ch.round(g)
                stage_a(g)
                stage_b(g)
                assert ch.n == ACT_ROUND, ch.n
            g = G - 1
            ch.round(g)
            stage_a(g)
            for k in range(8 * NB):
                stage_b_start(g, k)
                if k <= SLOTS:
                    hgrn(g, k)
                if k == SLOTS:
                    hgrn_rstd(g)
                t, b = divmod(k, NB)
                ui, used, n = a_unit(g, SLOTS + k)
                act.wait_ge(unit_done.sem, n + 1)
                if k < 2:
                    act.wait_ge(v_turned, g * NB + (k + 2))
                else:
                    act.wait_ge(gate_stored[ui], 16 * (G * (1 + ui) + k // 2))
                act.activation(th[ui][:, :], banks[ui][:, 0:BW], ACT.Tanh, scale=0.5).then_inc(bank_free[ui], 1)
                act.wait_ge(bank_free[ui], used + 1)
                act.dma_start(gate_dram[8 + t, :, blk(b)], th[ui][:, :]).then_inc(gate_stored[ui], 16)
                if b == 0 and t < 7:
                    high(g, 6 + t + 1)

        @block.vector
        def _(dve):
            ch = dve_s

            def wait(count, g, n):
                dve.wait_ge(count.sem, count.at(g, n))

            def per_head(v):
                return v.rearrange("p (h a) -> p h a", a=1).broadcast_to([P, v.shape[1], HD])

            def heads(v):
                return v.rearrange("p (h c) -> p h c", c=HD)

            def low(g, t, width=P):
                i, _, n = tile(g, t)
                dve.wait_ge(w_high.sem, n + 1)
                dve.tensor_tensor(w_lo[i][:, :, 0:width], raw[i][:, :, 0:width],
                                  w_hi[i][:, :, 0:width].bitcast(F32), ALU.subtract).then_inc(w_split.sem, 1)

            def b_dest(k):
                t, b = divmod(k, NB)
                return (b_t[:, blk(b)], c_t[:, blk(b)], z_t[:, 0, blk(b)], z_t[:, 1, blk(b)],
                        x_t[:, 0, blk(b)], x_t[:, 1, blk(b)])[t]

            def conv_silu(g, k):
                ui = b_unit(g, k)[0]
                wait(th_ok, g, k + (0 if g is None else 2 * NB) + 1)
                if k == 12 and g is not None:
                    dve.wait_ge(y_stored, g * 16 + 16)
                dve.scalar_tensor_tensor(b_dest(k), th[ui][:, :], 1.0, acc[ui][:, :], ALU.add,
                                         ALU.mult).then_inc(silu_done.sem, 1)

            def b_evac(g, k):
                t, b = divmod(k, NB)
                ui, used, _ = b_unit(g, k)
                if t in CONV_TILES:
                    ti = CONV_TILES.index(t)
                    if k == 0:
                        dve.wait_ge(taps_ok, 1 if g is None else g + 2)
                    dve.wait_ge(bank_free[ui], used + 1)
                    out = acc[ui][:, :].rearrange("p (r c) -> p r c", c=GRID)
                    for j in range(TAPS):
                        src = pad[b][:, :, j:j + GRID]
                        if j == 0:
                            ins = dve.tensor_scalar(out, src, taps[:, ti, 0:1], taps[:, ti, TAPS:TAPS + 1],
                                                    ALU.mult, ALU.add)
                        else:
                            ch.wait(dve)
                            ins = dve.scalar_tensor_tensor(out, src, taps[:, ti, j:j + 1], out, ALU.mult, ALU.add)
                        if j < TAPS - 1:
                            ch.add(ins)
                    ins.then_inc(conved.sem, 1)
                else:
                    wait(th_ok, g, k + (0 if g is None else 2 * NB) + 1)
                    dve.scalar_tensor_tensor(b_dest(k), th[ui][:, :], 1.0, banks[ui][:, 0:BW], ALU.add,
                                             ALU.mult).then_inc(bank_free[ui], 1)

            def ssd(g, k):
                if 3 <= k < 3 + NA1P:
                    p = k - 3
                    wait(ctb_ready, g, p + 1)
                    if p == 0:
                        wait(tr_kept, g, 1)
                        dve.wait_ge(grp_ready, g + 1)
                    for j in range(2 if p < 3 else 1):
                        c = 8 - 2 * p - j
                        ch.wait(dve)
                        if j == 0 and p > 0:
                            wait(ctb_used, g, p)
                        ch.add(dve.tensor_tensor(heads(s_b[:, c - 2, :]), heads(s_b[:, c - 1, :]),
                                                 per_head(dec_g[:, c, HPG:8]), ALU.mult))
                        ch.wait(dve)
                        ins = dve.tensor_tensor(s_b[:, c - 2, :], s_b[:, c - 2, :], S[2][:, j * GW:(j + 1) * GW],
                                                ALU.add)
                        if j == 0 and p < 3:
                            ch.add(ins)
                    ins.then_inc(ctb_used.sem, 1)
                if 7 <= k < 7 + NC:
                    c = k - 7
                    wait(y_ready, g, c + 1)
                    if c == 0:
                        dve.tensor_copy(y_tok[:, :], S[2][:, 0:GW])
                        dve.tensor_copy(st_in[:, 0:2, :].rearrange("p t n -> p (t n)"), S[2][:, GW:2 * GW])
                        ins = dve.tensor_copy(st_in[:, 2:4, :].rearrange("p t n -> p (t n)"), S[5][:, 0:GW])
                    else:
                        wait(yt_ready, g, c)
                        if c < NC - 1:
                            ch.add(dve.tensor_tensor(heads(s_f[:, :]), heads(s_f[:, :]),
                                                     per_head(dec_g[:, c, 0:HPG]), ALU.mult))
                        ch.add(dve.tensor_tensor(heads(t_off[:, :]), heads(S[5][:, :]),
                                                 per_head(tok_g[:, 2, c, :]), ALU.mult))
                        ch.wait(dve)
                        ch.add(dve.tensor_tensor(y_tok[:, :], t_off[:, 0:GW], S[2][:, 0:GW], ALU.add))
                        if c < NC - 1:
                            ch.add(dve.tensor_tensor(s_f[:, :], s_f[:, :], S[2][:, GW:2 * GW], ALU.add))
                        ch.wait(dve)
                        ins = dve.tensor_tensor(y_tok[:, :], y_tok[:, :], t_off[:, GW:2 * GW], ALU.add)
                    ins.then_inc(y_made.sem, 1)
                if 8 <= k < 8 + NC:
                    c = k - 8
                    wait(yt_ready, g, c + 1)
                    for e in range(2):
                        ch.add(dve.scalar_tensor_tensor(x_t[:, e, chunk(c)], x_t[:, e, chunk(c)],
                                                        vec_g[:, e:e + 1], S[1][:, e * P:(e + 1) * P],
                                                        ALU.mult, ALU.add))
                    ch.wait(dve)
                    dve.tensor_tensor(x_t[:, :, chunk(c)], x_t[:, :, chunk(c)], z_t[:, :, chunk(c)],
                                      ALU.mult).then_inc(yt_made.sem, 1)
                if 5 <= k < 5 + NC:
                    c = k - 5
                    wait(sum_ready, g, c + 1)
                    wait(tr_kept, g, 9 + c)
                    v = mm[:, c % 2, :].rearrange("p (h i) -> p h i", i=P)
                    cb = xb[c % 2][:, GW + P:GW + 2 * P].rearrange("p (a i) -> p a i", a=1).broadcast_to([P, HPG, P])
                    dve.tensor_tensor(v, v, cb, ALU.mult).then_inc(m_ready.sem, 1)

            def ssd_norm(g):
                dve.wait_ge(rstd_ok, g + 1)
                wait(yt_made, g, NC)
                for e in range(2):
                    ins = dve.scalar_tensor_tensor(x_t[:, e, :], x_t[:, e, :], vec_g[:, 2 + e:3 + e], rstd,
                                                   ALU.mult, ALU.mult)
                    if e == 0:
                        ch.add(ins)
                ins.then_inc(y_final, 1)

            def a_evac(g, k):
                t, b = divmod(k, NB)
                if t in (2, 3):
                    ui, used, _ = a_unit(g, k)
                    wait(th_ok, g, k - 6 + 1)
                    if k == 6:
                        dve.wait_ge(o_stored, g * 16 + 16)
                    dst = (q_t, s_t)[t - 2]
                    dve.scalar_tensor_tensor(dst[:, blk(b)], th[ui][:, :], 1.0, banks[ui][:, 0:BW], ALU.add,
                                             ALU.mult).then_inc(bank_free[ui], 1)

            def decay(g, k):
                for d, (e, u) in enumerate(((f_t, kf_t), (g_t, kb_t))):
                    if k == 7 + 2 * d:
                        dve.wait_ge(f_log, g * 2 + (d + 1))
                        ch.add(dve.scalar_tensor_tensor(e[:, :], u[:, :], 0.0, e[:, :], ALU.min, ALU.subtract))
                        ch.wait(dve)
                        dve.tensor_tensor(u[:, :], e[:, :], u[:, :], ALU.subtract).then_inc(f_lnk, 1)
                    if k == 8 + 2 * d:
                        dve.wait_ge(f_lnk, g * 2 + (d + 1))
                        for b in range(NB):
                            v = e[:, blk(b)] if d == 0 else back(e, b)
                            ins = dve.tensor_tensor_scan(v, reset, v, 0.0, ALU.mult, ALU.add)
                            if b < NB - 1:
                                ch.add(ins)
                        ins.then_inc(f_ready, 1)

            def back(e, b, r0=0, r1=P):
                return e[r0:r1, (b + 1) * BW - 1:b * BW - 1:-1] if b else e[r0:r1, BW - 1::-1]

            def hgrn(g, k):
                for i, n in enumerate(KSTEPS):
                    if k == (3 if i < 2 else 4 if i < 4 else slot_of(n) + 3):
                        kind, b, _ = STEPS[n]
                        bank = S[4] if i % 2 == 0 or i > 3 else S[3]
                        wait(kc_ready, g, i + 1)
                        if i == 0:
                            dve.wait_ge(hs_loaded, g * 32 + 32)
                            dve.wait_ge(hdec_ok, g + 1)
                        cs = range(b * CB, (b + 1) * CB)
                        todo = []
                        for c in (reversed(cs) if kind == "kb" else cs):
                            if c == 0 or (kind == "kb" and c >= 2) or (kind == "kf" and c < NC - 1):
                                todo.append(c)
                        for c in todo:
                            part = bank[:, (c - b * CB) * P:(c - b * CB + 1) * P]
                            if c == 0:
                                if kind == "kb":
                                    dve.wait_ge(soh_stored, g * 32 + 32)
                                ins = dve.tensor_copy(so_h[:, 0 if kind == "kf" else 1, :], part)
                            else:
                                ch.wait(dve)
                                if i > 0:
                                    wait(kc_used, g, i)
                                d, s = (0, hs_f) if kind == "kf" else (1, hs_b)
                                frm, to = (c - 1, c) if kind == "kf" else (c - 1, c - 2)
                                ins = dve.scalar_tensor_tensor(s[:, to, :], s[:, frm, :], hdec[:, d, c:c + 1],
                                                               part, ALU.mult, ALU.add)
                            if c != todo[-1]:
                                ch.add(ins)
                        ins.then_inc(kc_used.sem, 1)
                for i, n in enumerate(MSTEPS):
                    if k == slot_of(n) + 2:
                        kind, b, lv = STEPS[n]
                        wait(lv_ready, g, i + 1)
                        if lv > 0:
                            wait(lv_used, g, i)
                            dve.sem_inc(merge_clear, 1)
                        out = at[b % 2][:, :].rearrange("p (c i) -> p c i", i=P)
                        src = S[i % 3][:, 0:BW].rearrange("p (c i) -> p c i", i=P)
                        if lv == 0:
                            if b == 2:
                                wait(o_ready, g, 1)
                            mask = cst[:, K_M64:K_M64 + P].rearrange("p (a i) -> p a i", a=1)
                            ins = dve.tensor_tensor(out, src, mask.broadcast_to([P, CB, P]), ALU.mult)
                        else:
                            mask = masks[:, lv - 1, :].rearrange("p (a i) -> p a i", a=1)
                            ins = dve.copy_predicated(out, mask.broadcast_to([P, CB, P]), src)
                        ins.then_inc(lv_used.sem, 1)
                for n in steps_in(k):
                    kind, b, lv = STEPS[n]
                    q = qk[n % 4]
                    if kind != "dg":
                        wait(exp_made, g, ESTEPS.index(n) + 1)
                    if n == 0:
                        dve.wait_ge(k_ready, g * 2 + 2)
                    if kind in ("kb", "kf"):
                        src = kb_t if kind == "kb" else kf_t
                        ins = dve.tensor_tensor(q[:, 0, :], q[:, 0, :], src[:, blk(b)], ALU.mult)
                    elif kind == "lv":
                        s = 64 >> lv
                        dve.tensor_tensor(q[:, 0, :], q[:, 0, :], q_t[:, blk(b)], ALU.mult)
                        kv = halves(q[:, 1, :], s)
                        for half, src in ((0, kf_t), (1, kb_t)):
                            ins = dve.tensor_tensor(kv[half], kv[half], halves(src[:, blk(b)], s)[half], ALU.mult)
                    elif kind == "dg":
                        used_by_pe(dve, g, n - 4)
                        ins = dve.tensor_tensor(q[:, 1, :], kf_t[:, blk(b)], kb_t[:, blk(b)], ALU.add)
                    else:
                        qb = q_t[:, blk(b)].rearrange("p (a n) -> p a n", a=1).broadcast_to([P, 2, BW])
                        ins = dve.tensor_tensor(q[:, :, :], q[:, :, :], qb, ALU.mult)
                    ins.then_inc(qk_ready.sem, 1)

            def hgrn_norm(g):
                dve.wait_ge(hrstd_ok, g + 1)
                ch.add(dve.scalar_tensor_tensor(q_t[:, :], q_t[:, :], vec_g[:, 4:5], g_t[:, :], ALU.mult, ALU.mult))
                ch.wait(dve)
                dve.tensor_tensor(q_t[:, :], q_t[:, :], s_t[:, :], ALU.mult).then_inc(o_final, 1)

            def stage_a(g):
                for k in range(SLOTS):
                    ssd(g, k)
                    decay(g, k)
                    a_evac(g, k)
                    if k % NB == 1:
                        low(g, k // NB + 1)

            dve.wait_ge(cols_in, 48)
            for src, dst in ((ident, id_bf), (acc[0][:, 0:P], neg_bf[0]), (acc[0][:, P:2 * P], neg_bf[1])):
                dve.tensor_copy(dst[:, :], src).then_inc(bf_ok, 1)
            dve.sem_inc(o_final, 1)
            low(None, 0, 64)
            low(None, 1)
            dt = Chain(dt_dve)
            r = slice(0, 64)
            dve.wait_ge(dt_act, 4)
            dt.add(dve.scalar_tensor_tensor(dt_c[r, :], dt_v[r, :], 0.0, dt_a[r, :], ALU.max, ALU.add))
            dt.wait(dve)
            dt.add(dve.tensor_scalar(dt_d[r, :], dt_c[r, :], 2.0 ** -60, None, ALU.max))
            dt.add(dve.tensor_scalar(cols[:, 3:4], cols[:, 2:3], -1.0, None, ALU.mult))
            dt.wait(dve)
            dt.add(dve.tensor_scalar(dt_b[r, :], dt_c[r, :], cols[:, 3:4], None, ALU.mult))
            dt.wait(dve)
            for b in range(NB):
                dt.add(dve.tensor_tensor_scan(cum[0:32, blk(b)], reset[0:32, :], dt_b[0:32, blk(b)], 0.0,
                                              ALU.mult, ALU.add))
                dt.add(dve.tensor_tensor_scan(back(cum, b, 32, 64), reset[32:64, :], back(dt_b, b, 32, 64), 0.0,
                                              ALU.mult, ALU.add))
            dve.wait_ge(dt_act, 5)
            dt.wait(dve)
            dt.add(dve.tensor_tensor(dt_d[r, :], dt_d[r, :], dt_v[r, :], ALU.min))
            dt.wait(dve)
            dt.add(dve.tensor_tensor(dt_d[r, :], dt_d[r, :], cum[:, :], ALU.subtract))
            for lo, hi, at_col in ((0, 32, P - 1), (32, 64, 0)):
                cv = cum[lo:hi, :].rearrange("p (c t) -> p c t", t=P)
                ev = dt_e[lo:hi, :].rearrange("p (c t) -> p c t", t=P)
                dt.add(dve.tensor_tensor(ev, cv[:, :, at_col:at_col + 1].broadcast_to([32, NC, P]), cv,
                                         ALU.subtract))
            assert dt.n == 14, dt.n
            dve.wait_ge(dt_act, 7)
            dt.add(dve.tensor_tensor(dt_e[r, :], dt_e[r, :], dt_c[r, :], ALU.mult))
            for lo, hi, at_col in ((0, 32, P - 1), (32, 64, 0)):
                ev = dt_b[lo:hi, :].rearrange("p (c t) -> p c t", t=P)[:, :, at_col:at_col + 1]
                iv = cst[lo:hi, K_ID:K_ID + 64].rearrange("p (a r) -> p a r", a=1)
                ov = v_tok[lo:hi, :, :].rearrange("p c t -> p (c t)")[:, 0:NC * 64].rearrange(
                    "p (c r) -> p c r", r=64)
                dt.add(dve.tensor_tensor(ov, iv.broadcast_to([32, NC, 64]), ev.broadcast_to([32, NC, 64]),
                                         ALU.mult))
            assert dt.n == DT_DVE, dt.n
            pro = Chain(sem("dve_prologue"))
            ch = pro
            for k in range(SLOTS):
                if k > 0 and (k - 1) // NB in CONV_TILES:
                    conv_silu(None, k - 1)
                b_evac(None, k)
                if k % NB == 1:
                    low(None, k // NB + 2) if k < SLOTS - NB else low(0, 0)
            conv_silu(None, SLOTS - 1)
            ch = dve_s

            with dve.Fori(0, G - 1) as g:
                ch.round(g)
                stage_a(g)
                for k in range(SLOTS):
                    if k == 0:
                        ssd_norm(g)
                    if k > 0 and (k - 1) // NB in CONV_TILES:
                        conv_silu(g, k - 1)
                    hgrn(g, k)
                    b_evac(g, k)
                    if k % NB == 1:
                        low(g, 6 + k // NB + 1)
                conv_silu(g, SLOTS - 1)
                hgrn(g, SLOTS)
                hgrn_norm(g)
                assert ch.n == DVE_ROUND, ch.n
            g = G - 1
            ch.round(g)
            stage_a(g)
            for k in range(8 * NB):
                if k == 0:
                    ssd_norm(g)
                if k <= SLOTS:
                    hgrn(g, k)
                if k == SLOTS:
                    hgrn_norm(g)
                if k % NB == 1 and k // NB < 7:
                    low(g, 6 + k // NB + 1)

        @block.gpsimd
        def _(pool):
            def wait(count, g, n):
                pool.wait_ge(count.sem, count.at(g, n))

            def some(v, i, n):
                cut = slice(i, i + n) if isinstance(i, int) else bass.ds(i, n)
                return v[(slice(None),) * (len(v.shape) - 1) + (cut,)]

            def gather_taps(g):
                t4 = vec[:, 0:V_CONVB + 32].rearrange("p (k t) -> p k t", t=32)
                for i, (at_col, n) in enumerate(((g + 16, 1), (g + 24, 1), (g * 2, 2))):
                    last = pool.tensor_copy(taps[:, i:i + n, :].rearrange("p t k -> p k t"), some(t4, at_col, n))
                last.then_inc(taps_ok, 1)

            def gather_group(g):
                pool.wait_ge(o_final, g + 1)
                for a in range(3):
                    src = tok[:, a, :, :].rearrange("p c (d h) -> p c d h", d=2)
                    dst = tok_g[:, a, :, :].rearrange("p c (d h) -> p c d h", d=2)
                    for d in range(2):
                        pool.tensor_copy(dst[:, :, d, :], some(src[:, :, d, :], g * 4, 4))
                src = dec[:, :, :].rearrange("p c (d h) -> p c d h", d=2)
                dst = dec_g[:, :, :].rearrange("p c (d h) -> p c d h", d=2)
                for d in range(2):
                    pool.tensor_copy(dst[:, :, d, :], some(src[:, :, d, :], g * 4, 4))
                pool.tensor_copy(vec_g[:, 0:2], some(vec[:, V_D:V_D + 16], g * 2, 2))
                pool.tensor_copy(vec_g[:, 2:4], some(vec[:, V_SSDN:V_SSDN + 16], g * 2, 2))
                pool.tensor_copy(vec_g[:, 4:5], some(vec[:, V_HGRN:V_HGRN + 8], g, 1)).then_inc(grp_ready, 1)
                for d in range(2):
                    iv = some(cst[0:64, K_ID + 32 * d:K_ID + 32 * d + 32], g * 4, 4).rearrange(
                        "p (h a) -> p h a", a=1)
                    last = pool.tensor_copy(sel[:, 4 * d:4 * d + 4, :], iv.broadcast_to([64, HPG, P]))
                last.then_inc(sel_ready, 1)

            def scaled(out, x, w):
                return pool.tensor_tensor(out.rearrange("p (h c) -> p h c", c=HD),
                                          x.rearrange("p (h c) -> p h c", c=HD),
                                          w.rearrange("p (h a) -> p h a", a=1).broadcast_to([P, HPG, HD]), ALU.mult)

            def ssd(g, k):
                if k == 0:
                    gather_group(g)
                if 1 <= k < 1 + NA1P:
                    p = k - 1
                    if p == 0:
                        pool.wait_ge(grp_ready, g + 1)
                    else:
                        wait(ctb_ready, g, p)
                    wait(tr_kept, g, 3 + 2 * p if p < 3 else 8)
                    for j in range(2 if p < 3 else 1):
                        ins = scaled(xp[:, j, :], xb[2 * (p % 2) + j][:, 0:GW], tok_g[:, 1, 8 - 2 * p - j, 4:8])
                    ins.then_inc(xp_ready.sem, 1)
                if 5 <= k < 5 + NC:
                    c = k - 5
                    wait(tr_kept, g, 9 + c)
                    if c == 0:
                        wait(ctb_ready, g, NA1P)
                        scaled(xp[:, 1, :], xb[0][:, 0:GW], tok_g[:, 1, 0, 4:8])
                    else:
                        wait(y_ready, g, max(c - 1, 1))
                    scaled(xp[:, c % 2, :], xb[c % 2][:, 0:GW], tok_g[:, 1, c, 0:4]).then_inc(xp_ready.sem, 1)
                    wait(exp_ready, g, c + 1)
                    pool.tensor_tensor(mm[:, c % 2, :], ex[:, 0:512], ex[:, 512:1024],
                                       ALU.add).then_inc(sum_ready.sem, 1)

            def hgrn(g, k):
                if k == 0:
                    wait(yt_ready, g, NC)
                    pool.wait_ge(f_ready, g * 2 + 2)
                for n in steps_in(k):
                    if n not in ASTEPS:
                        continue
                    kind, b, lv = STEPS[n]
                    q = qk[n % 4]
                    if n >= 4:
                        used_by_pe(pool, g, n - 4)
                    if kind in ("kb", "kf"):
                        src, at_col = (g_t, 0) if kind == "kb" else (f_t, P - 1)
                        v = src[:, blk(b)].rearrange("p (c t) -> p c t", t=P)
                        ins = pool.tensor_tensor(q[:, 0, :].rearrange("p (c t) -> p c t", t=P),
                                                 v[:, :, at_col:at_col + 1].broadcast_to([P, CB, P]), v,
                                                 ALU.subtract)
                    else:
                        s = 64 >> lv
                        nb = BW // (2 * s)
                        (q_lo, q_up), (k_lo, k_up) = halves(q[:, 0, :], s), halves(q[:, 1, :], s)
                        (f_lo, f_up), (g_lo, g_up) = halves(f_t[:, blk(b)], s), halves(g_t[:, blk(b)], s)
                        rf = f_lo[:, :, s - 1:s].broadcast_to([P, nb, s])
                        rg = g_up[:, :, 0:1].broadcast_to([P, nb, s])
                        pool.tensor_tensor(q_up, f_up, rf, ALU.subtract)
                        pool.tensor_tensor(k_lo, rf, f_lo, ALU.subtract)
                        pool.tensor_tensor(q_lo, g_lo, rg, ALU.subtract)
                        ins = pool.tensor_tensor(k_up, rg, g_up, ALU.subtract)
                    ins.then_inc(arg_made.sem, 1)

            for b in range(NB):
                pool.memset(pad[b][:, :, :], 0.0).then_inc(pads_zero, 1)
            gather_taps(0)
            pool.wait_ge(dt_kept, 1)
            with pool.Fori(0, G - 1) as g:
                for k in range(SLOTS):
                    ssd(g, k)
                for k in range(SLOTS):
                    if k == 0:
                        wait(conved, g, 0)
                        gather_taps(g + 1)
                    hgrn(g, k)
            g = G - 1
            for k in range(SLOTS):
                ssd(g, k)
            for k in range(SLOTS):
                hgrn(g, k)


HID = FFN // P
HCH = [8, 8, 6]
PHASES = [("s1", 4), ("s2", 4), ("h", 4), ("o", 4)]
for _c, _n in enumerate(HCH):
    PHASES += [(f"up{_c}", _n), (f"down{_c}", 4)]
FIRST = {}
_i = 0
for _name, _n in PHASES:
    FIRST[_name] = _i
    _i += _n
PARTS = {"s1": 0, "s2": 24, "h": 48, "o": 72, "up": 96, "down0": 120, "down1": 144, "down2": 168}
UNITS = 2 * NB


def merge_and_ffn(nc, scope, sb, sem, m):
    cst, mod, raw, banks, x_acc = m["cst"], m["mod"], m["raw"], m["banks"], m["x_acc"]
    ones, w_src = m["ones"], m["w_src"]
    y_dram, gate_dram, x_dram = m["y_dram"], m["gate_dram"], m["x_dram"]
    a_hi, a_lo = (sb(n, [P, KT, T], F32R, scope) for n in ("a_hi", "a_lo"))
    b_hi, b_lo = (sb(n, [P, KT, T], F32R, scope) for n in ("b_hi", "b_lo"))
    w_hi = [sb(f"v_hi{i}", [P, KT, P], F32R, scope) for i in range(2)]
    w_lo = [sb(f"v_lo{i}", [P, KT, P], F32R, scope) for i in range(2)]
    small = [sb(f"small{i}", [P, BW], F32, scope) for i in range(9)]
    stage, gate, tmp = small[0:3], small[3:6], small[6:9]
    A, B = (a_hi, a_lo), (b_hi, b_lo)
    USES = {"s1": A, "s2": B, "h": A, "o": B}

    w_in = [sem(f"m_w_in{i}") for i in range(2)]
    w_high, w_split = sem("m_w_high"), sem("m_w_split")
    unit_done, freed, acc_done = sem("m_unit_done"), sem("m_freed"), sem("m_acc_done")
    small_in = [sem(f"m_small_in{i}") for i in range(6)]
    hi_done, parts = sem("m_hi_done"), sem("m_parts")
    sq_done, sq_added, sums_zero = sem("m_sq_done"), sem("m_sq_added"), sem("m_sums_zero")
    ms_done, ln_done, rstd_done, t_done = sem("m_ms_done"), sem("m_ln_done"), sem("m_rstd_done"), sem("m_t_done")
    th_done = sem("m_th_done")

    def loop(eng, body):
        for name, n in PHASES:
            if name == PHASES[-1][0]:
                with eng.Fori(0, n - 1) as i:
                    body(name, i, False)
                body(name, n - 1, True)
            else:
                with eng.Fori(0, n) as i:
                    body(name, i, False)

    def it(name, i):
        return i + FIRST[name]

    def done(name, i, s, b):
        return it(name, i) * UNITS + (UNITS + s * NB + b + 1)

    def free_at(name, i, s, b):
        return it(name, i) * UNITS + (UNITS + (2 * b + s + 1 if name[0:2] == "up" else s * NB + b + 1))

    def acc_at(name, i, s, b):
        return i * UNITS + ((FIRST[name] - FIRST["s2"]) * UNITS + s * NB + b + 2)

    def part_at(name, k, b):
        return k * NB + (PARTS[name] + b + 1)

    def tile_of(v, k):
        return v[:, k, :] if isinstance(k, int) else v[:, bass.ds(k, 1), :].rearrange("p a n -> p (a n)")

    def tile_blk(v, k, b):
        if isinstance(k, int):
            return v[:, k, blk(b)]
        return v[:, bass.ds(k, 1), blk(b)].rearrange("p a n -> p (a n)")

    def dram_blk(v, k, b):
        if isinstance(k, int):
            return v[k, :, blk(b)]
        return v[bass.ds(k, 1), :, blk(b)].rearrange("a p n -> p (a n)")

    def mod_col(j, t, who):
        if isinstance(t, int):
            return mod[:, j + t, who:who + 1]
        return mod[:, bass.ds(t + j, 1), who:who + 1].rearrange("p a b -> p (a b)")

    with nc.Block() as block:
        @block.sync
        def _(sp):
            def load(name, i, s):
                I = it(name, i)
                sp.wait_ge(w_split, I * 2 + (s + 1))
                kt = KT
                if name == "s1":
                    src = w_src(m["w_ssd_out"][0, 0:D, :], i * 256 + s * P)
                elif name == "s2":
                    src = w_src(m["w_ssd_out"][0, D:2 * D, :], i * 256 + s * P)
                elif name == "h":
                    src = w_src(m["w_hgrn_out"][0], i * 256 + s * P)
                elif name == "o":
                    src = w_src(m["w_out"][0], i * 256 + s * P)
                elif name[0:2] == "up":
                    c0 = int(name[2]) * KT * P
                    src = w_src((m["ffn_w1"], m["ffn_w3"])[s][0], i * P + c0)
                else:
                    c = int(name[4])
                    kt = HCH[c]
                    src = w_src(m["ffn_w2"][0, c * D:c * D + kt * P, :], i * 256 + s * P)
                sp.dma_start(raw[s][:, 0:kt, :], src).then_inc(w_in[s], 16)

            for u in range(24):
                b, k = divmod(u, KT)
                if u >= 6:
                    sp.wait_ge(parts, u - 5)
                sp.dma_start(small[u % 6][:, :], y_dram[k, :, blk(b)]).then_inc(small_in[u % 6], 16)
                if u == 5:
                    sp.dma_start(raw[0][:, :, :], w_src(m["w_ssd_out"][0, 0:D, :], 0)).then_inc(w_in[0], 16)
            first = True
            for name, n in PHASES:
                if first:
                    load(name, 0, 1)
                    first = False
                    with sp.Fori(1, n) as i:
                        load(name, i, 0)
                        load(name, i, 1)
                else:
                    with sp.Fori(0, n) as i:
                        load(name, i, 0)
                        load(name, i, 1)

        @block.tensor
        def _(pe):
            def body(name, i, last_it):
                I = it(name, i)
                operand = USES.get(name) or (A if name[0:2] == "up" else B)
                kt = HCH[int(name[4])] if name[0:4] == "down" else KT
                for s in range(2):
                    pe.wait_ge(w_split, I * 2 + (s + 3))
                    for b in range(NB):
                        pe.wait_ge(freed, I * UNITS + (2 * b + 1 if s == 0 else b + 4))
                        if s == 0 and name in ("s2", "h", "o") or name[0:4] == "down":
                            pe.wait_ge(parts, part_at(name, kt - 1, b))
                        for k in range(kt):
                            if s == 0 and name in ("s1", "up0"):
                                pe.wait_ge(parts, (0 if name == "s1" else PARTS["up"]) + b * KT + k + 1)
                            for j, (wp, ap) in enumerate(((w_hi, 0), (w_hi, 1), (w_lo, 0))):
                                last = pe.matmul(banks[3 * s + b][:, 0:BW], wp[s][:, k, :],
                                                 operand[ap][:, k, blk(b)],
                                                 start=(k == 0 and j == 0), stop=(k == kt - 1 and j == 2))
                        last.then_inc(unit_done, 1)

            for name, n in PHASES:
                with pe.Fori(0, n) as i:
                    body(name, i, False)
                if name == "o":
                    for b in range(NB):
                        pe.wait_ge(sq_added, 21 + b + 1)
                        if b == 2:
                            pe.wait_ge(ln_done, 1)
                        pe.matmul(banks[6 + b % 2][:, 0:BW], ones, tmp[b][:, :], start=True,
                                  stop=True).then_inc(ms_done, 1)

        @block.scalar
        def _(act):
            def high(n_const, I):
                s = n_const % 2
                act.wait_ge(w_in[s], I * 16 + (16 * (n_const // 2) + 16))
                act.wait_ge(unit_done, I * 6 + (3 * n_const + 3))
                act.activation(w_hi[s][:, :, :], raw[s][:, :, :], ACT.Copy).then_inc(w_high, 1)

            def body(name, i, last_it):
                I = it(name, i)
                for s in range(2):
                    for b in range(NB):
                        t = i * 2 + s
                        if name in ("s1", "s2", "h", "o"):
                            act.wait_ge(freed, I * UNITS + (s * NB + b + 4))
                            src = {"h": (gate_dram, t + KT), "o": (x_dram, t)}.get(name, (gate_dram, t))
                            act.dma_start(gate[b][:, :], dram_blk(src[0], src[1], b)).then_inc(small_in[3 + b], 16)
                        if name in ("s1", "s2"):
                            nxt = {"s1": "s2", "s2": "h"}[name]
                            y0 = 8 if name == "s1" else 16
                            act.wait_ge(parts, part_at(nxt, t, b) - 3)
                            act.dma_start(stage[b][:, :], dram_blk(y_dram, t + y0, b)).then_inc(small_in[b], 16)
                        if b == 0 and not (last_it and s == 1):
                            high(s + 1, I)
                        if name in ("s1", "s2"):
                            act.wait_ge(unit_done, FIRST[name] * UNITS + UNITS)
                            act.wait_ge(small_in[b], I * 32 + (64 + 16 * s + 16))
                            act.activation(tile_blk(USES[nxt][0], t, b), stage[b][:, :],
                                           ACT.Copy).then_inc(hi_done, 1)
                        elif name == "h":
                            act.wait_ge(acc_done, acc_at(name, i, s, b))
                            act.wait_ge(unit_done, FIRST[name] * UNITS + UNITS)
                            act.activation(tile_blk(b_hi, t, b), tile_blk(x_acc, t, b),
                                           ACT.Copy).then_inc(hi_done, 1)
                        elif name == "o":
                            act.wait_ge(freed, free_at(name, i, s, b))
                            act.wait_ge(sq_added, t * NB + b)
                            act.activation(stage[b][:, :], tile_blk(x_acc, t, b), ACT.Square).then_inc(sq_done, 1)
                        elif name[0:2] == "up" and s == 0:
                            act.wait_ge(freed, I * UNITS + (2 * b + 1))
                            act.wait_ge(unit_done, done(name, i, s, b))
                            act.activation(stage[b][:, :], banks[b][:, 0:BW], ACT.Tanh,
                                           scale=0.5).then_inc(th_done, 1)
                        elif name[0:2] == "up":
                            act.wait_ge(freed, free_at(name, i, s, b))
                            act.activation(tile_blk(b_hi, i, b), tmp[b][:, :], ACT.Copy).then_inc(hi_done, 1)

            act.wait_ge(w_in[0], 16)
            act.activation(w_hi[0][:, :, :], raw[0][:, :, :], ACT.Copy).then_inc(w_high, 1)
            for u in range(24):
                b, k = divmod(u, KT)
                act.wait_ge(small_in[u % 6], 16 * (u // 6) + 16)
                act.activation(a_hi[:, k, blk(b)], small[u % 6][:, :], ACT.Copy).then_inc(hi_done, 1)
            act.wait_ge(parts, 24)
            for name, n in PHASES:
                if name == "down2":
                    with act.Fori(0, n - 1) as i:
                        body(name, i, False)
                    body(name, n - 1, True)
                else:
                    with act.Fori(0, n) as i:
                        body(name, i, False)
                if name == "o":
                    for b in range(NB):
                        act.wait_ge(ms_done, b + 1)
                        act.activation(stage[b][:, :], banks[6 + b % 2][:, 0:BW], ACT.Ln, scale=1.0 / D,
                                       bias=cst[:, K_EPS:K_EPS + 1]).then_inc(ln_done, 1)
                        act.wait_ge(ln_done, b + 1)
                        act.activation(stage[b][:, :], stage[b][:, :], ACT.Exp, scale=-0.5).then_inc(rstd_done, 1)
                        for k in range(KT):
                            act.wait_ge(t_done, b * KT + k + 1)
                            for who, lo, hi in ranges(b):
                                last = act.activation(a_hi[:, k, lo:hi], gate[(b * KT + k) % 3][:, lo - b * BW:hi - b * BW],
                                                      ACT.Identity, bias=mod[:, 24 + k, who:who + 1])
                            last.then_inc(hi_done, 1)

        @block.vector
        def _(dve):
            def low(n_const, I):
                s = n_const % 2
                dve.wait_ge(w_high, I * 2 + (n_const + 1))
                dve.tensor_tensor(w_lo[s][:, :, :], raw[s][:, :, :], w_hi[s][:, :, :].bitcast(F32),
                                  ALU.subtract).then_inc(w_split, 1)

            def body(name, i, last_it):
                I = it(name, i)
                for s in range(2):
                    for b in range(NB):
                        t = i * 2 + s
                        bank = banks[3 * s + b][:, 0:BW]
                        if name in ("s1", "s2", "h"):
                            dve.wait_ge(small_in[3 + b], I * 32 + (64 + 16 * s + 16))
                            dve.wait_ge(unit_done, done(name, i, s, b))
                            dst = tile_blk(x_acc, t, b)
                            if name == "s1":
                                dve.scalar_tensor_tensor(dst, gate[b][:, :], 1.0, bank, ALU.add,
                                                         ALU.mult).then_inc(freed, 1)
                            else:
                                dve.wait_ge(acc_done, acc_at(name, i, s, b) - 1)
                                dve.scalar_tensor_tensor(tmp[b][:, :], gate[b][:, :], 1.0, bank, ALU.add,
                                                         ALU.mult).then_inc(freed, 1)
                                dve.wait_ge(freed, free_at(name, i, s, b))
                                dve.tensor_tensor(dst, dst, tmp[b][:, :], ALU.add).then_inc(acc_done, 1)
                            nxt = {"s1": "s2", "s2": "h", "h": "o"}[name]
                            dve.wait_ge(hi_done, part_at(nxt, t, b))
                            src = dst if name == "h" else stage[b][:, :]
                            dve.tensor_tensor(tile_blk(USES[nxt][1], t, b), src,
                                              tile_blk(USES[nxt][0], t, b).bitcast(F32),
                                              ALU.subtract).then_inc(parts, 1)
                        elif name == "o" or name[0:4] == "down":
                            if name == "o":
                                dve.wait_ge(small_in[3 + b], I * 32 + (64 + 16 * s + 16))
                                dve.wait_ge(parts, PARTS["up"])
                            else:
                                dve.wait_ge(freed, I * UNITS + (UNITS + s * NB + b))
                            dve.wait_ge(unit_done, done(name, i, s, b))
                            j = 16 if name == "o" else 40
                            for who, lo, hi in ranges(b):
                                r = slice(lo - b * BW, hi - b * BW)
                                dst = tile_blk(x_acc, t, b)[:, r]
                                add = gate[b][:, r] if name == "o" else dst
                                last = dve.scalar_tensor_tensor(dst, bank[:, r], mod_col(j, t, who), add,
                                                                ALU.mult, ALU.add)
                            last.then_inc(freed, 1)
                        elif s == 1:
                            dve.wait_ge(th_done, (it(name, i) - n_th[name]) * NB + (b + 1))
                            dve.wait_ge(freed, free_at(name, i, 0, b) - 1)
                            dve.scalar_tensor_tensor(gate[b][:, :], stage[b][:, :], 1.0, banks[b][:, 0:BW],
                                                     ALU.add, ALU.mult).then_inc(freed, 1)
                            dve.wait_ge(freed, free_at(name, i, 0, b))
                            dve.wait_ge(unit_done, done(name, i, 1, b))
                            nxt = "down" + name[2]
                            dve.wait_ge(parts, part_at(nxt, i, b) - 3)
                            dve.tensor_tensor(tmp[b][:, :], gate[b][:, :], bank, ALU.mult).then_inc(freed, 1)
                            dve.wait_ge(hi_done, part_at(nxt, i, b))
                            dve.tensor_tensor(tile_blk(b_lo, i, b), tmp[b][:, :],
                                              tile_blk(b_hi, i, b).bitcast(F32), ALU.subtract).then_inc(parts, 1)
                        if b == (0 if name[0:2] == "up" else 1) and not (last_it and s == 1):
                            low(s + 1, I)

            n_th, off = {}, 0
            for name, n in PHASES:
                if name[0:2] == "up":
                    n_th[name] = off
                else:
                    off += n
            dve.sem_inc(freed, UNITS)
            dve.sem_inc(unit_done, UNITS)
            dve.sem_inc(acc_done, 1)
            dve.sem_inc(w_split, 2)
            low(0, 0)
            for u in range(24):
                b, k = divmod(u, KT)
                dve.wait_ge(hi_done, u + 1)
                dve.tensor_tensor(a_lo[:, k, blk(b)], small[u % 6][:, :], a_hi[:, k, blk(b)].bitcast(F32),
                                  ALU.subtract).then_inc(parts, 1)
            for name, n in PHASES:
                if name == "down2":
                    with dve.Fori(0, n - 1) as i:
                        body(name, i, False)
                    body(name, n - 1, True)
                else:
                    with dve.Fori(0, n) as i:
                        body(name, i, False)
                if name == "o":
                    def scaled(u):
                        b, k = divmod(u, KT)
                        dve.wait_ge(rstd_done, b + 1)
                        if u >= 3:
                            dve.wait_ge(parts, PARTS["up"] + u - 2)
                        for who, lo, hi in ranges(b):
                            last = dve.scalar_tensor_tensor(
                                gate[(b * KT + k) % 3][:, lo - b * BW:hi - b * BW], x_acc[:, k, lo:hi],
                                mod[:, 32 + k, who:who + 1], stage[b][:, lo - b * BW:hi - b * BW],
                                ALU.mult, ALU.mult)
                        last.then_inc(t_done, 1)

                    dve.wait_ge(freed, (FIRST["o"] + 5) * UNITS)
                    for u in range(24):
                        b, k = divmod(u, KT)
                        if k == 0:
                            scaled(u)
                        if k < KT - 1:
                            scaled(u + 1)
                        dve.wait_ge(hi_done, PARTS["up"] + u + 1)
                        for who, lo, hi in ranges(b):
                            last = dve.scalar_tensor_tensor(
                                a_lo[:, k, lo:hi], gate[(b * KT + k) % 3][:, lo - b * BW:hi - b * BW],
                                mod[:, 24 + k, who:who + 1], a_hi[:, k, lo:hi].bitcast(F32), ALU.add, ALU.subtract)
                        last.then_inc(parts, 1)

        @block.gpsimd
        def _(pool):
            pool.wait_ge(acc_done, acc_at("h", 3, 1, 2))
            for b in range(NB):
                pool.memset(tmp[b][:, :], 0.0).then_inc(sums_zero, 1)
            pool.wait_ge(sums_zero, 3)
            with pool.Fori(0, KT) as t:
                for b in range(NB):
                    pool.wait_ge(sq_done, t * NB + (b + 1))
                    pool.tensor_tensor(tmp[b][:, :], tmp[b][:, :], stage[b][:, :], ALU.add).then_inc(sq_added, 1)


def last_norm(nc, scope, sb, sem, m):
    cst, banks, x_acc, ident = m["cst"], m["banks"], m["x_acc"], m["ident"]
    out = [sb(f"out{i}", [P, D], F32, scope) for i in range(3)]
    sq = sb("last_sq", [P, 512], F32, scope)
    w_all = sb("w_all", [P, D], F32, scope)
    stat = sb("last_stat", [P, NC, 4], F32, scope)
    w_here, turned, sums, total = sem("w_here"), sem("turned"), sem("sums"), sem("total")
    lns, rstds, scaled = sem("lns"), sem("rstds"), sem("scaled")
    stored = [sem(f"stored{i}") for i in range(3)]

    with nc.Block() as block:
        @block.sync
        def _(sp):
            sp.dma_start(w_all[:, :], m["norm_final_w"].rearrange("(a n) -> a n", a=1).broadcast_to([P, D])
                         ).then_inc(w_here, 16)
            for c in range(NC):
                sp.wait_ge(scaled, 2 * (c + 1))
                dst = m["y_prompt"][0] if c == 0 else m["y_sample"][0, (c - 1) * P:c * P, :]
                sp.dma_start(dst, out[c % 3][:, :]).then_inc(stored[c % 3], 16)
            for i in range(3):
                sp.wait_ge(stored[i], 16 * NC // 3)

        @block.tensor
        def _(pe):
            for c in range(NC):
                if c >= 4:
                    pe.wait_ge(scaled, 2 * (c - 3))
                for k in range(KT):
                    last = pe.transpose(banks[2 * (c % 4) + k // 4][:, (k % 4) * P:(k % 4 + 1) * P],
                                        x_acc[:, k, chunk(c)], ident)
                last.then_inc(turned, 1)

        @block.scalar
        def _(act):
            for c in range(NC):
                act.wait_ge(turned, c + 1)
                for j in range(2):
                    if c or j:
                        act.wait_ge(sums, 2 * c + j)
                    act.activation(sq[:, :], banks[2 * (c % 4) + j][:, :], ACT.Square,
                                   accum_out=stat[:, c, j:j + 1]).then_inc(sums, 1)
                act.wait_ge(total, c + 1)
                act.activation(stat[:, c, 3:4], stat[:, c, 2:3], ACT.Ln, scale=1.0 / D,
                               bias=cst[:, K_EPS:K_EPS + 1]).then_inc(lns, 1)
                act.wait_ge(lns, c + 1)
                act.activation(stat[:, c, 0:1], stat[:, c, 3:4], ACT.Exp, scale=-0.5).then_inc(rstds, 1)

        @block.vector
        def _(dve):
            dve.wait_ge(w_here, 16)
            for c in range(NC):
                dve.wait_ge(sums, 2 * c + 2)
                dve.tensor_tensor(stat[:, c, 2:3], stat[:, c, 0:1], stat[:, c, 1:2], ALU.add).then_inc(total, 1)
                dve.wait_ge(rstds, c + 1)
                if c >= 3:
                    dve.wait_ge(stored[c % 3], 16 * (c // 3))
                for j in range(2):
                    dve.scalar_tensor_tensor(out[c % 3][:, j * 512:(j + 1) * 512], banks[2 * (c % 4) + j][:, :],
                                             stat[:, c, 0:1], w_all[:, j * 512:(j + 1) * 512], ALU.mult,
                                             ALU.mult).then_inc(scaled, 1)


_INS = ["x_prompt", "x_sample", "c", "state_ssm", "state_hgrn", "c_ctx", "norm_mix_w", "norm_ffn_w", "ada_w", "ada_b",
        "w_in", "ssd_conv_w", "ssd_conv_b", "ssd_dt_bias", "ssd_a_log", "ssd_d", "ssd_norm_w", "hgrn_norm_w",
        "w_ssd_out", "w_hgrn_out", "w_out", "ffn_w1", "ffn_w3", "ffn_w2", "norm_final_w"]
_OUTS = [(1, 128, 1024), (1, 1024, 1024), (1, 1, 2, 32, 64, 128), (1, 1, 2, 8, 128, 128)]


def constants(np):
    cst = np.zeros((P, K_W), np.float32)
    i = np.arange(P)
    cst[:, K_ID:K_ID + P] = np.eye(P)
    cst[:, K_ONE:K_ONE + P] = 1
    cst[:, K_RESET:K_RESET + BW] = np.arange(BW)[None, :] % P != 0
    apart = i[:, None] ^ i[None, :]
    masks = np.zeros((P, LEVELS, P), np.float32)
    for lv in range(1, LEVELS):
        masks[:, lv - 1] = (apart >= 64 >> lv) & (apart < 128 >> lv)
    masks[:, LEVELS - 1] = apart == 0
    cst[:, K_M64:K_M64 + P] = apart >= 64
    neg = np.zeros((P, 2, P), np.float32)
    neg[:, 0] = np.where(i[None, :] >= i[:, None], 0, -1e30)
    neg[:, 1] = np.where(i[None, :] <= i[:, None], 0, -1e30)
    cst[:, K_EPS], cst[:, K_EPS4], cst[:, K_1] = EPS, 4 * EPS, 1
    return cst, neg, masks


def kernel(**inputs):
    import numpy as np
    import concourse.bacc as bacc
    from concourse.bass_utils import run_bass_kernel_spmd

    nc = bacc.Bacc("TRN2", target_bir_lowering=False, num_devices=1, dynamic_dma_scratch_size=1024)
    arrays = dict(zip(("constants", "causal_masks", "chunk_masks"), constants(np)))
    for name in _INS:
        arrays[f"in_{name}"] = np.ascontiguousarray(inputs[name])
    args = [nc.dram_tensor(n, a.shape, mybir.dt.from_np(a.dtype), kind="ExternalInput").ap()
            for n, a in arrays.items()]
    for i, shape in enumerate(_OUTS):
        args.append(nc.dram_tensor(f"out_{i}", shape, F32, kind="ExternalOutput").ap())
    build(nc, *args)
    r = run_bass_kernel_spmd(nc, [arrays], core_ids=[0])
    return tuple(r.results[0][f"out_{i}"] for i in range(len(_OUTS)))
```

```python
from contextlib import ExitStack

import concourse.bass as bass
from concourse import mybir

F32 = mybir.dt.float32
F32R = mybir.dt.float32r
BF16 = mybir.dt.bfloat16
U8 = mybir.dt.uint8
ALU = mybir.AluOpType
ACT = mybir.ActivationFunctionType

P = 128
D = 1024
KT = D // P
CTX = 128
T = 1152
NC = T // P
NB = 3
BW = T // NB
CB = BW // P
GRID = 64
ROWS = BW // GRID
G = 8
HPG = 4
HD = 64
GW = HPG * HD
TAPS = 5
FFN = 2816
EPS = 1e-6

COL_X, COL_B, COL_C, COL_Z, COL_DT = 0, 2048, 3072, 4096, 6144
COL_Q, COL_FF, COL_FB, COL_I, COL_G, COL_GATE = 6208, 7232, 8256, 9280, 10304, 11328

V_TAP4, V_CONVB, V_ADAB, V_MIX, V_FFN = 128, 160, 192, 240, 248
V_SSDN, V_HGRN, V_C, V_CCTX, V_D, V_END = 256, 272, 280, 288, 296, 312

TILES_BEFORE = 7
TILES_GROUP = 12
UNITS_BEFORE = TILES_BEFORE * NB
UNITS_GROUP = TILES_GROUP * NB
SLOTS = 18

LEVELS = 7
STEPS = [("kb", 2, 0), ("kb", 1, 0), ("kb", 0, 0), ("kf", 0, 0)]
for _b in range(NB):
    STEPS += [("lv", _b, _l) for _l in range(LEVELS)] + [("dg", _b, LEVELS), ("q", _b, 0)]
    if _b < NB - 1:
        STEPS.append(("kf", _b + 1, 0))
NSTEP = len(STEPS)
ACT_ROUND, DVE_ROUND, DT_ACT, DT_DVE = 11, 112, 7, 19
KSTEPS = [n for n, s in enumerate(STEPS) if s[0] in ("kb", "kf")]
QSTEPS = [n for n, s in enumerate(STEPS) if s[0] == "q"]
ASTEPS = [n for n, s in enumerate(STEPS) if s[0] != "q"]
VSTEPS = [n for n, s in enumerate(STEPS) if s[0] not in ("kb", "kf")]
MSTEPS = [n for n, s in enumerate(STEPS) if s[0] in ("lv", "dg")]


def slot_of(n):
    return 0 if n < 4 else (n - 2) // 2


def steps_in(slot):
    return [n for n in range(NSTEP) if slot_of(n) == slot]


def contrib_slot(n):
    return slot_of(n) + (3 if n in (2, 3) else 2)


class Count:

    def __init__(self, sem, per_round=0, before=0):
        self.sem, self.per, self.before = sem, per_round, before

    def at(self, g, n):
        return n if g is None else g * self.per + (self.before + n)


class Chain:

    def __init__(self, sem, per_round=0, before=0):
        self.sem, self.per, self.before, self.n, self.g = sem, per_round, before, 0, 0

    def round(self, g):
        self.g, self.n = g, 0

    def add(self, ins):
        self.n += 1
        ins.then_inc(self.sem, 1)
        return ins

    def wait(self, eng):
        if self.n > 0:
            eng.wait_ge(self.sem, self.g * self.per + (self.before + self.n))


CONV_TILES = (2, 3, 4, 5)


def conv_index(k):
    return k - 2 * NB


def b_tile(k):
    return k // NB, NB - 1 - k % NB


def halves(v, s):
    v = v.rearrange("p (n two s) -> p n two s", two=2, s=s)
    return v[:, :, 0, :], v[:, :, 1, :]


def blk(b):
    return slice(b * BW, (b + 1) * BW)


def chunk(c):
    return slice(c * P, (c + 1) * P)


def ranges(b):
    return [(0, 0, CTX), (1, CTX, BW)] if b == 0 else [(1, b * BW, (b + 1) * BW)]


K_ID, K_ONE, K_RESET, K_M64 = 0, 128, 256, 640
K_FOLD, K_EPS, K_EPS4, K_1, K_W = 768, 832, 833, 834, 836


def build(nc, cst_in, neg_in, masks_in, x_prompt, x_sample, c_in, state_ssm, state_hgrn, c_ctx, norm_mix_w, norm_ffn_w,
          ada_w, ada_b, w_in, ssd_conv_w, ssd_conv_b, ssd_dt_bias, ssd_a_log, ssd_d, ssd_norm_w, hgrn_norm_w,
          w_ssd_out, w_hgrn_out, w_out, ffn_w1, ffn_w3, ffn_w2, norm_final_w,
          y_prompt, y_sample, new_ssm, new_hgrn):
    with ExitStack() as ctx:
        def sb(name, shape, dt=F32, stack=ctx):
            return stack.enter_context(nc.sbuf_tensor(name, shape, dt))

        def sem(name):
            return ctx.enter_context(nc.semaphore(name))

        mem = {}
        cst = sb("cst", [P, K_W])
        vec = sb("vec", [P, V_END])
        mod = sb("mod", [P, 48, 2])
        raw = [sb(f"raw{i}", [P, KT, P]) for i in range(2)]
        banks = [ctx.enter_context(nc.psum_tensor(f"bank{i}", [P, 512], F32)) for i in range(8)]
        y_dram = nc.dram_tensor("y_scratch", [24, P, T], F32, kind="Internal").ap()
        gate_dram = nc.dram_tensor("gate_scratch", [16, P, T], F32, kind="Internal").ap()
        x_dram = nc.dram_tensor("x_scratch", [KT, P, T], F32, kind="Internal").ap()
        ident, ones = cst[:, K_ID:K_ID + P], cst[:, K_ONE:K_ONE + P]

        def x_rows(c):
            return x_prompt[0] if c == 0 else x_sample[0, (c - 1) * P:c * P, :]

        def w_tile(w, col, width=P):
            return w[:, col:col + width] if isinstance(col, int) else w[:, bass.ds(col, width)]

        def w_src(w, col, width=P):
            return w_tile(w, col, width).rearrange("(k p) c -> p k c", p=P)

        w_landed = [sem("w_landed0"), sem("w_landed1")]
        m_w_in = [sem(f"m_w_in{i}") for i in range(2)]
        with ExitStack() as keep_h:
            masks = sb("masks", [P, LEVELS, P], U8, keep_h)
            h_hi = sb("h_hi", [P, KT, T], F32R, keep_h)
            h_lo = sb("h_lo", [P, KT, T], F32R, keep_h)
            with ExitStack() as scope:
                setup(nc, scope, sb, sem, locals())
            with ExitStack() as scope:
                mixers(nc, scope, sb, sem, locals())
        x_acc = sb("x_acc", [P, KT, T])
        with ExitStack() as scope:
            merge_and_ffn(nc, scope, sb, sem, locals())
        with ExitStack() as scope:
            last_norm(nc, scope, sb, sem, locals())


def setup(nc, scope, sb, sem, m):
    cst, masks, vec, mod, banks, ident = m["cst"], m["masks"], m["vec"], m["mod"], m["banks"], m["ident"]
    h_hi, h_lo, x_rows, raw = m["h_hi"], m["h_lo"], m["x_rows"], m["raw"]
    ada_w = m["ada_w"][0]
    ADA_T = 4
    ADA_N = 48 // ADA_T
    H_AT = {5: 0, 8: 1, 10: 2}
    rows = sb("rows", [P, 3, P], F32, scope)
    ada = [sb(f"ada{i}", [P, KT, ADA_T * P], F32, scope) for i in range(3)]
    mod_row = [sb(f"mod_row{i}", [2, ADA_T * P], F32, scope) for i in range(2)]
    xt = [sb(f"xt{i}", [P, D], F32, scope) for i in range(3)]
    xn_t = sb("xn_t", [P, KT, T], F32, scope)
    d_all = sb("d_all", [P, 32], F32, scope)
    junk = sb("junk", [P, D], F32, scope)
    stat = sb("stat", [P, NC, 3], F32, scope)
    cs = sb("cs", [P, KT, 2], F32, scope)
    cth = sb("cth", [P, 16], F32, scope)
    aff = sb("aff", [P, KT, 2], F32, scope)
    xs = [sb(f"xs{i}", [P, KT, P], F32, scope) for i in range(2)]

    consts_in, rows_in = sem("consts_in"), sem("rows_in")
    masks_in, masks_ok = sem("masks_in"), sem("masks_ok")
    x_in = [sem(f"x_in{i}") for i in range(3)]
    ada_in = [sem(f"ada_in{i}") for i in range(3)]
    row_kept, mod_turned, mod_read = sem("row_kept"), sem("mod_turned"), sem("mod_read")
    rows_turned, vec_ready, c_ready = sem("rows_turned"), sem("vec_ready"), sem("c_ready")
    x_scaled, x_turned, x_kept = sem("x_scaled"), sem("x_turned"), sem("x_kept")
    x_kept2 = sem("x_kept2")
    raw_turned, raw_kept, raw_kept2 = sem("raw_turned"), sem("raw_kept"), sem("raw_kept2")
    xs_stored = [sem("xs_stored0"), sem("xs_stored1")]
    ada_used, aff_ready = sem("ada_used"), sem("aff_ready")
    h_made, rstd_ready, th_ready = sem("h_made"), sem("rstd_ready"), sem("th_ready")
    act_s, dve_s = sem("setup_act"), sem("setup_dve")

    def keep_dve(dve, c):
        dve.wait_ge(x_turned, c + 1)
        dve.tensor_copy(xn_t[:, 0:4, chunk(c)],
                        banks[2 + 2 * (c % 2)][:, :].rearrange("p (k t) -> p k t", t=P)
                        ).then_inc(x_kept, 1)

    with nc.Block() as block:
        @block.sync
        def _(sp):
            sp.dma_start(cst[:, :], m["cst_in"]).then_inc(consts_in, 16)
            sp.dma_start(junk[:, 0:LEVELS * P], m["masks_in"].rearrange("p l i -> p (l i)")).then_inc(masks_in, 16)

            def row(part, col, src, n):
                sp.dma_start(rows[part:part + n, col, :], src).then_inc(rows_in, 16)

            row(0, 0, m["ssd_conv_w"][0, 0:4, :].rearrange("k (t p) -> (k t) p", p=P), 128)
            row(0, 1, m["ssd_conv_w"][0, 4, :].rearrange("(t p) -> t p", p=P), 32)
            row(32, 1, m["ssd_conv_b"][0].rearrange("(t p) -> t p", p=P), 32)
            row(64, 1, m["ada_b"][0].rearrange("(t p) -> t p", p=P), 48)
            row(112, 1, m["norm_mix_w"][0].rearrange("(t p) -> t p", p=P), 8)
            row(120, 1, m["norm_ffn_w"][0].rearrange("(t p) -> t p", p=P), 8)
            row(0, 2, m["ssd_norm_w"][0].rearrange("(t p) -> t p", p=P), 16)
            row(16, 2, m["hgrn_norm_w"][0].rearrange("(t p) -> t p", p=P), 8)
            row(24, 2, m["c_in"][0].rearrange("(t p) -> t p", p=P), 8)
            row(32, 2, m["c_ctx"].rearrange("(t p) -> t p", p=P), 8)
            sp.dma_start(d_all[:, :], m["ssd_d"][0].rearrange("(a h) -> a h", a=1).broadcast_to([P, 32])
                         ).then_inc(rows_in, 16)
            def load_ada(j):
                sp.dma_start(ada[j % 3][:, :, :], ada_w[:, j * ADA_T * P:(j + 1) * ADA_T * P]
                             .rearrange("(k p) c -> p k c", p=P)).then_inc(ada_in[j % 3], 16)

            for c in range(3):
                sp.dma_start(xt[c][:, :], x_rows(c)).then_inc(x_in[c], 16)
                load_ada(c)
            for i, (col, n) in enumerate(((COL_DT, HD), (COL_Z, P))):
                sp.dma_start(raw[i][:, :, 0:n], m["w_src"](m["w_in"][0], col, n)).then_inc(m["w_landed"][i], 16)
            for j in range(3, ADA_N):
                sp.wait_ge(ada_used, j - 2)
                load_ada(j)
                if j < NC:
                    sp.wait_ge(x_turned, j - 2)
                    sp.dma_start(xt[j % 3][:, :], x_rows(j)).then_inc(x_in[j % 3], 16)

        @block.tensor
        def _(pe):
            pe.wait_ge(consts_in, 16)
            pe.wait_ge(rows_in, 16 * 11)
            for i in range(3):
                n = P if i < 2 else 40
                last = pe.transpose(banks[0][:, i * P:i * P + n], rows[0:n, i, :], ident[0:n, 0:n])
            last.then_inc(rows_turned, 1)

            def turn_raw(c):
                pe.wait_ge(x_in[c % 3], 16 * (c // 3 + 1))
                if c > 0:
                    pe.wait_ge(raw_kept, c)
                    pe.wait_ge(raw_kept2, c)
                for k in range(KT):
                    last = pe.transpose(banks[6 + k // 4][:, (k % 4) * P:(k % 4 + 1) * P],
                                        xt[c % 3][:, k * P:(k + 1) * P], ident)
                last.then_inc(raw_turned, 1)

            def turn(c):
                pe.wait_ge(x_scaled, c + 1)
                if c >= 2:
                    pe.wait_ge(x_kept, c - 1)
                    pe.wait_ge(x_kept2, c - 1)
                for k in range(KT):
                    last = pe.transpose(banks[2 + 2 * (c % 2) + k // 4][:, (k % 4) * P:(k % 4 + 1) * P],
                                        xt[c % 3][:, k * P:(k + 1) * P], ident)
                last.then_inc(x_turned, 1)

            pe.wait_ge(c_ready, 2)
            for j in range(ADA_N):
                pe.wait_ge(ada_in[j % 3], 16 * (j // 3 + 1))
                if j > 0:
                    pe.wait_ge(row_kept, j)
                for k in range(KT):
                    last = pe.matmul(banks[1][0:2, :], cs[:, k, :], ada[j % 3][:, k, :],
                                     start=(k == 0), stop=(k == KT - 1))
                last.then_inc(ada_used, 1)
                if j < NC:
                    turn_raw(j)
                    turn(j)
                pe.wait_ge(row_kept, j + 1)
                if j == ADA_T:
                    pe.wait_ge(mod_read, 1)
                for t in range(ADA_T):
                    col = 2 * (j * ADA_T + t)
                    last = pe.transpose(banks[0][:, col:col + 2], mod_row[j % 2][:, t * P:(t + 1) * P],
                                        ident[0:2, 0:2])
                last.then_inc(mod_turned, 1)

        @block.scalar
        def _(act):
            ch = Chain(act_s)
            act.wait_ge(rows_turned, 1)
            ch.add(act.activation(vec[:, 0:256], banks[0][:, 0:256], ACT.Copy))
            for e in range(2):
                r = slice(e * HD, (e + 1) * HD)
                ch.add(act.activation(vec[r, V_D:V_END], d_all[r, e:32:2], ACT.Copy))
            act.activation(vec[:, 256:V_D], banks[0][:, 256:V_D], ACT.Copy).then_inc(vec_ready, 1)
            act.wait_ge(vec_ready, 1)
            act.activation(cth[:, :], vec[:, V_C:V_C + 16], ACT.Tanh, scale=0.5).then_inc(th_ready, 1)
            ch.wait(act)
            ch.add(act.mul(vec[:, 0:V_ADAB], vec[:, 0:V_ADAB], 0.5))
            ch.add(act.mul(vec[:, V_HGRN:V_HGRN + 8], vec[:, V_HGRN:V_HGRN + 8], 0.5))

            def rstd(c):
                act.wait_ge(x_in[c % 3], 16 * (c // 3 + 1))
                ch.wait(act)
                ch.add(act.activation(junk[:, :], xt[c % 3][:, :], ACT.Square, accum_out=stat[:, c, 0:1]))
                ch.wait(act)
                ch.add(act.activation(stat[:, c, 1:2], stat[:, c, 0:1], ACT.Ln, scale=1.0 / D,
                                      bias=cst[:, K_EPS:K_EPS + 1]))
                ch.wait(act)
                act.activation(stat[:, c, 2:3], stat[:, c, 1:2], ACT.Exp, scale=-0.5).then_inc(rstd_ready, 1)

            def keep(c):
                act.wait_ge(x_turned, c + 1)
                act.activation(xn_t[:, 4:8, chunk(c)],
                               banks[3 + 2 * (c % 2)][:, :].rearrange("p (k t) -> p k t", t=P),
                               ACT.Copy).then_inc(x_kept2, 1)

            act.wait_ge(masks_ok, 1)
            def make_h(b):
                act.wait_ge(aff_ready, 1)
                act.wait_ge(x_kept2, CB * (b + 1))
                act.wait_ge(x_kept, CB * (b + 1))
                for k in range(KT):
                    for who, lo, hi in ranges(b):
                        last = act.activation(xn_t[:, k, lo:hi], xn_t[:, k, lo:hi], ACT.Identity,
                                              scale=aff[:, k, who:who + 1], bias=mod[:, k, who:who + 1])
                    last.then_inc(h_made, 1)

            for c in range(ADA_N):
                if c < NC:
                    rstd(c)
                    act.wait_ge(raw_turned, c + 1)
                    if c >= 2:
                        act.wait_ge(xs_stored[c % 2], 16 * (c // 2))
                    act.activation(xs[c % 2][:, 4:8, :], banks[7][:, :].rearrange("p (k t) -> p k t", t=P),
                                   ACT.Copy).then_inc(raw_kept2, 1)
                    act.wait_ge(raw_kept2, c + 1)
                    act.wait_ge(raw_kept, c + 1)
                    act.dma_start(m["x_dram"][:, :, chunk(c)].rearrange("k p t -> p k t"),
                                  xs[c % 2][:, :, :]).then_inc(xs_stored[c % 2], 16)
                if 0 < c <= NC:
                    keep(c - 1)
                if c in H_AT:
                    make_h(H_AT[c])
            for i in range(2):
                act.wait_ge(xs_stored[i], 16 * ((NC + 1 - i) // 2))

        @block.vector
        def _(dve):
            ch = Chain(dve_s)
            dve.wait_ge(masks_in, 16)
            dve.tensor_copy(masks[:, :, :].rearrange("p l i -> p (l i)"), junk[:, 0:LEVELS * P]
                            ).then_inc(masks_ok, 1)
            dve.wait_ge(th_ready, 1)
            for who, col in ((1, V_C), (0, V_CCTX)):
                dve.scalar_tensor_tensor(cs[:, :, who], cth[:, col - V_C:col - V_C + 8], 1.0,
                                         vec[:, col:col + 8], ALU.add, ALU.mult).then_inc(c_ready, 1)
            def spread(v):
                return v.rearrange("p (m a) -> p m a", a=1).broadcast_to([P, v.shape[1], 2])

            def read_mod(lo, hi):
                dve.wait_ge(mod_turned, hi // ADA_T)
                return dve.scalar_tensor_tensor(mod[:, lo:hi, :],
                                                banks[0][:, 2 * lo:2 * hi].rearrange("p (m a) -> p m a", a=2), 0.5,
                                                spread(vec[:, V_ADAB + lo:V_ADAB + hi]), ALU.mult, ALU.add)

            def split_h(b):
                for k in range(KT):
                    dve.wait_ge(h_made, b * KT + k + 1)
                    ch.add(dve.tensor_copy(h_hi[:, k, blk(b)], xn_t[:, k, blk(b)]))
                    ch.wait(dve)
                    ch.add(dve.tensor_tensor(h_lo[:, k, blk(b)], xn_t[:, k, blk(b)],
                                             h_hi[:, k, blk(b)].bitcast(F32), ALU.subtract))

            for j in range(ADA_N):
                dve.wait_ge(ada_used, j + 1)
                if j >= 2:
                    dve.wait_ge(mod_turned, j - 1)
                dve.tensor_copy(mod_row[j % 2][:, :], banks[1][0:2, :]).then_inc(row_kept, 1)
                if j < NC:
                    c = j
                    dve.wait_ge(raw_turned, c + 1)
                    if c >= 2:
                        dve.wait_ge(xs_stored[c % 2], 16 * (c // 2))
                    dve.tensor_copy(xs[c % 2][:, 0:4, :], banks[6][:, :].rearrange("p (k t) -> p k t", t=P)
                                    ).then_inc(raw_kept, 1)
                    dve.wait_ge(rstd_ready, c + 1)
                    dve.tensor_scalar(xt[c % 3][:, :], xt[c % 3][:, :], stat[:, c, 2:3], None,
                                      ALU.mult).then_inc(x_scaled, 1)
                if 0 < j <= NC:
                    keep_dve(dve, j - 1)
                if j == ADA_T:
                    read_mod(0, 16).then_inc(mod_read, 1)
                    dve.wait_ge(mod_read, 1)
                    dve.scalar_tensor_tensor(aff[:, :, :], mod[:, 8:16, :], 1.0, spread(vec[:, V_MIX:V_MIX + 8]),
                                             ALU.add, ALU.mult).then_inc(aff_ready, 1)
                if j in H_AT:
                    split_h(H_AT[j])
            ch.add(read_mod(16, 48))
            ch.wait(dve)
            ch.add(dve.scalar_tensor_tensor(mod[:, 32:40, :], mod[:, 32:40, :], 1.0, spread(vec[:, V_FFN:V_FFN + 8]),
                                            ALU.add, ALU.mult))
            ch.add(dve.tensor_scalar(mod[:, 16:24, :], mod[:, 16:24, :], 0.5, None, ALU.mult))
            ch.add(dve.tensor_scalar(mod[:, 40:48, :], mod[:, 40:48, :], 0.5, None, ALU.mult))


def mixers(nc, scope, sb, sem, m):
    cst, masks, vec, raw, banks = m["cst"], m["masks"], m["vec"], m["raw"], m["banks"]
    ident, ones = m["ident"], m["ones"]
    h_hi, h_lo, w_src = m["h_hi"], m["h_lo"], m["w_src"]
    w_in, y_dram, gate_dram = m["w_in"][0], m["y_dram"], m["gate_dram"]
    S = banks[2:8]
    K_BANKS = (S[1], S[2], S[0], S[5], S[5], S[5])
    reset = cst[:, K_RESET:K_RESET + BW]

    w_hi = [sb(f"w_hi{i}", [P, KT, P], F32R, scope) for i in range(2)]
    w_lo = [sb(f"w_lo{i}", [P, KT, P], F32R, scope) for i in range(2)]
    pad = [sb(f"pad{b}", [P, ROWS, GRID + 4], F32, scope) for b in range(NB)]
    acc = [sb(f"acc{i}", [P, BW], F32, scope) for i in range(2)]
    th = [sb(f"th{i}", [P, BW], F32, scope) for i in range(2)]
    x_t = sb("x_t", [P, 2, T], F32, scope)
    z_t = sb("z_t", [P, 2, T], F32, scope)
    b_t = sb("b_t", [P, T], F32, scope)
    c_t = sb("c_t", [P, T], F32, scope)
    f_t = sb("f_t", [P, T], F32, scope)
    g_t = sb("g_t", [P, T], F32, scope)
    kf_t = sb("kf_t", [P, T], F32, scope)
    kb_t = sb("kb_t", [P, T], F32, scope)
    q_t = sb("q_t", [P, T], F32, scope)
    s_t = sb("s_t", [P, T], F32, scope)
    v_tok = sb("v_tok", [P, NC, P], F32, scope)
    cum_hl = sb("cum_hl", [P, T], F32R, scope)
    tok = sb("tok", [P, 3, NC, 64], F32, scope)
    dec = sb("dec", [P, NC, 64], F32, scope)
    tok_g = sb("tok_g", [P, 3, NC, 8], F32, scope)
    dec_g = sb("dec_g", [P, NC, 8], F32, scope)
    sel = sb("sel", [P, 8, P], F32R, scope)
    taps = sb("taps", [P, 4, TAPS + 1], F32, scope)
    vec_g = sb("vec_g", [P, 5], F32, scope)
    id_bf = sb("id_bf", [P, P], BF16, scope)
    neg_bf = [sb(f"neg_bf{d}", [P, P], BF16, scope) for d in range(2)]
    cols = sb("cols", [64, 4], F32, scope)

    st_in = sb("st_in", [P, 4, P], F32, scope)
    so_h = sb("so_h", [P, 2, P], F32, scope)
    with ExitStack() as ssd_scope:
        xb = [sb(f"xb{i}", [P, 512], F32, ssd_scope) for i in range(4)]
        xp = sb("xp", [P, 2, GW], F32, ssd_scope)
        s_b = sb("s_b", [P, NC - 1, GW], F32, ssd_scope)
        s_f = sb("s_f", [P, GW], F32, ssd_scope)
        t_off = sb("t_off", [P, 512], F32, ssd_scope)
        y_tok = t_off[:, 0:GW]
        me = sb("me", [P, 2048], F32, ssd_scope)
        mm = me[:, 0:1024].rearrange("p (e n) -> p e n", e=2)
        ex = me[:, 1024:2048]
        rstd = me[:, 2048 - T:2048]
    with ExitStack() as hgrn_scope:
        qk = [sb(f"qk{i}", [P, 2, BW], F32, hgrn_scope) for i in range(4)]
        ktok = [sb(f"ktok{i}", [P, BW], F32, hgrn_scope) for i in range(4)]
        at = [sb(f"at{i}", [P, BW], F32, hgrn_scope) for i in range(2)]
        hs_f = sb("hs_f", [P, NC - 1, P], F32, hgrn_scope)
        hs_b = sb("hs_b", [P, NC - 1, P], F32, hgrn_scope)
        hdec = sb("hdec", [P, 2, NC], F32, hgrn_scope)
    dt_v, dt_a, dt_b, dt_c, dt_d, dt_e = f_t, g_t, kf_t, kb_t, q_t, s_t
    cum = x_t[0:64, 0, :]

    w_landed = m["w_landed"]
    w_high, w_split = Count(sem("w_high"), TILES_GROUP), Count(sem("w_split"), TILES_GROUP)
    unit_done = Count(sem("unit_done"), UNITS_GROUP)
    bank_free = [sem("bank_free0"), sem("bank_free1")]
    cols_in, cols_ok, bf_ok = sem("cols_in"), sem("cols_ok"), sem("bf_ok")
    pads_zero, taps_ok = sem("pads_zero"), sem("taps_ok")
    conved, silu_done = Count(sem("conved"), 4 * NB, 4 * NB), Count(sem("silu_done"), 4 * NB, 4 * NB)
    tap_done = Count(sem("tap_done"), 4 * NB, 4 * NB)
    th_ok = Count(sem("th_ok"), 8 * NB, 6 * NB)
    gate_stored = [sem("gate_stored0"), sem("gate_stored1")]
    v_turned, v_kept = sem("v_turned"), sem("v_kept")
    dt_act, dt_dve, dt_turned, dt_kept = sem("dt_act"), sem("dt_dve"), sem("dt_turned"), sem("dt_kept")
    f_raw, f_log, f_lnk, f_ready = sem("f_raw"), sem("f_log"), sem("f_lnk"), sem("f_ready")
    k_ready = sem("k_ready")
    act_s = Chain(sem("act_step"), ACT_ROUND)
    dve_s = Chain(sem("dve_step"), DVE_ROUND)
    NTR, NA1, NA1P = 1 + 7 + NC, 7, 4
    st_loaded = sem("st_loaded")
    tr_ready, tr_kept = Count(sem("tr_ready"), NTR), Count(sem("tr_kept"), NTR)
    grp_ready, sel_ready = sem("grp_ready"), sem("sel_ready")
    xp_ready = Count(sem("xp_ready"), NA1P + NC)
    ctb_ready, ctb_used = Count(sem("ctb_ready"), NA1P), Count(sem("ctb_used"), NA1P)
    arg_ready, exp_ready = Count(sem("arg_ready"), NC), Count(sem("exp_ready"), NC)
    sum_ready, m_ready = Count(sem("sum_ready"), NC), Count(sem("m_ready"), NC)
    y_ready, y_made = Count(sem("y_ready"), NC), Count(sem("y_made"), NC)
    yt_ready, yt_made = Count(sem("yt_ready"), NC), Count(sem("yt_made"), NC)
    sq_ready, ms_ready = Count(sem("sq_ready"), NB), Count(sem("ms_ready"), NB)
    ms_read = sem("ms_read")
    rstd_ok, y_final, y_stored, so_stored = sem("rstd_ok"), sem("y_final"), sem("y_stored"), sem("so_stored")
    NK, NM = len(KSTEPS), len(MSTEPS)
    hs_loaded, hdec_ok = sem("hs_loaded"), sem("hdec_ok")
    arg_made, exp_made = Count(sem("arg_made"), len(ASTEPS)), Count(sem("exp_made"), NSTEP)
    qk_ready = Count(sem("qk_ready"), len(VSTEPS))
    kt_ready, kt_kept = Count(sem("kt_ready"), NK), Count(sem("kt_kept"), NK)
    kc_ready, kc_used = Count(sem("kc_ready"), NK), Count(sem("kc_used"), NK)
    lv_ready, lv_used = Count(sem("lv_ready"), NM), Count(sem("lv_used"), NM)
    merge_clear = sem("merge_clear")
    o_ready, o_kept = Count(sem("o_ready"), NB), Count(sem("o_kept"), NB)
    hms_ready, hms_kept = Count(sem("hms_ready"), NB), Count(sem("hms_kept"), NB, before=1)
    hrstd_ok, o_final, o_stored, soh_stored = sem("hrstd_ok"), sem("o_final"), sem("o_stored"), sem("soh_stored")

    def numbered(const, g):
        if g is None:
            return const % 2, const // 2, const
        return const % 2, g * (UNITS_GROUP // 2) + const // 2, g * UNITS_GROUP + const

    def used_by_pe(eng, g, n):
        for count, steps in ((kt_ready, KSTEPS), (lv_ready, MSTEPS), (o_ready, QSTEPS)):
            if n in steps:
                eng.wait_ge(count.sem, count.at(g, steps.index(n) + 1))

    def a_unit(g, k):
        return numbered(UNITS_BEFORE + k, g)

    def b_unit(g, k):
        return numbered(NB + k, None) if g is None else numbered(UNITS_BEFORE + SLOTS + k, g)

    def tile(g, t):
        if g is None:
            return t % 2, t // 2, t
        n = TILES_BEFORE + t
        return n % 2, g * (TILES_GROUP // 2) + n // 2, g * TILES_GROUP + n

    PRO_COLS = [(COL_DT, 64), (COL_Z, P), (COL_Z + P, P), (COL_B, P), (COL_C, P), (COL_X, P), (COL_X + P, P)]
    A_COLS = [(COL_FF, P), (COL_FB, P), (COL_Q, P), (COL_G, P), (COL_GATE, P), (COL_I, P)]
    B_COLS = [(COL_Z, GW), (COL_Z + P, GW), (COL_B, P), (COL_C, P), (COL_X, GW), (COL_X + P, GW)]

    with nc.Block() as block:
        @block.sync
        def _(sp):
            def load(g, t, col, width=P):
                i, _, n = tile(g, t)
                if not (g is None and t < 2):
                    sp.wait_ge(w_split.sem, n - 1)
                sp.dma_start(raw[i][:, :, 0:width], w_src(w_in, col, width)).then_inc(w_landed[i], 16)

            def stage_a(g):
                for t, (base, step) in enumerate(A_COLS):
                    load(g, t, g * step + base)

            def stores(g, last):
                sp.wait_ge(y_final, g + 1)
                dst = y_dram[2 * g:2 * g + 2] if isinstance(g, int) else y_dram[bass.ds(g * 2, 2)]
                sp.dma_start(dst.rearrange("t p n -> p t n"), x_t[:, :, :]).then_inc(y_stored, 16)
                hs = slice(HPG * g, HPG * (g + 1)) if isinstance(g, int) else bass.ds(g * HPG, HPG)
                for d in range(2):
                    sp.dma_start(m["new_ssm"][0, 0, d, hs].rearrange("(t e) p n -> (e p) t n", e=2),
                                 st_in[:, 2 * d:2 * d + 2, :]).then_inc(so_stored, 16)

            def store_h(g):
                sp.wait_ge(kc_used.sem, kc_used.at(g, 4))
                hh = slice(g, g + 1) if isinstance(g, int) else bass.ds(g, 1)
                for d in range(2):
                    sp.dma_start(m["new_hgrn"][0, 0, d, hh].rearrange("a k v -> k (a v)"),
                                 so_h[:, d, :]).then_inc(soh_stored, 16)

            sp.dma_start(cols[:, 0:1], m["ssd_dt_bias"][0].rearrange("d (h a) -> (d h) a", a=1)
                         ).then_inc(cols_in, 16)
            sp.dma_start(cols[:, 1:2], m["ssd_a_log"][0].rearrange("d (h a) -> (d h) a", a=1)
                         ).then_inc(cols_in, 16)
            sp.dma_start(acc[0][:, 0:2 * P], m["neg_in"].rearrange("p d i -> p (d i)")).then_inc(cols_in, 16)
            for t, (col, _) in enumerate(PRO_COLS):
                if t >= 2:
                    load(None, t, col)

            with sp.Fori(0, G - 1) as g:
                stage_a(g)
                for t, (base, step) in enumerate(B_COLS):
                    if t == 4:
                        stores(g, False)
                    load(g, 6 + t, g * step + (base + step))
                store_h(g)
            g = G - 1
            stage_a(g)
            for t in range(8):
                if t == 4:
                    stores(g, True)
                load(g, 6 + t, COL_GATE + D + t * P)
            store_h(g)
            last_tile = tile(G - 1, 13)[2]
            for i in range(2):
                sp.wait_ge(w_split.sem, last_tile + i)
                slot = (last_tile + 1 + i) % 2
                sp.dma_start(raw[slot][:, :, :], w_src(m["w_ssd_out"][0, 0:D, :], slot * P)
                             ).then_inc(m["m_w_in"][slot], 16)
            sp.wait_ge(y_stored, 16 * G)
            sp.wait_ge(so_stored, 32 * G)
            sp.wait_ge(soh_stored, 32 * (G + 1))
            sp.wait_ge(o_stored, 16 * (G + 1))
            for i in range(2):
                sp.wait_ge(gate_stored[i], 16 * (G * (1 + i) + 4 * NB))

        @block.tensor
        def _(pe):
            def project(g, t, b, hb, cols_n=P):
                i, _, n = tile(g, t)
                ui, used, _ = numbered(t * NB + b, None) if g is None else a_unit(g, t * NB + b)
                if b == 0:
                    pe.wait_ge(w_split.sem, n + 1)
                if not (g is None and t * NB + b < 2):
                    pe.wait_ge(bank_free[ui], used)
                out = banks[ui][0:cols_n, 0:BW]
                for k in range(KT):
                    for j, (w, h) in enumerate(((w_hi, h_hi), (w_hi, h_lo), (w_lo, h_hi))):
                        last = pe.matmul(out, w[i][:, k, 0:cols_n], h[:, k, blk(hb)],
                                         start=(k == 0 and j == 0), stop=(k == KT - 1 and j == 2))
                last.then_inc(unit_done.sem, 1)

            def turn_xb(c, bank, with_cb):
                for e in range(2):
                    last = pe.transpose(bank[:, e * P:(e + 1) * P], x_t[:, e, chunk(c)], ident)
                last = pe.transpose(bank[:, GW:GW + P], b_t[:, chunk(c)], ident)
                if with_cb:
                    last = pe.matmul(bank[:, GW + P:GW + 2 * P], b_t[:, chunk(c)], c_t[:, chunk(c)],
                                     start=True, stop=True)
                return last

            def ssd(g, k):
                if k == 0:
                    pe.wait_ge(hms_kept.sem, hms_kept.at(g, 0))
                    pe.wait_ge(st_loaded, (g + 1) * 32)
                    for j in range(4):
                        last = pe.transpose(S[3][:, j * P:(j + 1) * P], st_in[:, j, :], ident)
                    last.then_inc(tr_ready.sem, 1)
                if k < NB:
                    pe.wait_ge(silu_done.sem, silu_done.at(g, k - 2))
                if k < NA1P:
                    if k > 0:
                        pe.wait_ge(tr_kept.sem, tr_kept.at(g, 2 * k + 1))
                    turn_xb(8 - 2 * k, S[0], False).then_inc(tr_ready.sem, 1)
                    if k < 3:
                        turn_xb(7 - 2 * k, S[1], False).then_inc(tr_ready.sem, 1)
                if 2 <= k < 2 + NA1P:
                    p = k - 2
                    pe.wait_ge(xp_ready.sem, xp_ready.at(g, p + 1))
                    if p > 0:
                        pe.wait_ge(ctb_used.sem, ctb_used.at(g, p))
                    for j in range(2 if p < 3 else 1):
                        last = pe.matmul(S[2][:, j * GW:(j + 1) * GW], xb[2 * (p % 2) + j][:, GW:GW + P],
                                         xp[:, j, :], start=True, stop=True)
                    last.then_inc(ctb_ready.sem, 1)
                if 4 <= k < 4 + NC:
                    c = k - 4
                    pe.wait_ge(tr_kept.sem, tr_kept.at(g, 8 + c))
                    turn_xb(c, S[0], True).then_inc(tr_ready.sem, 1)
                    if c > 0:
                        pe.wait_ge(exp_ready.sem, exp_ready.at(g, c))
                    else:
                        pe.wait_ge(sel_ready, g + 1)
                    for d in range(2):
                        pe.matmul(S[3 + d][:, :].rearrange("p (h i) -> p h i", i=P), id_bf[:, :],
                                  neg_bf[d][:, :].rearrange("p (a i) -> p a i", a=1).broadcast_to([P, HPG, P]),
                                  start=True, stop=False, skip_group_check=True)
                        for h in range(HPG):
                            last = pe.matmul(S[3 + d][:, h * P:(h + 1) * P], sel[:, d * HPG + h, :],
                                             cum_hl[:, chunk(c)], start=False, stop=(h == HPG - 1),
                                             skip_group_check=True)
                    last.then_inc(arg_ready.sem, 1)
                if 6 <= k < 6 + NC:
                    c = k - 6
                    pe.wait_ge(m_ready.sem, m_ready.at(g, c + 1))
                    pe.wait_ge(xp_ready.sem, xp_ready.at(g, NA1P + c + 1))
                    if c > 0:
                        pe.wait_ge(y_made.sem, y_made.at(g, c))
                    else:
                        pe.wait_ge(ctb_used.sem, ctb_used.at(g, NA1P))
                    x, bt = xb[c % 4], xb[c % 4][:, GW:GW + P]
                    for h in range(HPG):
                        last = pe.matmul(S[2][:, h * HD:(h + 1) * HD], mm[:, c % 2, h * P:(h + 1) * P],
                                         x[:, h * HD:(h + 1) * HD], start=True, stop=True)
                    if c == 0:
                        for e in range(2):
                            pe.matmul(S[2][:, GW + e * P:GW + (e + 1) * P], xp[:, 0, e * P:(e + 1) * P], bt,
                                      start=True, stop=True)
                        for e in range(2):
                            last = pe.matmul(S[5][:, e * P:(e + 1) * P], t_off[:, GW + e * P:GW + (e + 1) * P], bt,
                                             start=True, stop=True)
                    else:
                        if c < NC - 1:
                            pe.matmul(S[2][:, GW:2 * GW], bt, xp[:, c % 2, :], start=True, stop=True)
                        pe.matmul(S[5][:, 0:GW], c_t[:, chunk(c)], s_f[:, :], start=True, stop=True)
                        last = pe.matmul(S[5][:, GW:2 * GW], c_t[:, chunk(c)], s_b[:, c - 1, :],
                                         start=True, stop=True)
                    last.then_inc(y_ready.sem, 1)
                if 7 <= k < 7 + NC:
                    c = k - 7
                    pe.wait_ge(y_made.sem, y_made.at(g, c + 1))
                    if c > 0:
                        pe.wait_ge(yt_made.sem, yt_made.at(g, c))
                    for e in range(2):
                        last = pe.transpose(S[1][:, e * P:(e + 1) * P], y_tok[:, e * P:(e + 1) * P], ident)
                    last.then_inc(yt_ready.sem, 1)
                if k >= SLOTS - NB:
                    b = k - (SLOTS - NB)
                    bank = (S[3], S[4], S[0])[b]
                    pe.wait_ge(sq_ready.sem, sq_ready.at(g, b + 1))
                    for e in range(2):
                        last = pe.matmul(bank[:, 0:BW], ones, mm[:, e, 0:BW], start=(e == 0), stop=(e == 1))
                    last.then_inc(ms_ready.sem, 1)

            def turn_v(g, b):
                bank = (S[5], S[2], S[5])[b]
                ui, used, _ = a_unit(g, 5 * NB + b)
                pe.wait_ge(bank_free[ui], used + 1)
                if b == 2:
                    pe.wait_ge(v_kept, g * NB + 1)
                for j in range(CB):
                    last = pe.transpose(bank[:, chunk(j)], th[ui][:, chunk(j)], ident)
                last.then_inc(v_turned, 1)

            def hgrn(g, k):
                if k == 0:
                    return
                for n in steps_in(k - 1):
                    kind, b, lv = STEPS[n]
                    q = qk[n % 4]
                    if kind in ("kb", "kf"):
                        pe.wait_ge(exp_made.sem, exp_made.at(g, n + 1))
                    else:
                        pe.wait_ge(qk_ready.sem, qk_ready.at(g, VSTEPS.index(n) + 1))
                    if kind in ("kb", "kf"):
                        i = KSTEPS.index(n)
                        bank = K_BANKS[i]
                        if i > 3:
                            pe.wait_ge(kt_kept.sem, kt_kept.at(g, i))
                        elif i == 2:
                            pe.wait_ge(ms_read, g * NB + NB)
                        else:
                            pe.wait_ge(v_kept, g * NB + (3 if i == 3 else 2))
                        for j in range(CB):
                            last = pe.transpose(bank[:, chunk(j)], q[:, 0, chunk(j)], ident)
                        last.then_inc(kt_ready.sem, 1)
                    elif kind in ("lv", "dg"):
                        i = MSTEPS.index(n)
                        if i < 3:
                            pe.wait_ge(kt_kept.sem, kt_kept.at(g, i + 1))
                        else:
                            pe.wait_ge(lv_used.sem, lv_used.at(g, i - 2))
                        for j in range(CB):
                            rhs = q[:, 0, chunk(j)] if kind == "lv" else q_t[:, chunk(b * CB + j)]
                            last = pe.matmul(S[(i + 1) % 3][:, chunk(j)], q[:, 1, chunk(j)], rhs,
                                             start=True, stop=True)
                        last.then_inc(lv_ready.sem, 1)
                    else:
                        pe.wait_ge(lv_used.sem, lv_used.at(g, 8 * (b + 1)))
                        pe.wait_ge(kc_used.sem, kc_used.at(g, 4 + b))
                        if b > 0:
                            pe.wait_ge(hms_kept.sem, hms_kept.at(g, b))
                        for j in range(CB):
                            c = b * CB + j
                            last = pe.matmul(S[3][:, chunk(j)], v_tok[:, c, :], at[b % 2][:, chunk(j)],
                                             start=True, stop=(c == 0))
                            if c > 0:
                                pe.matmul(S[3][:, chunk(j)], hs_f[:, c - 1, :], q[:, 0, chunk(j)],
                                          start=False, stop=False)
                                last = pe.matmul(S[3][:, chunk(j)], hs_b[:, c - 1, :], q[:, 1, chunk(j)],
                                                 start=False, stop=True)
                        last.then_inc(o_ready.sem, 1)
                for n in [n for n in KSTEPS if contrib_slot(n) == k]:
                    i = KSTEPS.index(n)
                    kind, b, _ = STEPS[n]
                    bank = S[4] if i % 2 == 0 or i > 3 else S[3]
                    pe.wait_ge(kt_kept.sem, kt_kept.at(g, i + 1))
                    if i in (2, 3):
                        pe.wait_ge(kc_used.sem, kc_used.at(g, i - 1))
                    if i > 3:
                        pe.wait_ge(kc_used.sem, kc_used.at(g, i))
                    kt = ktok[i if i < 4 else 0]
                    for j in range(CB):
                        last = pe.matmul(bank[:, chunk(j)], kt[:, chunk(j)], v_tok[:, b * CB + j, :],
                                         start=True, stop=True)
                    last.then_inc(kc_ready.sem, 1)
                for n in QSTEPS:
                    if slot_of(n) + 2 == k:
                        b = STEPS[n][1]
                        pe.wait_ge(o_kept.sem, o_kept.at(g, b + 1))
                        pe.matmul(S[3][:, 0:BW], ones, ktok[2][:, :], start=True,
                                  stop=True).then_inc(hms_ready.sem, 1)

            pe.wait_ge(bf_ok, 3)
            for t in range(TILES_BEFORE):
                for b in range(NB):
                    project(None, t, b, b if t == 0 else NB - 1 - b, 64 if t == 0 else P)
            pe.wait_ge(dt_dve, DT_DVE)
            pe.wait_ge(dt_act, DT_ACT)
            for a, src in enumerate((dt_d, dt_e, dt_b)):
                for c in range(NC):
                    i = a * NC + c
                    pe.transpose(S[i // 8][:, (i % 8) * 64:(i % 8 + 1) * 64], src[0:64, chunk(c)],
                                 ident[0:64, 0:64])
            flat = v_tok[0:64, :, :].rearrange("p c t -> p (c t)")
            for j in range(2):
                last = pe.matmul(S[4 + j][:, 0:288], ones[0:64, :], flat[:, j * 288:(j + 1) * 288],
                                 start=True, stop=True)
            last.then_inc(dt_turned, 1)
            pe.wait_ge(dt_kept, 1)

            with pe.Fori(0, G - 1) as g:
                for k in range(SLOTS):
                    project(g, k // NB, k % NB, k % NB)
                    ssd(g, k)
                    if k >= SLOTS - 2:
                        turn_v(g, k - (SLOTS - 2))
                for k in range(SLOTS):
                    project(g, 6 + k // NB, k % NB, b_tile(k)[1])
                    if k == 0:
                        turn_v(g, 2)
                    hgrn(g, k + 1)
            g = G - 1
            for k in range(SLOTS):
                project(g, k // NB, k % NB, k % NB)
                ssd(g, k)
                if k >= SLOTS - 2:
                    turn_v(g, k - (SLOTS - 2))
            for k in range(8 * NB):
                project(g, 6 + k // NB, k % NB, k % NB)
                if k == 0:
                    turn_v(g, 2)
                hgrn(g, k + 1)

        @block.scalar
        def _(act):
            ch = act_s

            def wait(count, g, n):
                act.wait_ge(count.sem, count.at(g, n))

            def high(g, t):
                i, used, n = tile(g, t)
                act.wait_ge(w_landed[i], used * 16 + 16)
                if not (g is None and t < 2):
                    act.wait_ge(unit_done.sem, (n - 1) * NB)
                act.activation(w_hi[i][:, :, :], raw[i][:, :, :], ACT.Copy).then_inc(w_high.sem, 1)

            def conv_tanh(g, k):
                ui = b_unit(g, k)[0]
                ci = conv_index(k)
                wait(conved, g, ci + 1)
                act.activation(th[ui][:, :], acc[ui][:, :], ACT.Tanh).then_inc(th_ok.sem, 1)

            def b_evac(g, k):
                t, b = b_tile(k)
                ui, used, n = b_unit(g, k)
                act.wait_ge(unit_done.sem, n + 1)
                bank = banks[ui]
                if t in CONV_TILES:
                    ci = conv_index(k)
                    if g is not None or ci >= NB:
                        wait(conved, g, ci - NB + 1)
                    else:
                        act.wait_ge(pads_zero, NB)
                    src = bank[:, 0:BW].rearrange("p (r c) -> p r c", c=GRID)
                    if b == 0:
                        act.activation(pad[0][:, 0, GRID + 2:GRID + 4], bank[:, GRID:GRID + 2], ACT.Copy)
                        act.activation(pad[0][:, 1, 0:2], bank[:, GRID - 2:GRID], ACT.Copy)
                    act.activation(pad[b][:, :, 2:2 + GRID], src, ACT.Copy).then_inc(bank_free[ui], 1)
                    act.wait_ge(bank_free[ui], used + 1)
                    act.wait_ge(taps_ok, 1 if g is None else g + 2)
                    if ci >= 2:
                        wait(silu_done, g, ci - 1)
                    ti = CONV_TILES.index(t)
                    act.activation(acc[ui][:, :].rearrange("p (r c) -> p r c", c=GRID), pad[b][:, :, 0:GRID],
                                   ACT.Identity, scale=taps[:, ti, 0:1], bias=taps[:, ti, TAPS:TAPS + 1]
                                   ).then_inc(tap_done.sem, 1)
                else:
                    if k >= 2:
                        act.wait_ge(bank_free[ui], used)
                    elif g is not None:
                        act.wait_ge(v_turned, g * NB + (k + 2))
                    act.activation(th[ui][:, :], bank[:, 0:BW], ACT.Tanh, scale=0.5).then_inc(th_ok.sem, 1)

            def b_th_free(g, k):
                ci = conv_index(k)
                if ci >= 2:
                    wait(silu_done, g, ci - 1)

            def a_evac(g, k):
                t, b = divmod(k, NB)
                ui, used, n = a_unit(g, k)
                act.wait_ge(unit_done.sem, n + 1)
                bank = banks[ui][:, 0:BW]
                if t < 2:
                    u, e = ((kf_t, f_t), (kb_t, g_t))[t]
                    act.wait_ge(o_final, g + 1)
                    act.activation(u[:, blk(b)], bank, ACT.Copy)
                    act.activation(e[:, blk(b)], bank, ACT.Abs).then_inc(bank_free[ui], 1)
                    act.wait_ge(bank_free[ui], used + 1)
                    ch.add(act.activation(e[:, blk(b)], e[:, blk(b)], ACT.Exp, scale=-1.0))
                elif t < 4:
                    if k == 6 or k == 7:
                        wait(silu_done, g, 0)
                    act.activation(th[ui][:, :], bank, ACT.Tanh, scale=0.5).then_inc(th_ok.sem, 1)
                elif t == 4:
                    if b == 2:
                        act.wait_ge(gate_stored[ui], g * 32 + 16)
                    act.activation(th[ui][:, :], bank, ACT.Tanh, scale=0.5).then_inc(bank_free[ui], 1)
                    act.wait_ge(bank_free[ui], used + 1)
                    dst = gate_dram[g:g + 1] if isinstance(g, int) else gate_dram[bass.ds(g, 1)]
                    act.dma_start(dst[:, :, blk(b)].rearrange("a p n -> p (a n)"),
                                  th[ui][:, :]).then_inc(gate_stored[ui], 16)
                else:
                    if b == 0:
                        act.wait_ge(gate_stored[ui], g * 16 + 16)
                    elif b == 1:
                        act.wait_ge(gate_stored[ui], g * 32 + 32)
                    else:
                        act.wait_ge(v_turned, g * NB + 1)
                    act.activation(th[ui][:, :], bank, ACT.Copy).then_inc(bank_free[ui], 1)

            def keep_v(g, b):
                bank = (S[5], S[2], S[5])[b]
                act.wait_ge(v_turned, g * NB + (b + 1))
                act.activation(v_tok[:, b * CB:(b + 1) * CB, :].rearrange("p c t -> p (c t)"), bank[:, 0:BW],
                               ACT.Copy).then_inc(v_kept, 1)

            def load_states(g):
                if g is not None:
                    act.wait_ge(so_stored, g * 32 + 32)
                hs = slice(0, HPG) if g is None else bass.ds(g * HPG + HPG, HPG)
                for d in range(2):
                    act.dma_start(st_in[:, 2 * d:2 * d + 2, :],
                                  m["state_ssm"][0, 0, d, hs].rearrange("(t e) p n -> (e p) t n", e=2)
                                  ).then_inc(st_loaded, 16)

            def ssd(g, k):
                if k == 1:
                    wait(tr_ready, g, 1)
                    act.activation(s_f[:, :], S[3][:, 0:GW], ACT.Copy)
                    act.activation(s_b[:, NC - 2, :], S[3][:, GW:2 * GW], ACT.Copy).then_inc(tr_kept.sem, 1)
                if 1 <= k < 1 + NA1P:
                    p = k - 1
                    if p >= 2:
                        wait(ctb_ready, g, p - 1)
                    for j in range(2 if p < 3 else 1):
                        wait(tr_ready, g, 2 + 2 * p + j)
                        act.activation(xb[2 * (p % 2) + j][:, 0:BW], S[j][:, 0:BW],
                                       ACT.Copy).then_inc(tr_kept.sem, 1)
                if 5 <= k < 5 + NC:
                    c = k - 5
                    wait(tr_ready, g, 9 + c)
                    if c < 4:
                        wait(ctb_ready, g, 3 if c < 2 else 4)
                    else:
                        wait(y_ready, g, c - 3)
                    act.activation(xb[c % 4][:, :], S[0][:, :], ACT.Copy).then_inc(tr_kept.sem, 1)
                    wait(arg_ready, g, c + 1)
                    if c == 0:
                        act.wait_ge(grp_ready, g + 1)
                    else:
                        wait(sum_ready, g, c)
                    for d in range(2):
                        for h in range(HPG):
                            o = d * 512 + h * P
                            last = act.activation(ex[:, o:o + P], S[3 + d][:, h * P:(h + 1) * P], ACT.Exp,
                                                  bias=tok_g[:, 0, c, d * HPG + h:d * HPG + h + 1])
                    last.then_inc(exp_ready.sem, 1)
                if k >= SLOTS - NB:
                    b = k - (SLOTS - NB)
                    wait(yt_made, g, CB * (b + 1))
                    if b == 0:
                        wait(y_ready, g, NC)
                    else:
                        wait(ms_ready, g, b)
                    act.activation(mm[:, :, 0:BW], x_t[:, :, blk(b)], ACT.Square).then_inc(sq_ready.sem, 1)

            def keep_ms(g, b):
                if b == 0:
                    wait(sum_ready, g, NC)
                wait(ms_ready, g, b + 1)
                act.activation(rstd[:, blk(b)], (S[3], S[4], S[0])[b][:, 0:BW], ACT.Copy).then_inc(ms_read, 1)

            def ssd_rstd(g):
                act.wait_ge(ms_read, g * NB + NB)
                ch.add(act.activation(rstd, rstd, ACT.Ln, scale=1.0 / GW, bias=cst[:, K_EPS4:K_EPS4 + 1]))
                ch.wait(act)
                act.activation(rstd, rstd, ACT.Exp, scale=-0.5).then_inc(rstd_ok, 1)

            def hgrn_keep(g, k):
                for i, n in enumerate(KSTEPS):
                    if k == slot_of(n) + 2:
                        wait(kt_ready, g, i + 1)
                        if i == 4:
                            wait(kc_ready, g, 1)
                        elif i == 5:
                            wait(kc_ready, g, 5)
                        bank = K_BANKS[i]
                        act.activation(ktok[i if i < 4 else 0][:, :], bank[:, 0:BW],
                                       ACT.Copy).then_inc(kt_kept.sem, 1)
                for n in QSTEPS:
                    b = STEPS[n][1]
                    if k == slot_of(n) + 2:
                        wait(o_ready, g, b + 1)
                        ch.add(act.activation(q_t[:, blk(b)], S[3][:, 0:BW], ACT.Copy))
                        act.activation(ktok[2][:, :], S[3][:, 0:BW], ACT.Square).then_inc(o_kept.sem, 1)
                    if k == slot_of(n) + 3:
                        wait(hms_ready, g, b + 1)
                        act.activation(g_t[:, blk(b)], S[3][:, 0:BW], ACT.Copy).then_inc(hms_kept.sem, 1)

            def hgrn_exp(g, k):
                if k == 2:
                    act.wait_ge(y_final, g + 1)
                    hh = slice(g, g + 1) if isinstance(g, int) else bass.ds(g, 1)
                    for d, dst in enumerate((hs_f[:, 0, :], hs_b[:, NC - 2, :])):
                        act.dma_start(dst, m["state_hgrn"][0, 0, d, hh].rearrange("a k v -> k (a v)")
                                      ).then_inc(hs_loaded, 16)
                    act.activation(hdec[:, 0, :], f_t[:, P - 1:T:P], ACT.Exp)
                    act.activation(hdec[:, 1, :], g_t[:, 0:T:P], ACT.Exp).then_inc(hdec_ok, 1)
                for n in steps_in(k):
                    kind, b, lv = STEPS[n]
                    q = qk[n % 4]
                    if kind == "q":
                        used_by_pe(act, g, n - 4)
                        act.wait_ge(f_ready, g * 2 + 2)
                        act.activation(q[:, 0, :], f_t[:, blk(b)], ACT.Exp)
                        last = act.activation(q[:, 1, :], g_t[:, blk(b)], ACT.Exp)
                    else:
                        wait(arg_made, g, ASTEPS.index(n) + 1)
                        v = q[:, 0, :] if kind in ("kb", "kf") else q[:, :, :]
                        last = act.activation(v, v, ACT.Exp)
                    last.then_inc(exp_made.sem, 1)

            def hgrn_rstd(g):
                wait(hms_kept, g, NB)
                ch.add(act.activation(g_t[:, :], g_t[:, :], ACT.Ln, scale=1.0 / P,
                                      bias=cst[:, K_EPS4:K_EPS4 + 1]))
                ch.wait(act)
                act.activation(g_t[:, :], g_t[:, :], ACT.Exp, scale=-0.5).then_inc(hrstd_ok, 1)

            def store_o(g):
                act.wait_ge(o_final, g + 2)
                dst = y_dram[16 + g:17 + g] if isinstance(g, int) else y_dram[bass.ds(g + 16, 1)]
                act.dma_start(dst.rearrange("a p n -> p (a n)"), q_t[:, :]).then_inc(o_stored, 16)

            def stage_a(g):
                for k in range(SLOTS):
                    if k == 6:
                        ch.wait(act)
                        for e in (f_t, g_t):
                            act.activation(e[:, :], e[:, :], ACT.Ln,
                                           bias=cst[:, K_1:K_1 + 1]).then_inc(f_log, 1)
                    if k != 1:
                        ssd(g, k)
                    if k == 0:
                        ssd(g, 1)
                    if k == SLOTS - 1:
                        keep_v(g, 0)
                        keep_ms(g, 0)
                    a_evac(g, k)
                    if k == SLOTS - 1:
                        keep_ms(g, 1)
                    if k % NB == 0:
                        high(g, k // NB + 1)
                    if k == SLOTS - 2:
                        hgrn_exp(g, 0)

            def stage_b_start(g, k):
                if k == 0:
                    keep_v(g, 1)
                    keep_ms(g, 2)
                    ssd_rstd(g)
                    keep_v(g, 2)

            act.sem_inc(hms_kept.sem, 1)
            act.sem_inc(o_stored, 16)
            act.sem_inc(soh_stored, 32)
            load_states(None)
            act.wait_ge(cols_in, 48)
            for b in range(NB):
                if b == 0:
                    i = 0
                    act.wait_ge(w_landed[0], 16)
                    act.activation(w_hi[0][:, :, 0:64], raw[0][:, :, 0:64], ACT.Copy).then_inc(w_high.sem, 1)
                    high(None, 1)
                ui, used, n = numbered(b, None)
                act.wait_ge(unit_done.sem, n + 1)
                act.activation(dt_v[0:64, blk(b)], banks[ui][0:64, 0:BW], ACT.Identity,
                               bias=cols[:, 0:1]).then_inc(bank_free[ui], 1)
            act.wait_ge(bank_free[0], 2)
            act.wait_ge(bank_free[1], 1)
            dt = Chain(dt_act)

            def dt_step(out, in_, f, **kw):
                dt.add(act.activation(out, in_, f, **kw))
                dt.wait(act)

            dt_step(cols[:, 2:3], cols[:, 1:2], ACT.Exp)
            dt_step(dt_a[0:64, :], dt_v[0:64, :], ACT.Abs)
            dt_step(dt_a[0:64, :], dt_a[0:64, :], ACT.Exp, scale=-1.0)
            dt_step(dt_a[0:64, :], dt_a[0:64, :], ACT.Ln, bias=cst[0:64, K_1:K_1 + 1])
            act.wait_ge(dt_dve, 2)
            dt_step(dt_d[0:64, :], dt_d[0:64, :], ACT.Ln)
            act.wait_ge(dt_dve, 14)
            dt_step(dt_e[0:64, :], dt_e[0:64, :], ACT.Exp)
            dt_step(dt_b[0:64, :], cum, ACT.Exp)
            assert dt.n == DT_ACT, dt.n
            for k in range(SLOTS):
                if k > 0 and (k - 1) // NB in CONV_TILES:
                    b_th_free(None, k - 1)
                    conv_tanh(None, k - 1)
                b_evac(None, k)
                if k % NB == 0:
                    high(None, k // NB + 2) if k < SLOTS - NB else high(0, 0)
            b_th_free(None, SLOTS - 1)
            conv_tanh(None, SLOTS - 1)
            act.wait_ge(dt_turned, 1)
            flat = tok[:, :, :, :].rearrange("p a c r -> p (a c r)")
            for i in range(4):
                n = min(512, 3 * NC * 64 - i * 512)
                act.activation(flat[:, i * 512:i * 512 + n], S[i][:, 0:n], ACT.Copy)
            flat = dec[:, :, :].rearrange("p c r -> p (c r)")
            for i in range(2):
                last = act.activation(flat[:, i * 288:(i + 1) * 288], S[4 + i][:, 0:288], ACT.Copy)
            last.then_inc(dt_kept, 1)

            def stage_b(g):
                for k in range(SLOTS):
                    stage_b_start(g, k)
                    hgrn_keep(g, k + 1)
                    if k > 0 and (k - 1) // NB in CONV_TILES:
                        b_th_free(g, k - 1)
                        conv_tanh(g, k - 1)
                    hgrn_exp(g, k + 1)
                    if k == 12:
                        load_states(g)
                    b_evac(g, k)
                    if k == SLOTS - 1:
                        hgrn_rstd(g)
                    if k % NB == 0:
                        high(g, 6 + k // NB + 1)
                b_th_free(g, SLOTS - 1)
                conv_tanh(g, SLOTS - 1)
                store_o(g)

            with act.Fori(0, G - 1) as g:
                ch.round(g)
                stage_a(g)
                stage_b(g)
                assert ch.n == ACT_ROUND, ch.n
            g = G - 1
            ch.round(g)
            stage_a(g)
            for k in range(8 * NB):
                stage_b_start(g, k)
                if k < SLOTS:
                    hgrn_keep(g, k + 1)
                    hgrn_exp(g, k + 1)
                if k == SLOTS - 1:
                    hgrn_rstd(g)
                if k == SLOTS + 1:
                    store_o(g)
                t, b = divmod(k, NB)
                ui, used, n = a_unit(g, SLOTS + k)
                act.wait_ge(unit_done.sem, n + 1)
                if k < 2:
                    act.wait_ge(v_turned, g * NB + (k + 2))
                else:
                    act.wait_ge(gate_stored[ui], 16 * (G * (1 + ui) + k // 2))
                act.activation(th[ui][:, :], banks[ui][:, 0:BW], ACT.Tanh, scale=0.5).then_inc(bank_free[ui], 1)
                act.wait_ge(bank_free[ui], used + 1)
                act.dma_start(gate_dram[8 + t, :, blk(b)], th[ui][:, :]).then_inc(gate_stored[ui], 16)
                if b == 0 and t < 7:
                    high(g, 6 + t + 1)

        @block.vector
        def _(dve):
            ch = dve_s

            def wait(count, g, n):
                dve.wait_ge(count.sem, count.at(g, n))

            def per_head(v):
                return v.rearrange("p (h a) -> p h a", a=1).broadcast_to([P, v.shape[1], HD])

            def heads(v):
                return v.rearrange("p (h c) -> p h c", c=HD)

            def low(g, t, width=P):
                i, _, n = tile(g, t)
                dve.wait_ge(w_high.sem, n + 1)
                dve.tensor_tensor(w_lo[i][:, :, 0:width], raw[i][:, :, 0:width],
                                  w_hi[i][:, :, 0:width].bitcast(F32), ALU.subtract).then_inc(w_split.sem, 1)

            def b_dest(k):
                t, b = b_tile(k)
                return (z_t[:, 0, blk(b)], z_t[:, 1, blk(b)], b_t[:, blk(b)], c_t[:, blk(b)],
                        x_t[:, 0, blk(b)], x_t[:, 1, blk(b)])[t]

            def conv_silu(g, k):
                ui = b_unit(g, k)[0]
                wait(th_ok, g, k + (0 if g is None else 2 * NB) + 1)
                if k == 12 and g is not None:
                    dve.wait_ge(y_stored, g * 16 + 16)
                dve.scalar_tensor_tensor(b_dest(k), th[ui][:, :], 1.0, acc[ui][:, :], ALU.add,
                                         ALU.mult).then_inc(silu_done.sem, 1)

            def b_evac(g, k):
                t, b = b_tile(k)
                ui, used, _ = b_unit(g, k)
                if t in CONV_TILES:
                    ti = CONV_TILES.index(t)
                    wait(tap_done, g, conv_index(k) + 1)
                    out = acc[ui][:, :].rearrange("p (r c) -> p r c", c=GRID)
                    for j in range(1, TAPS):
                        if j > 1:
                            ch.wait(dve)
                        ins = dve.scalar_tensor_tensor(out, pad[b][:, :, j:j + GRID], taps[:, ti, j:j + 1], out,
                                                       ALU.mult, ALU.add)
                        if j < TAPS - 1:
                            ch.add(ins)
                    ins.then_inc(conved.sem, 1)
                else:
                    wait(th_ok, g, k + (0 if g is None else 2 * NB) + 1)
                    dve.scalar_tensor_tensor(b_dest(k), th[ui][:, :], 1.0, banks[ui][:, 0:BW], ALU.add,
                                             ALU.mult).then_inc(bank_free[ui], 1)

            def ssd(g, k):
                if 3 <= k < 3 + NA1P:
                    p = k - 3
                    wait(ctb_ready, g, p + 1)
                    if p == 0:
                        wait(tr_kept, g, 1)
                        dve.wait_ge(grp_ready, g + 1)
                    for j in range(2 if p < 3 else 1):
                        c = 8 - 2 * p - j
                        ch.wait(dve)
                        if j == 0 and p > 0:
                            wait(ctb_used, g, p)
                        ch.add(dve.tensor_tensor(heads(s_b[:, c - 2, :]), heads(s_b[:, c - 1, :]),
                                                 per_head(dec_g[:, c, HPG:8]), ALU.mult))
                        ch.wait(dve)
                        ins = dve.tensor_tensor(s_b[:, c - 2, :], s_b[:, c - 2, :], S[2][:, j * GW:(j + 1) * GW],
                                                ALU.add)
                        if j == 0 and p < 3:
                            ch.add(ins)
                    ins.then_inc(ctb_used.sem, 1)
                if 7 <= k < 7 + NC:
                    c = k - 7
                    wait(y_ready, g, c + 1)
                    if c == 0:
                        dve.tensor_copy(y_tok[:, :], S[2][:, 0:GW])
                        dve.tensor_copy(st_in[:, 0:2, :].rearrange("p t n -> p (t n)"), S[2][:, GW:2 * GW])
                        ins = dve.tensor_copy(st_in[:, 2:4, :].rearrange("p t n -> p (t n)"), S[5][:, 0:GW])
                    else:
                        wait(yt_ready, g, c)
                        if c < NC - 1:
                            ch.add(dve.tensor_tensor(heads(s_f[:, :]), heads(s_f[:, :]),
                                                     per_head(dec_g[:, c, 0:HPG]), ALU.mult))
                        ch.add(dve.tensor_tensor(heads(t_off[:, :]), heads(S[5][:, :]),
                                                 per_head(tok_g[:, 2, c, :]), ALU.mult))
                        ch.wait(dve)
                        ch.add(dve.tensor_tensor(y_tok[:, :], t_off[:, 0:GW], S[2][:, 0:GW], ALU.add))
                        if c < NC - 1:
                            ch.add(dve.tensor_tensor(s_f[:, :], s_f[:, :], S[2][:, GW:2 * GW], ALU.add))
                        ch.wait(dve)
                        ins = dve.tensor_tensor(y_tok[:, :], y_tok[:, :], t_off[:, GW:2 * GW], ALU.add)
                    ins.then_inc(y_made.sem, 1)
                if 8 <= k < 8 + NC:
                    c = k - 8
                    wait(yt_ready, g, c + 1)
                    for e in range(2):
                        ch.add(dve.scalar_tensor_tensor(x_t[:, e, chunk(c)], x_t[:, e, chunk(c)],
                                                        vec_g[:, e:e + 1], S[1][:, e * P:(e + 1) * P],
                                                        ALU.mult, ALU.add))
                    ch.wait(dve)
                    dve.tensor_tensor(x_t[:, :, chunk(c)], x_t[:, :, chunk(c)], z_t[:, :, chunk(c)],
                                      ALU.mult).then_inc(yt_made.sem, 1)
                if 5 <= k < 5 + NC:
                    c = k - 5
                    wait(sum_ready, g, c + 1)
                    wait(tr_kept, g, 9 + c)
                    v = mm[:, c % 2, :].rearrange("p (h i) -> p h i", i=P)
                    cb = xb[c % 4][:, GW + P:GW + 2 * P].rearrange("p (a i) -> p a i", a=1).broadcast_to([P, HPG, P])
                    dve.tensor_tensor(v, v, cb, ALU.mult).then_inc(m_ready.sem, 1)

            def ssd_norm(g):
                dve.wait_ge(rstd_ok, g + 1)
                wait(yt_made, g, NC)
                for e in range(2):
                    ins = dve.scalar_tensor_tensor(x_t[:, e, :], x_t[:, e, :], vec_g[:, 2 + e:3 + e], rstd,
                                                   ALU.mult, ALU.mult)
                    if e == 0:
                        ch.add(ins)
                ins.then_inc(y_final, 1)

            def a_evac(g, k):
                t, b = divmod(k, NB)
                if t in (2, 3):
                    ui, used, _ = a_unit(g, k)
                    wait(th_ok, g, k - 6 + 1)
                    if k == 6:
                        dve.wait_ge(o_stored, g * 16 + 16)
                    dst = (q_t, s_t)[t - 2]
                    dve.scalar_tensor_tensor(dst[:, blk(b)], th[ui][:, :], 1.0, banks[ui][:, 0:BW], ALU.add,
                                             ALU.mult).then_inc(bank_free[ui], 1)

            def decay(g, k):
                for d, (e, u) in enumerate(((f_t, kf_t), (g_t, kb_t))):
                    if k == 7 + 2 * d:
                        dve.wait_ge(f_log, g * 2 + (d + 1))
                        ch.add(dve.scalar_tensor_tensor(e[:, :], u[:, :], 0.0, e[:, :], ALU.min, ALU.subtract))
                        ch.wait(dve)
                        dve.tensor_tensor(u[:, :], e[:, :], u[:, :], ALU.subtract).then_inc(f_lnk, 1)
                    if k == 8 + 2 * d:
                        dve.wait_ge(f_lnk, g * 2 + (d + 1))
                        for b in range(NB):
                            v = e[:, blk(b)] if d == 0 else back(e, b)
                            ins = dve.tensor_tensor_scan(v, reset, v, 0.0, ALU.mult, ALU.add)
                            if b < NB - 1:
                                ch.add(ins)
                        ins.then_inc(f_ready, 1)
                        dve.wait_ge(f_ready, g * 2 + (d + 1))
                        dve.tensor_tensor(u[:, :], u[:, :], e[:, :], ALU.subtract).then_inc(k_ready, 1)

            def back(e, b, r0=0, r1=P):
                return e[r0:r1, (b + 1) * BW - 1:b * BW - 1:-1] if b else e[r0:r1, BW - 1::-1]

            def hgrn(g, k):
                for i, n in enumerate(KSTEPS):
                    if k == contrib_slot(n) + 1:
                        kind, b, _ = STEPS[n]
                        bank = S[4] if i % 2 == 0 or i > 3 else S[3]
                        wait(kc_ready, g, i + 1)
                        if i == 0:
                            dve.wait_ge(hs_loaded, g * 32 + 32)
                            dve.wait_ge(hdec_ok, g + 1)
                        cs = range(b * CB, (b + 1) * CB)
                        todo = []
                        for c in (reversed(cs) if kind == "kb" else cs):
                            if c == 0 or (kind == "kb" and c >= 2) or (kind == "kf" and c < NC - 1):
                                todo.append(c)
                        for c in todo:
                            part = bank[:, (c - b * CB) * P:(c - b * CB + 1) * P]
                            if c == 0:
                                if kind == "kb":
                                    dve.wait_ge(soh_stored, g * 32 + 32)
                                ins = dve.tensor_copy(so_h[:, 0 if kind == "kf" else 1, :], part)
                            else:
                                ch.wait(dve)
                                if i > 0:
                                    wait(kc_used, g, i)
                                d, s = (0, hs_f) if kind == "kf" else (1, hs_b)
                                frm, to = (c - 1, c) if kind == "kf" else (c - 1, c - 2)
                                ins = dve.scalar_tensor_tensor(s[:, to, :], s[:, frm, :], hdec[:, d, c:c + 1],
                                                               part, ALU.mult, ALU.add)
                            if c != todo[-1]:
                                ch.add(ins)
                        ins.then_inc(kc_used.sem, 1)
                for i, n in enumerate(MSTEPS):
                    if k == slot_of(n) + 2:
                        kind, b, lv = STEPS[n]
                        wait(lv_ready, g, i + 1)
                        if lv > 0:
                            wait(lv_used, g, i)
                            dve.sem_inc(merge_clear, 1)
                        out = at[b % 2][:, :].rearrange("p (c i) -> p c i", i=P)
                        src = S[(i + 1) % 3][:, 0:BW].rearrange("p (c i) -> p c i", i=P)
                        if lv == 0:
                            if b == 2:
                                wait(o_ready, g, 1)
                            mask = cst[:, K_M64:K_M64 + P].rearrange("p (a i) -> p a i", a=1)
                            ins = dve.tensor_tensor(out, src, mask.broadcast_to([P, CB, P]), ALU.mult)
                        else:
                            mask = masks[:, lv - 1, :].rearrange("p (a i) -> p a i", a=1)
                            ins = dve.copy_predicated(out, mask.broadcast_to([P, CB, P]), src)
                        ins.then_inc(lv_used.sem, 1)
                for n in steps_in(k):
                    kind, b, lv = STEPS[n]
                    q = qk[n % 4]
                    if kind in ("kb", "kf"):
                        continue
                    wait(exp_made, g, n + 1)
                    if kind == "lv":
                        ins = dve.tensor_tensor(q[:, 0, :], q[:, 0, :], q_t[:, blk(b)], ALU.mult)
                    elif kind == "dg":
                        ins = dve.tensor_tensor(q[:, 1, :], q[:, 0, :], q[:, 1, :], ALU.add)
                    else:
                        qb = q_t[:, blk(b)].rearrange("p (a n) -> p a n", a=1).broadcast_to([P, 2, BW])
                        ins = dve.tensor_tensor(q[:, :, :], q[:, :, :], qb, ALU.mult)
                    ins.then_inc(qk_ready.sem, 1)

            def hgrn_norm(g):
                dve.wait_ge(hrstd_ok, g + 1)
                ch.add(dve.scalar_tensor_tensor(q_t[:, :], q_t[:, :], vec_g[:, 4:5], g_t[:, :], ALU.mult, ALU.mult))
                ch.wait(dve)
                dve.tensor_tensor(q_t[:, :], q_t[:, :], s_t[:, :], ALU.mult).then_inc(o_final, 1)

            def stage_a(g):
                for k in range(SLOTS):
                    ssd(g, k)
                    decay(g, k)
                    a_evac(g, k)
                    if k % NB == 1:
                        low(g, k // NB + 1)
                hgrn(g, 0)

            dve.wait_ge(cols_in, 48)
            for src, dst in ((ident, id_bf), (acc[0][:, 0:P], neg_bf[0]), (acc[0][:, P:2 * P], neg_bf[1])):
                dve.tensor_copy(dst[:, :], src).then_inc(bf_ok, 1)
            dve.sem_inc(o_final, 1)
            low(None, 0, 64)
            low(None, 1)
            dt = Chain(dt_dve)
            r = slice(0, 64)
            dve.wait_ge(dt_act, 4)
            dt.add(dve.scalar_tensor_tensor(dt_c[r, :], dt_v[r, :], 0.0, dt_a[r, :], ALU.max, ALU.add))
            dt.wait(dve)
            dt.add(dve.tensor_scalar(dt_d[r, :], dt_c[r, :], 2.0 ** -60, None, ALU.max))
            dt.add(dve.tensor_scalar(cols[:, 3:4], cols[:, 2:3], -1.0, None, ALU.mult))
            dt.wait(dve)
            dt.add(dve.tensor_scalar(dt_b[r, :], dt_c[r, :], cols[:, 3:4], None, ALU.mult))
            dt.wait(dve)
            for b in range(NB):
                dt.add(dve.tensor_tensor_scan(cum[0:32, blk(b)], reset[0:32, :], dt_b[0:32, blk(b)], 0.0,
                                              ALU.mult, ALU.add))
                dt.add(dve.tensor_tensor_scan(back(cum, b, 32, 64), reset[32:64, :], back(dt_b, b, 32, 64), 0.0,
                                              ALU.mult, ALU.add))
            dve.wait_ge(dt_act, 5)
            dt.wait(dve)
            dt.add(dve.tensor_tensor(dt_d[r, :], dt_d[r, :], dt_v[r, :], ALU.min))
            dt.wait(dve)
            dt.add(dve.tensor_tensor(dt_d[r, :], dt_d[r, :], cum, ALU.subtract))
            for lo, hi, at_col in ((0, 32, P - 1), (32, 64, 0)):
                cv = cum[lo:hi, :].rearrange("p (c t) -> p c t", t=P)
                ev = dt_e[lo:hi, :].rearrange("p (c t) -> p c t", t=P)
                dt.add(dve.tensor_tensor(ev, cv[:, :, at_col:at_col + 1].broadcast_to([32, NC, P]), cv,
                                         ALU.subtract))
            assert dt.n == 14, dt.n
            dt.add(dve.tensor_copy(cum_hl[0:64, :], cum))
            dt.wait(dve)
            dt.add(dve.tensor_tensor(cum_hl[64:128, :], cum, cum_hl[0:64, :].bitcast(F32), ALU.subtract))
            dve.wait_ge(dt_act, 7)
            dt.add(dve.tensor_tensor(dt_e[r, :], dt_e[r, :], dt_c[r, :], ALU.mult))
            for lo, hi, at_col in ((0, 32, P - 1), (32, 64, 0)):
                ev = dt_b[lo:hi, :].rearrange("p (c t) -> p c t", t=P)[:, :, at_col:at_col + 1]
                iv = cst[lo:hi, K_ID:K_ID + 64].rearrange("p (a r) -> p a r", a=1)
                ov = v_tok[lo:hi, :, :].rearrange("p c t -> p (c t)")[:, 0:NC * 64].rearrange(
                    "p (c r) -> p c r", r=64)
                dt.add(dve.tensor_tensor(ov, iv.broadcast_to([32, NC, 64]), ev.broadcast_to([32, NC, 64]),
                                         ALU.mult))
            assert dt.n == DT_DVE, dt.n
            pro = Chain(sem("dve_prologue"))
            ch = pro
            for k in range(SLOTS):
                if k > 0 and (k - 1) // NB in CONV_TILES:
                    conv_silu(None, k - 1)
                b_evac(None, k)
                if k % NB == 1:
                    low(None, k // NB + 2) if k < SLOTS - NB else low(0, 0)
            conv_silu(None, SLOTS - 1)
            ch = dve_s

            with dve.Fori(0, G - 1) as g:
                ch.round(g)
                stage_a(g)
                for k in range(SLOTS):
                    if k == 0:
                        ssd_norm(g)
                    if k > 0 and (k - 1) // NB in CONV_TILES:
                        conv_silu(g, k - 1)
                    hgrn(g, k + 1)
                    b_evac(g, k)
                    if k == SLOTS - 1:
                        hgrn_norm(g)
                    if k % NB == 1:
                        low(g, 6 + k // NB + 1)
                conv_silu(g, SLOTS - 1)
                assert ch.n == DVE_ROUND, ch.n
            g = G - 1
            ch.round(g)
            stage_a(g)
            for k in range(8 * NB):
                if k == 0:
                    ssd_norm(g)
                if k < SLOTS:
                    hgrn(g, k + 1)
                if k == SLOTS - 1:
                    hgrn_norm(g)
                if k % NB == 1 and k // NB < 7:
                    low(g, 6 + k // NB + 1)

        @block.gpsimd
        def _(pool):
            def wait(count, g, n):
                pool.wait_ge(count.sem, count.at(g, n))

            def some(v, i, n):
                cut = slice(i, i + n) if isinstance(i, int) else bass.ds(i, n)
                return v[(slice(None),) * (len(v.shape) - 1) + (cut,)]

            def gather_taps(g):
                t4 = vec[:, 0:V_CONVB + 32].rearrange("p (k t) -> p k t", t=32)
                for i, (at_col, n) in enumerate(((g + 16, 1), (g + 24, 1), (g * 2, 2))):
                    last = pool.tensor_copy(taps[:, i:i + n, :].rearrange("p t k -> p k t"), some(t4, at_col, n))
                last.then_inc(taps_ok, 1)

            def gather_group(g):
                pool.wait_ge(o_final, g + 1)
                for a in range(3):
                    src = tok[:, a, :, :].rearrange("p c (d h) -> p c d h", d=2)
                    dst = tok_g[:, a, :, :].rearrange("p c (d h) -> p c d h", d=2)
                    for d in range(2):
                        pool.tensor_copy(dst[:, :, d, :], some(src[:, :, d, :], g * 4, 4))
                src = dec[:, :, :].rearrange("p c (d h) -> p c d h", d=2)
                dst = dec_g[:, :, :].rearrange("p c (d h) -> p c d h", d=2)
                for d in range(2):
                    pool.tensor_copy(dst[:, :, d, :], some(src[:, :, d, :], g * 4, 4))
                pool.tensor_copy(vec_g[:, 0:2], some(vec[:, V_D:V_D + 16], g * 2, 2))
                pool.tensor_copy(vec_g[:, 2:4], some(vec[:, V_SSDN:V_SSDN + 16], g * 2, 2))
                pool.tensor_copy(vec_g[:, 4:5], some(vec[:, V_HGRN:V_HGRN + 8], g, 1)).then_inc(grp_ready, 1)
                for d in range(2):
                    iv = some(cst[:, K_FOLD + 32 * d:K_FOLD + 32 * d + 32], g * 4, 4).rearrange(
                        "p (h a) -> p h a", a=1)
                    last = pool.tensor_copy(sel[:, 4 * d:4 * d + 4, :], iv.broadcast_to([P, HPG, P]))
                last.then_inc(sel_ready, 1)

            def scaled(out, x, w):
                return pool.tensor_tensor(out.rearrange("p (h c) -> p h c", c=HD),
                                          x.rearrange("p (h c) -> p h c", c=HD),
                                          w.rearrange("p (h a) -> p h a", a=1).broadcast_to([P, HPG, HD]), ALU.mult)

            def ssd(g, k):
                if k == 0:
                    gather_group(g)
                if 1 <= k < 1 + NA1P:
                    p = k - 1
                    if p == 0:
                        pool.wait_ge(grp_ready, g + 1)
                    else:
                        wait(ctb_ready, g, p)
                    wait(tr_kept, g, 3 + 2 * p if p < 3 else 8)
                    for j in range(2 if p < 3 else 1):
                        ins = scaled(xp[:, j, :], xb[2 * (p % 2) + j][:, 0:GW], tok_g[:, 1, 8 - 2 * p - j, 4:8])
                    ins.then_inc(xp_ready.sem, 1)
                if 5 <= k < 5 + NC:
                    c = k - 5
                    wait(tr_kept, g, 9 + c)
                    if c == 0:
                        wait(ctb_ready, g, NA1P)
                        scaled(t_off[:, GW:2 * GW], xb[0][:, 0:GW], tok_g[:, 1, 0, 4:8])
                    elif c > 1:
                        wait(y_ready, g, c - 1)
                    scaled(xp[:, c % 2, :], xb[c % 4][:, 0:GW], tok_g[:, 1, c, 0:4]).then_inc(xp_ready.sem, 1)
                    wait(exp_ready, g, c + 1)
                    pool.tensor_tensor(mm[:, c % 2, :], ex[:, 0:512], ex[:, 512:1024],
                                       ALU.add).then_inc(sum_ready.sem, 1)

            def hgrn(g, k):
                if k == 0:
                    wait(y_ready, g, NC)
                    pool.wait_ge(k_ready, g * 2 + 2)
                for n in steps_in(k):
                    if n not in ASTEPS:
                        continue
                    kind, b, lv = STEPS[n]
                    q = qk[n % 4]
                    if n >= 4:
                        used_by_pe(pool, g, n - 4)
                    if kind in ("kb", "kf"):
                        src, ks, at_col = (g_t, kb_t, 0) if kind == "kb" else (f_t, kf_t, P - 1)
                        v = src[:, blk(b)].rearrange("p (c t) -> p c t", t=P)
                        ins = pool.tensor_tensor(q[:, 0, :].rearrange("p (c t) -> p c t", t=P),
                                                 v[:, :, at_col:at_col + 1].broadcast_to([P, CB, P]),
                                                 ks[:, blk(b)].rearrange("p (c t) -> p c t", t=P), ALU.add)
                    elif kind == "dg":
                        pool.tensor_tensor(q[:, 0, :], kf_t[:, blk(b)], f_t[:, blk(b)], ALU.add)
                        ins = pool.tensor_tensor(q[:, 1, :], kb_t[:, blk(b)], g_t[:, blk(b)], ALU.add)
                    else:
                        s = 64 >> lv
                        nb = BW // (2 * s)
                        (q_lo, q_up), (k_lo, k_up) = halves(q[:, 0, :], s), halves(q[:, 1, :], s)
                        (f_lo, f_up), (g_lo, g_up) = halves(f_t[:, blk(b)], s), halves(g_t[:, blk(b)], s)
                        rf = f_lo[:, :, s - 1:s].broadcast_to([P, nb, s])
                        rg = g_up[:, :, 0:1].broadcast_to([P, nb, s])
                        pool.tensor_tensor(q_up, f_up, rf, ALU.subtract)
                        pool.tensor_tensor(k_lo, rf, halves(kf_t[:, blk(b)], s)[0], ALU.add)
                        pool.tensor_tensor(q_lo, g_lo, rg, ALU.subtract)
                        ins = pool.tensor_tensor(k_up, rg, halves(kb_t[:, blk(b)], s)[1], ALU.add)
                    ins.then_inc(arg_made.sem, 1)

            for b in range(NB):
                pool.memset(pad[b][:, :, :], 0.0).then_inc(pads_zero, 1)
            gather_taps(0)
            pool.wait_ge(dt_kept, 1)
            with pool.Fori(0, G - 1) as g:
                for k in range(SLOTS):
                    ssd(g, k)
                for k in range(SLOTS):
                    if k == 0:
                        wait(conved, g, 0)
                        gather_taps(g + 1)
                    hgrn(g, k)
            g = G - 1
            for k in range(SLOTS):
                ssd(g, k)
            for k in range(SLOTS):
                hgrn(g, k)


HID = FFN // P
HCH = [8, 8, 6]
PHASES = [("s1", 4), ("s2", 4), ("h", 4), ("o", 4)]
for _c, _n in enumerate(HCH):
    PHASES += [(f"up{_c}", _n), (f"down{_c}", 4)]
FIRST = {}
_i = 0
for _name, _n in PHASES:
    FIRST[_name] = _i
    _i += _n
PARTS = {"s1": 0, "s2": 24, "h": 48, "o": 72, "up": 96, "down0": 120, "down1": 144, "down2": 168}
UNITS = 2 * NB


def merge_and_ffn(nc, scope, sb, sem, m):
    cst, mod, raw, banks, x_acc = m["cst"], m["mod"], m["raw"], m["banks"], m["x_acc"]
    ones, w_src = m["ones"], m["w_src"]
    y_dram, gate_dram, x_dram = m["y_dram"], m["gate_dram"], m["x_dram"]
    a_hi, a_lo = (sb(n, [P, KT, T], F32R, scope) for n in ("a_hi", "a_lo"))
    b_hi, b_lo = (sb(n, [P, KT, T], F32R, scope) for n in ("b_hi", "b_lo"))
    w_hi = [sb(f"v_hi{i}", [P, KT, P], F32R, scope) for i in range(2)]
    w_lo = [sb(f"v_lo{i}", [P, KT, P], F32R, scope) for i in range(2)]
    small = [sb(f"small{i}", [P, BW], F32, scope) for i in range(9)]
    stage, gate, tmp = small[0:3], small[3:6], small[6:9]
    A, B = (a_hi, a_lo), (b_hi, b_lo)
    USES = {"s1": A, "s2": B, "h": A, "o": B}

    w_in = m["m_w_in"]
    w_high, w_split = sem("m_w_high"), sem("m_w_split")
    unit_done, freed, acc_done = sem("m_unit_done"), sem("m_freed"), sem("m_acc_done")
    small_in = [sem(f"m_small_in{i}") for i in range(6)]
    hi_done, parts = sem("m_hi_done"), sem("m_parts")
    sq_done, sq_added, sums_zero = sem("m_sq_done"), sem("m_sq_added"), sem("m_sums_zero")
    ms_done, ln_done, rstd_done, t_done = sem("m_ms_done"), sem("m_ln_done"), sem("m_rstd_done"), sem("m_t_done")
    th_done = sem("m_th_done")

    def loop(eng, body):
        for name, n in PHASES:
            if name == PHASES[-1][0]:
                with eng.Fori(0, n - 1) as i:
                    body(name, i, False)
                body(name, n - 1, True)
            else:
                with eng.Fori(0, n) as i:
                    body(name, i, False)

    def it(name, i):
        return i + FIRST[name]

    def done(name, i, s, b):
        return it(name, i) * UNITS + (UNITS + s * NB + b + 1)

    def free_at(name, i, s, b):
        return it(name, i) * UNITS + (UNITS + (2 * b + s + 1 if name[0:2] == "up" else s * NB + b + 1))

    def acc_at(name, i, s, b):
        return i * UNITS + ((FIRST[name] - FIRST["s2"]) * UNITS + s * NB + b + 2)

    def part_at(name, k, b):
        return k * NB + (PARTS[name] + b + 1)

    def tile_of(v, k):
        return v[:, k, :] if isinstance(k, int) else v[:, bass.ds(k, 1), :].rearrange("p a n -> p (a n)")

    def tile_blk(v, k, b):
        if isinstance(k, int):
            return v[:, k, blk(b)]
        return v[:, bass.ds(k, 1), blk(b)].rearrange("p a n -> p (a n)")

    def dram_blk(v, k, b):
        if isinstance(k, int):
            return v[k, :, blk(b)]
        return v[bass.ds(k, 1), :, blk(b)].rearrange("a p n -> p (a n)")

    def mod_col(j, t, who):
        if isinstance(t, int):
            return mod[:, j + t, who:who + 1]
        return mod[:, bass.ds(t + j, 1), who:who + 1].rearrange("p a b -> p (a b)")

    with nc.Block() as block:
        @block.sync
        def _(sp):
            def load(name, i, s):
                I = it(name, i)
                sp.wait_ge(w_split, I * 2 + (s + 1))
                kt = KT
                if name == "s1":
                    src = w_src(m["w_ssd_out"][0, 0:D, :], i * 256 + s * P)
                elif name == "s2":
                    src = w_src(m["w_ssd_out"][0, D:2 * D, :], i * 256 + s * P)
                elif name == "h":
                    src = w_src(m["w_hgrn_out"][0], i * 256 + s * P)
                elif name == "o":
                    src = w_src(m["w_out"][0], i * 256 + s * P)
                elif name[0:2] == "up":
                    c0 = int(name[2]) * KT * P
                    src = w_src((m["ffn_w1"], m["ffn_w3"])[s][0], i * P + c0)
                else:
                    c = int(name[4])
                    kt = HCH[c]
                    src = w_src(m["ffn_w2"][0, c * D:c * D + kt * P, :], i * 256 + s * P)
                sp.dma_start(raw[s][:, 0:kt, :], src).then_inc(w_in[s], 16)

            for u in range(24):
                b, k = divmod(u, KT)
                if u >= 6:
                    sp.wait_ge(parts, u - 5)
                sp.dma_start(small[u % 6][:, :], y_dram[k, :, blk(b)]).then_inc(small_in[u % 6], 16)
            first = True
            for name, n in PHASES:
                if first:
                    first = False
                    with sp.Fori(1, n) as i:
                        load(name, i, 0)
                        load(name, i, 1)
                else:
                    with sp.Fori(0, n) as i:
                        load(name, i, 0)
                        load(name, i, 1)

        @block.tensor
        def _(pe):
            def body(name, i, last_it):
                I = it(name, i)
                operand = USES.get(name) or (A if name[0:2] == "up" else B)
                kt = HCH[int(name[4])] if name[0:4] == "down" else KT
                for s in range(2):
                    pe.wait_ge(w_split, I * 2 + (s + 3))
                    for b in range(NB):
                        pe.wait_ge(freed, I * UNITS + (2 * b + 1 if s == 0 else b + 4))
                        if s == 0 and name in ("s2", "h", "o") or name[0:4] == "down":
                            pe.wait_ge(parts, part_at(name, kt - 1, b))
                        for k in range(kt):
                            if s == 0 and name in ("s1", "up0"):
                                pe.wait_ge(parts, (0 if name == "s1" else PARTS["up"]) + b * KT + k + 1)
                            for j, (wp, ap) in enumerate(((w_hi, 0), (w_hi, 1), (w_lo, 0))):
                                last = pe.matmul(banks[3 * s + b][:, 0:BW], wp[s][:, k, :],
                                                 operand[ap][:, k, blk(b)],
                                                 start=(k == 0 and j == 0), stop=(k == kt - 1 and j == 2))
                        last.then_inc(unit_done, 1)

            for name, n in PHASES:
                with pe.Fori(0, n) as i:
                    body(name, i, False)
                if name == "o":
                    for b in range(NB):
                        pe.wait_ge(sq_added, 21 + b + 2)
                        if b == 2:
                            pe.wait_ge(ln_done, 1)
                        pe.matmul(banks[6 + b % 2][:, 0:BW], ones, tmp[b][:, :], start=True,
                                  stop=True).then_inc(ms_done, 1)

        @block.scalar
        def _(act):
            def high(n_const, I):
                s = n_const % 2
                act.wait_ge(w_in[s], I * 16 + (16 * (n_const // 2) + 16))
                act.wait_ge(unit_done, I * 6 + (3 * n_const + 3))
                act.activation(w_hi[s][:, :, :], raw[s][:, :, :], ACT.Copy).then_inc(w_high, 1)

            def body(name, i, last_it):
                I = it(name, i)
                for s in range(2):
                    for b in range(NB):
                        t = i * 2 + s
                        if name in ("s1", "s2", "h", "o"):
                            act.wait_ge(freed, I * UNITS + (s * NB + b + 4))
                            src = {"h": (gate_dram, t + KT), "o": (x_dram, t)}.get(name, (gate_dram, t))
                            act.dma_start(gate[b][:, :], dram_blk(src[0], src[1], b)).then_inc(small_in[3 + b], 16)
                        if name in ("s1", "s2"):
                            nxt = {"s1": "s2", "s2": "h"}[name]
                            y0 = 8 if name == "s1" else 16
                            act.wait_ge(parts, part_at(nxt, t, b) - 3)
                            act.dma_start(stage[b][:, :], dram_blk(y_dram, t + y0, b)).then_inc(small_in[b], 16)
                        if b == 0 and not (last_it and s == 1):
                            high(s + 1, I)
                        if name in ("s1", "s2"):
                            act.wait_ge(unit_done, FIRST[name] * UNITS + UNITS)
                            act.wait_ge(small_in[b], I * 32 + (64 + 16 * s + 16))
                            act.activation(tile_blk(USES[nxt][0], t, b), stage[b][:, :],
                                           ACT.Copy).then_inc(hi_done, 1)
                        elif name == "h":
                            act.wait_ge(acc_done, acc_at(name, i, s, b))
                            act.wait_ge(unit_done, FIRST[name] * UNITS + UNITS)
                            act.activation(tile_blk(b_hi, t, b), tile_blk(x_acc, t, b),
                                           ACT.Copy).then_inc(hi_done, 1)
                        elif name == "o":
                            act.wait_ge(freed, free_at(name, i, s, b))
                            act.wait_ge(sq_added, t * NB + (b + 1))
                            act.activation(stage[b][:, :], tile_blk(x_acc, t, b), ACT.Square).then_inc(sq_done, 1)
                        elif name[0:2] == "up" and s == 0:
                            act.wait_ge(freed, I * UNITS + (2 * b + 1))
                            act.wait_ge(unit_done, done(name, i, s, b))
                            act.activation(stage[b][:, :], banks[b][:, 0:BW], ACT.Tanh,
                                           scale=0.5).then_inc(th_done, 1)
                        elif name[0:2] == "up":
                            act.wait_ge(freed, free_at(name, i, s, b))
                            act.activation(tile_blk(b_hi, i, b), tmp[b][:, :], ACT.Copy).then_inc(hi_done, 1)

            act.wait_ge(w_in[0], 16)
            act.activation(w_hi[0][:, :, :], raw[0][:, :, :], ACT.Copy).then_inc(w_high, 1)
            for u in range(24):
                b, k = divmod(u, KT)
                act.wait_ge(small_in[u % 6], 16 * (u // 6) + 16)
                act.activation(a_hi[:, k, blk(b)], small[u % 6][:, :], ACT.Copy).then_inc(hi_done, 1)
            act.wait_ge(parts, 24)
            for name, n in PHASES:
                if name == "down2":
                    with act.Fori(0, n - 1) as i:
                        body(name, i, False)
                    body(name, n - 1, True)
                else:
                    with act.Fori(0, n) as i:
                        body(name, i, False)
                if name == "o":
                    for b in range(NB):
                        act.wait_ge(ms_done, b + 1)
                        act.activation(stage[b][:, :], banks[6 + b % 2][:, 0:BW], ACT.Ln, scale=1.0 / D,
                                       bias=cst[:, K_EPS:K_EPS + 1]).then_inc(ln_done, 1)
                        act.wait_ge(ln_done, b + 1)
                        act.activation(stage[b][:, :], stage[b][:, :], ACT.Exp, scale=-0.5).then_inc(rstd_done, 1)
                        for k in range(KT):
                            act.wait_ge(t_done, b * KT + k + 1)
                            for who, lo, hi in ranges(b):
                                last = act.activation(a_hi[:, k, lo:hi], gate[(b * KT + k) % 3][:, lo - b * BW:hi - b * BW],
                                                      ACT.Identity, bias=mod[:, 24 + k, who:who + 1])
                            last.then_inc(hi_done, 1)

        @block.vector
        def _(dve):
            def low(n_const, I):
                s = n_const % 2
                dve.wait_ge(w_high, I * 2 + (n_const + 1))
                dve.tensor_tensor(w_lo[s][:, :, :], raw[s][:, :, :], w_hi[s][:, :, :].bitcast(F32),
                                  ALU.subtract).then_inc(w_split, 1)

            def body(name, i, last_it):
                I = it(name, i)
                for s in range(2):
                    for b in range(NB):
                        t = i * 2 + s
                        bank = banks[3 * s + b][:, 0:BW]
                        if name in ("s1", "s2", "h"):
                            dve.wait_ge(small_in[3 + b], I * 32 + (64 + 16 * s + 16))
                            dve.wait_ge(unit_done, done(name, i, s, b))
                            dst = tile_blk(x_acc, t, b)
                            if name == "s1":
                                dve.scalar_tensor_tensor(dst, gate[b][:, :], 1.0, bank, ALU.add,
                                                         ALU.mult).then_inc(freed, 1)
                            else:
                                dve.wait_ge(acc_done, acc_at(name, i, s, b) - 1)
                                dve.scalar_tensor_tensor(tmp[b][:, :], gate[b][:, :], 1.0, bank, ALU.add,
                                                         ALU.mult).then_inc(freed, 1)
                                dve.wait_ge(freed, free_at(name, i, s, b))
                                dve.tensor_tensor(dst, dst, tmp[b][:, :], ALU.add).then_inc(acc_done, 1)
                            nxt = {"s1": "s2", "s2": "h", "h": "o"}[name]
                            dve.wait_ge(hi_done, part_at(nxt, t, b))
                            src = dst if name == "h" else stage[b][:, :]
                            dve.tensor_tensor(tile_blk(USES[nxt][1], t, b), src,
                                              tile_blk(USES[nxt][0], t, b).bitcast(F32),
                                              ALU.subtract).then_inc(parts, 1)
                        elif name == "o" or name[0:4] == "down":
                            if name == "o":
                                dve.wait_ge(small_in[3 + b], I * 32 + (64 + 16 * s + 16))
                                dve.wait_ge(parts, PARTS["up"])
                            else:
                                dve.wait_ge(freed, I * UNITS + (UNITS + s * NB + b))
                            dve.wait_ge(unit_done, done(name, i, s, b))
                            j = 16 if name == "o" else 40
                            for who, lo, hi in ranges(b):
                                r = slice(lo - b * BW, hi - b * BW)
                                dst = tile_blk(x_acc, t, b)[:, r]
                                add = gate[b][:, r] if name == "o" else dst
                                last = dve.scalar_tensor_tensor(dst, bank[:, r], mod_col(j, t, who), add,
                                                                ALU.mult, ALU.add)
                            last.then_inc(freed, 1)
                        elif s == 1:
                            dve.wait_ge(th_done, (it(name, i) - n_th[name]) * NB + (b + 1))
                            dve.wait_ge(freed, free_at(name, i, 0, b) - 1)
                            dve.scalar_tensor_tensor(gate[b][:, :], stage[b][:, :], 1.0, banks[b][:, 0:BW],
                                                     ALU.add, ALU.mult).then_inc(freed, 1)
                            dve.wait_ge(freed, free_at(name, i, 0, b))
                            dve.wait_ge(unit_done, done(name, i, 1, b))
                            nxt = "down" + name[2]
                            dve.wait_ge(parts, part_at(nxt, i, b) - 3)
                            dve.tensor_tensor(tmp[b][:, :], gate[b][:, :], bank, ALU.mult).then_inc(freed, 1)
                            dve.wait_ge(hi_done, part_at(nxt, i, b))
                            dve.tensor_tensor(tile_blk(b_lo, i, b), tmp[b][:, :],
                                              tile_blk(b_hi, i, b).bitcast(F32), ALU.subtract).then_inc(parts, 1)
                        if b == (0 if name[0:2] == "up" else 1) and not (last_it and s == 1):
                            low(s + 1, I)

            n_th, off = {}, 0
            for name, n in PHASES:
                if name[0:2] == "up":
                    n_th[name] = off
                else:
                    off += n
            dve.sem_inc(freed, UNITS)
            dve.sem_inc(unit_done, UNITS)
            dve.sem_inc(acc_done, 1)
            dve.sem_inc(w_split, 2)
            low(0, 0)
            for u in range(24):
                b, k = divmod(u, KT)
                dve.wait_ge(hi_done, u + 1)
                dve.tensor_tensor(a_lo[:, k, blk(b)], small[u % 6][:, :], a_hi[:, k, blk(b)].bitcast(F32),
                                  ALU.subtract).then_inc(parts, 1)
            for name, n in PHASES:
                if name == "down2":
                    with dve.Fori(0, n - 1) as i:
                        body(name, i, False)
                    body(name, n - 1, True)
                else:
                    with dve.Fori(0, n) as i:
                        body(name, i, False)
                if name == "o":
                    def scaled(u):
                        b, k = divmod(u, KT)
                        dve.wait_ge(rstd_done, b + 1)
                        if u >= 3:
                            dve.wait_ge(parts, PARTS["up"] + u - 2)
                        for who, lo, hi in ranges(b):
                            last = dve.scalar_tensor_tensor(
                                gate[(b * KT + k) % 3][:, lo - b * BW:hi - b * BW], x_acc[:, k, lo:hi],
                                mod[:, 32 + k, who:who + 1], stage[b][:, lo - b * BW:hi - b * BW],
                                ALU.mult, ALU.mult)
                        last.then_inc(t_done, 1)

                    dve.wait_ge(freed, (FIRST["o"] + 5) * UNITS)
                    for u in range(24):
                        b, k = divmod(u, KT)
                        if k == 0:
                            scaled(u)
                        if k < KT - 1:
                            scaled(u + 1)
                        dve.wait_ge(hi_done, PARTS["up"] + u + 1)
                        for who, lo, hi in ranges(b):
                            last = dve.scalar_tensor_tensor(
                                a_lo[:, k, lo:hi], gate[(b * KT + k) % 3][:, lo - b * BW:hi - b * BW],
                                mod[:, 24 + k, who:who + 1], a_hi[:, k, lo:hi].bitcast(F32), ALU.add, ALU.subtract)
                        last.then_inc(parts, 1)

        @block.gpsimd
        def _(pool):
            pool.wait_ge(acc_done, acc_at("h", 3, 1, 2))
            for b in range(NB):
                pool.memset(tmp[b][:, :], 0.0).then_inc(sums_zero, 1)
            pool.wait_ge(sums_zero, 3)
            pool.sem_inc(sq_added, 1)
            with pool.Fori(0, KT) as t:
                for b in range(NB):
                    pool.wait_ge(sq_done, t * NB + (b + 1))
                    pool.tensor_tensor(tmp[b][:, :], tmp[b][:, :], stage[b][:, :], ALU.add).then_inc(sq_added, 1)


def last_norm(nc, scope, sb, sem, m):
    cst, banks, x_acc, ident = m["cst"], m["banks"], m["x_acc"], m["ident"]
    out = [sb(f"out{i}", [P, D], F32, scope) for i in range(3)]
    sq = sb("last_sq", [P, 512], F32, scope)
    w_all = sb("w_all", [P, D], F32, scope)
    stat = sb("last_stat", [P, NC, 4], F32, scope)
    w_here, turned, sums, total = sem("w_here"), sem("turned"), sem("sums"), sem("total")
    lns, rstds, scaled = sem("lns"), sem("rstds"), sem("scaled")
    stored = [sem(f"stored{i}") for i in range(3)]

    with nc.Block() as block:
        @block.sync
        def _(sp):
            sp.dma_start(w_all[:, :], m["norm_final_w"].rearrange("(a n) -> a n", a=1).broadcast_to([P, D])
                         ).then_inc(w_here, 16)
            for c in range(NC):
                sp.wait_ge(scaled, 2 * (c + 1))
                dst = m["y_prompt"][0] if c == 0 else m["y_sample"][0, (c - 1) * P:c * P, :]
                sp.dma_start(dst, out[c % 3][:, :]).then_inc(stored[c % 3], 16)
            for i in range(3):
                sp.wait_ge(stored[i], 16 * NC // 3)

        @block.tensor
        def _(pe):
            for c in range(NC):
                if c >= 4:
                    pe.wait_ge(scaled, 2 * (c - 3))
                for k in range(KT):
                    last = pe.transpose(banks[2 * (c % 4) + k // 4][:, (k % 4) * P:(k % 4 + 1) * P],
                                        x_acc[:, k, chunk(c)], ident)
                last.then_inc(turned, 1)

        @block.scalar
        def _(act):
            for c in range(NC):
                act.wait_ge(turned, c + 1)
                for j in range(2):
                    if c or j:
                        act.wait_ge(sums, 2 * c + j)
                    act.activation(sq[:, :], banks[2 * (c % 4) + j][:, :], ACT.Square,
                                   accum_out=stat[:, c, j:j + 1]).then_inc(sums, 1)
                if c % 3 == 2:
                    cs = slice(c - 2, c + 1)
                    act.wait_ge(total, c // 3 + 1)
                    act.activation(stat[:, cs, 3:4], stat[:, cs, 2:3], ACT.Ln, scale=1.0 / D,
                                   bias=cst[:, K_EPS:K_EPS + 1]).then_inc(lns, 1)
                    act.wait_ge(lns, c // 3 + 1)
                    act.activation(stat[:, cs, 0:1], stat[:, cs, 3:4], ACT.Exp, scale=-0.5).then_inc(rstds, 1)

        @block.vector
        def _(dve):
            dve.wait_ge(w_here, 16)
            for c in range(NC):
                if c % 3 == 0:
                    cs = slice(c, c + 3)
                    dve.wait_ge(sums, 2 * (c + 3))
                    dve.tensor_tensor(stat[:, cs, 2:3], stat[:, cs, 0:1], stat[:, cs, 1:2],
                                      ALU.add).then_inc(total, 1)
                    dve.wait_ge(rstds, c // 3 + 1)
                if c >= 3:
                    dve.wait_ge(stored[c % 3], 16 * (c // 3))
                for j in range(2):
                    dve.scalar_tensor_tensor(out[c % 3][:, j * 512:(j + 1) * 512], banks[2 * (c % 4) + j][:, :],
                                             stat[:, c, 0:1], w_all[:, j * 512:(j + 1) * 512], ALU.mult,
                                             ALU.mult).then_inc(scaled, 1)


_INS = ["x_prompt", "x_sample", "c", "state_ssm", "state_hgrn", "c_ctx", "norm_mix_w", "norm_ffn_w", "ada_w", "ada_b",
        "w_in", "ssd_conv_w", "ssd_conv_b", "ssd_dt_bias", "ssd_a_log", "ssd_d", "ssd_norm_w", "hgrn_norm_w",
        "w_ssd_out", "w_hgrn_out", "w_out", "ffn_w1", "ffn_w3", "ffn_w2", "norm_final_w"]
_OUTS = [(1, 128, 1024), (1, 1024, 1024), (1, 1, 2, 32, 64, 128), (1, 1, 2, 8, 128, 128)]


def constants(np):
    cst = np.zeros((P, K_W), np.float32)
    i = np.arange(P)
    cst[:, K_ID:K_ID + P] = np.eye(P)
    cst[:, K_ONE:K_ONE + P] = 1
    cst[:, K_RESET:K_RESET + BW] = np.arange(BW)[None, :] % P != 0
    apart = i[:, None] ^ i[None, :]
    masks = np.zeros((P, LEVELS, P), np.float32)
    for lv in range(1, LEVELS):
        masks[:, lv - 1] = (apart >= 64 >> lv) & (apart < 128 >> lv)
    masks[:, LEVELS - 1] = apart == 0
    cst[:, K_M64:K_M64 + P] = apart >= 64
    neg = np.zeros((P, 2, P), np.float32)
    neg[:, 0] = np.where(i[None, :] >= i[:, None], 0, -1e30)
    neg[:, 1] = np.where(i[None, :] <= i[:, None], 0, -1e30)
    cst[:, K_FOLD:K_FOLD + 64] = i[:, None] % 64 == np.arange(64)[None, :]
    cst[:, K_EPS], cst[:, K_EPS4], cst[:, K_1] = EPS, 4 * EPS, 1
    return cst, neg, masks


def kernel(**inputs):
    import numpy as np
    import concourse.bacc as bacc
    from concourse.bass_utils import run_bass_kernel_spmd

    nc = bacc.Bacc("TRN2", target_bir_lowering=False, num_devices=1, dynamic_dma_scratch_size=1024)
    arrays = dict(zip(("constants", "causal_masks", "chunk_masks"), constants(np)))
    for name in _INS:
        arrays[f"in_{name}"] = np.ascontiguousarray(inputs[name])
    args = [nc.dram_tensor(n, a.shape, mybir.dt.from_np(a.dtype), kind="ExternalInput").ap()
            for n, a in arrays.items()]
    for i, shape in enumerate(_OUTS):
        args.append(nc.dram_tensor(f"out_{i}", shape, F32, kind="ExternalOutput").ap())
    build(nc, *args)
    r = run_bass_kernel_spmd(nc, [arrays], core_ids=[0])
    return tuple(r.results[0][f"out_{i}"] for i in range(len(_OUTS)))
```
